# Optimizing a Trainium2 kernel written in Bass

```python
import math
import jax, jax.numpy as jnp
from jax import lax
import numpy as np

D_MODEL = 1024
BATCH = 1
SEQ = 1024
DEPTH = 2

CHUNK = 64
N_META = 16
Q_BLOCK = 128
HEAD_DIM = 64
DIFF_WIDTH = D_MODEL // 2
FOX_WIDTH = D_MODEL - DIFF_WIDTH
DIFF_HEADS = DIFF_WIDTH // (2 * HEAD_DIM)
FOX_HEADS = FOX_WIDTH // HEAD_DIM
ROT_DIM = HEAD_DIM // 4
ROPE_THETA = 500000.0
RMS_EPS = 1e-6
SUBLN_EPS = 1e-5
COL_SIZES = (DIFF_WIDTH, DIFF_WIDTH, DIFF_WIDTH, DIFF_WIDTH,
             FOX_WIDTH, FOX_WIDTH, FOX_WIDTH, FOX_HEADS, FOX_WIDTH)
D_IN = 4 * DIFF_WIDTH + 4 * FOX_WIDTH + FOX_HEADS


def rmsnorm(x, gain, eps=RMS_EPS):
    xf = x.astype(jnp.float32)
    y = xf * lax.rsqrt(jnp.mean(xf * xf, axis=-1, keepdims=True) + eps)
    return (y * gain.astype(jnp.float32)).astype(x.dtype)

def partial_rope(t, cos, sin):
    half = ROT_DIM // 2
    t1, t2, tp = t[..., :half], t[..., half:ROT_DIM], t[..., ROT_DIM:]
    cos = cos.astype(t.dtype)
    sin = sin.astype(t.dtype)
    return jnp.concatenate([t1 * cos - t2 * sin, t2 * cos + t1 * sin, tp], axis=-1)

def to_blocks(t, axis):
    shp = t.shape
    nb = shp[axis] // Q_BLOCK
    t = t.reshape(shp[:axis] + (nb, Q_BLOCK) + shp[axis + 1:])
    return jnp.moveaxis(t, axis, 0)

def from_blocks(o):
    o = jnp.moveaxis(o, 0, 2)
    b, h, nb, qb, d = o.shape
    return o.reshape(b, h, nb * qb, d)

def diff_attention(q, k, v, lam, chunk_ids):
    scale = HEAD_DIM ** -0.5
    q_blocks = to_blocks(q, 3)
    cq_blocks = chunk_ids.reshape(-1, Q_BLOCK)

    def step(blk):
        qb, cq = blk
        s = jnp.einsum('bhmqd,bhmkd->bhmqk', qb, k).astype(jnp.float32) * scale
        visible = chunk_ids[None, :] <= cq[:, None]
        s = jnp.where(visible, s, -jnp.inf)
        p = jax.nn.softmax(s, axis=-1)
        a = p[:, :, 0] - lam * p[:, :, 1]
        return jnp.einsum('bhqk,bhkd->bhqd', a.astype(v.dtype), v)

    return from_blocks(lax.map(step, (q_blocks, cq_blocks)))

def forgetting_attention(q, k, v, cum_logf, positions):
    scale = HEAD_DIM ** -0.5
    q_blocks = to_blocks(q, 2)
    c_blocks = jnp.moveaxis(cum_logf.reshape(cum_logf.shape[:2] + (-1, Q_BLOCK)), 2, 0)
    p_blocks = positions.reshape(-1, Q_BLOCK)

    def step(blk):
        qb, cq, pq = blk
        s = jnp.einsum('bhqd,bhkd->bhqk', qb, k).astype(jnp.float32) * scale
        s = s + cq[..., None] - cum_logf[:, :, None, :]
        visible = positions[None, :] <= pq[:, None]
        s = jnp.where(visible, s, -jnp.inf)
        p = jax.nn.softmax(s, axis=-1)
        return jnp.einsum('bhqk,bhkd->bhqd', p.astype(v.dtype), v)

    return from_blocks(lax.map(step, (q_blocks, c_blocks, p_blocks)))

def first_inputs(seed: int = 0) -> dict:
    key = jax.random.key(seed)
    ks = jax.random.split(key, 12)
    f32 = jnp.float32
    return {
        "x": jax.random.normal(ks[0], (BATCH, SEQ, D_MODEL), f32),
        "meta_tokens": jax.random.normal(ks[1], (N_META, D_MODEL), f32),
        "norm_gain": 1.0 + 0.02 * jax.random.normal(ks[2], (DEPTH, D_MODEL), f32),
        "w_in": jax.random.normal(ks[3], (DEPTH, D_MODEL, D_IN), f32) * D_MODEL ** -0.5,
        "forget_bias": 0.1 * jax.random.normal(ks[4], (DEPTH, FOX_HEADS), f32),
        "lambda_q1": 0.1 * jax.random.normal(ks[5], (DEPTH, HEAD_DIM), f32),
        "lambda_k1": 0.1 * jax.random.normal(ks[6], (DEPTH, HEAD_DIM), f32),
        "lambda_q2": 0.1 * jax.random.normal(ks[7], (DEPTH, HEAD_DIM), f32),
        "lambda_k2": 0.1 * jax.random.normal(ks[8], (DEPTH, HEAD_DIM), f32),
        "subln_gain": 1.0 + 0.02 * jax.random.normal(ks[9], (DEPTH, 2 * HEAD_DIM), f32),
        "w_out": jax.random.normal(ks[10], (DEPTH, D_MODEL, D_MODEL), f32) * D_MODEL ** -0.5,
        "final_gain": 1.0 + 0.02 * jax.random.normal(ks[11], (D_MODEL,), f32),
    }

def first_block(x, meta_tokens, norm_gain, w_in, forget_bias, lambda_q1, lambda_k1,
              lambda_q2, lambda_k2, subln_gain, w_out, final_gain):
    b, seq, d = x.shape
    total = N_META + seq
    lp = ((total + Q_BLOCK - 1) // Q_BLOCK) * Q_BLOCK
    meta = jnp.broadcast_to(meta_tokens.astype(x.dtype)[None], (b, N_META, d))
    h = jnp.concatenate([meta, x], axis=1)
    h = jnp.pad(h, ((0, 0), (0, lp - total), (0, 0)))

    positions = jnp.arange(lp, dtype=jnp.int32)
    chunk_ids = jnp.where(positions < N_META, 0, (positions - N_META) // CHUNK + 1)
    inv_freq = 1.0 / (ROPE_THETA ** (jnp.arange(0, ROT_DIM, 2, dtype=jnp.float32) / ROT_DIM))
    ang = positions.astype(jnp.float32)[:, None] * inv_freq[None, :]
    cos = jnp.cos(ang)[None, :, None, None, :]
    sin = jnp.sin(ang)[None, :, None, None, :]
    split_points = [int(v) for v in np.cumsum(COL_SIZES)[:-1]]

    for l in range(DEPTH):
        hn = rmsnorm(h, norm_gain[l])
        proj = hn @ w_in[l]
        dq, dk, dv, dg, fq, fk, fv, ff, fg = jnp.split(proj, split_points, axis=-1)

        dq = partial_rope(dq.reshape(b, lp, DIFF_HEADS, 2, HEAD_DIM), cos, sin)
        dk = partial_rope(dk.reshape(b, lp, DIFF_HEADS, 2, HEAD_DIM), cos, sin)
        dq = jnp.transpose(dq, (0, 2, 3, 1, 4))
        dk = jnp.transpose(dk, (0, 2, 3, 1, 4))
        dv = jnp.transpose(dv.reshape(b, lp, DIFF_HEADS, 2 * HEAD_DIM), (0, 2, 1, 3))
        lam_init = 0.8 - 0.6 * math.exp(-0.3 * l)
        lam = (jnp.exp(jnp.sum(lambda_q1[l].astype(jnp.float32) * lambda_k1[l].astype(jnp.float32)))
               - jnp.exp(jnp.sum(lambda_q2[l].astype(jnp.float32) * lambda_k2[l].astype(jnp.float32)))
               + lam_init)
        do = diff_attention(dq, dk, dv, lam, chunk_ids)
        do = rmsnorm(do, subln_gain[l], SUBLN_EPS) * (1.0 - lam_init)
        do = jnp.transpose(do, (0, 2, 1, 3)).reshape(b, lp, DIFF_WIDTH)
        do = do * jax.nn.silu(dg)

        fq = jnp.transpose(fq.reshape(b, lp, FOX_HEADS, HEAD_DIM), (0, 2, 1, 3))
        fk = jnp.transpose(fk.reshape(b, lp, FOX_HEADS, HEAD_DIM), (0, 2, 1, 3))
        fv = jnp.transpose(fv.reshape(b, lp, FOX_HEADS, HEAD_DIM), (0, 2, 1, 3))
        log_f = jax.nn.log_sigmoid(ff.astype(jnp.float32) + forget_bias[l].astype(jnp.float32))
        cum_logf = jnp.transpose(jnp.cumsum(log_f, axis=1), (0, 2, 1))
        fo = forgetting_attention(fq, fk, fv, cum_logf, positions)
        fo = jnp.transpose(fo, (0, 2, 1, 3)).reshape(b, lp, FOX_WIDTH)
        fo = fo * jax.nn.silu(fg)

        h = h + jnp.concatenate([do, fo], axis=-1) @ w_out[l]

    out = rmsnorm(h, final_gain)
    return out[:, N_META:N_META + seq]


DEPTH_2 = 1

CTX_LEN = 256
GRID_W = 64
RET_W = D_MODEL // 2
RET_HEADS = 4
RET_HEAD_DIM = RET_W // RET_HEADS
FOURIER_W = D_MODEL - RET_W
FOURIER_GROUPS = 4
FOURIER_GROUP_DIM = FOURIER_W // FOURIER_GROUPS
MIX_W = RET_W + FOURIER_W
IN_W = 4 * RET_W + FOURIER_W
D_FF = ((8 * D_MODEL // 3 + 127) // 128) * 128
CONV_WIDTH = 3
CHUNK_2 = 128
ROPE_BASE = 10000.0
NORM_EPS = 1e-6
N_MOD = 6


def rms_norm(x, g):
    xf = x.astype(jnp.float32)
    xf = xf * lax.rsqrt(jnp.mean(xf * xf, axis=-1, keepdims=True) + NORM_EPS)
    return xf.astype(x.dtype) * g

def modulate(h, shift, scale):
    return h * (1 + scale) + shift

def adaln(cond, w, b):
    return jnp.split(jax.nn.silu(cond) @ w + b, N_MOD, axis=-1)

def split_heads(t):
    bsz, length, _ = t.shape
    return t.reshape(bsz, length, RET_HEADS, RET_HEAD_DIM).transpose(0, 2, 1, 3).astype(jnp.float32)

def axial_rope(length):
    t = jnp.arange(length)
    row = (t // GRID_W).astype(jnp.float32)
    col = (t % GRID_W).astype(jnp.float32)
    n_freq = RET_HEAD_DIM // 4
    freqs = ROPE_BASE ** (-jnp.arange(n_freq, dtype=jnp.float32) / n_freq)
    ang = jnp.concatenate([row[:, None] * freqs, col[:, None] * freqs], axis=-1)
    return jnp.cos(ang), jnp.sin(ang)

def apply_rope(t, cos, sin):
    half = RET_HEAD_DIM // 2
    t1, t2 = t[..., :half], t[..., half:]
    return jnp.concatenate([t1 * cos - t2 * sin, t1 * sin + t2 * cos], axis=-1)

def retention_scan(q, k, v, log_gamma, init_state, strict):
    bsz, heads, length, dk = q.shape
    dv = v.shape[-1]
    n_chunks = length // CHUNK_2
    pos = jnp.arange(CHUNK_2, dtype=jnp.float32)
    diff = pos[:, None] - pos[None, :]
    mask = diff > 0 if strict else diff >= 0
    dmask = jnp.where(mask[None], jnp.exp(jnp.where(mask, diff, 0.0)[None] * log_gamma[:, None, None]), 0.0)
    qc = q.reshape(bsz, heads, n_chunks, CHUNK_2, dk)
    kc = k.reshape(bsz, heads, n_chunks, CHUNK_2, dk)
    vc = v.reshape(bsz, heads, n_chunks, CHUNK_2, dv)
    scores = jnp.einsum('bhncd,bhnmd->bhncm', qc, kc) * dmask[:, None]
    intra = jnp.einsum('bhncm,bhnme->bhnce', scores, vc)
    zeta = jnp.exp((CHUNK_2 - 1 - pos)[None, :] * log_gamma[:, None])
    xi = jnp.exp((pos + 1)[None, :] * log_gamma[:, None])
    kv = jnp.einsum('bhnmd,bhnme->nbhde', kc * zeta[None, :, None, :, None], vc)
    chunk_decay = jnp.exp(CHUNK_2 * log_gamma)[None, :, None, None]

    def step(state, kv_i):
        return state * chunk_decay + kv_i, state

    _, prev = lax.scan(step, init_state, kv)
    cross = jnp.einsum('bhncd,nbhde->bhnce', qc * xi[None, :, None, :, None], prev)
    return (intra + cross).reshape(bsz, heads, length, dv)

def context_states(h_ctx, w_in, lg_f, lg_b):
    kv = h_ctx @ w_in[:, RET_W:3 * RET_W]
    k, v = jnp.split(kv, 2, axis=-1)
    k = split_heads(k) * RET_HEAD_DIM ** -0.5
    v = split_heads(v)
    length = k.shape[2]
    m = jnp.arange(length, dtype=jnp.float32)
    w_f = jnp.exp((length - 1 - m)[None, :] * lg_f[:, None])
    w_b = jnp.exp(m[None, :] * lg_b[:, None])
    s_f = jnp.einsum('bhld,hl,bhle->bhde', k, w_f, v)
    s_b = jnp.einsum('bhld,hl,bhle->bhde', k, w_b, v)
    return s_f, s_b

def fourier_mix(f):
    bsz, length, _ = f.shape
    fg = f.reshape(bsz, length, FOURIER_GROUPS, FOURIER_GROUP_DIM).astype(jnp.float32)
    out = jnp.fft.fft2(fg, axes=(1, 3), norm="ortho").real
    return out.reshape(bsz, length, FOURIER_W).astype(f.dtype)

def token_mixer(h, w_in, w_out, lg_f, lg_b, init_f, init_b, rope):
    proj = h @ w_in
    q, k, v, g, f = jnp.split(proj, [RET_W, 2 * RET_W, 3 * RET_W, 4 * RET_W], axis=-1)
    q = split_heads(q)
    k = split_heads(k) * RET_HEAD_DIM ** -0.5
    v = split_heads(v)
    if rope is not None:
        q = apply_rope(q, *rope)
        k = apply_rope(k, *rope)
    o_f = retention_scan(q, k, v, lg_f, init_f, strict=False)
    flip = lambda t: jnp.flip(t, axis=2)
    o_b = flip(retention_scan(flip(q), flip(k), flip(v), lg_b, init_b, strict=True))
    o = o_f + o_b
    o = o * lax.rsqrt(jnp.mean(o * o, axis=-1, keepdims=True) + NORM_EPS)
    bsz, length = h.shape[0], h.shape[1]
    o = o.transpose(0, 2, 1, 3).reshape(bsz, length, RET_W).astype(h.dtype)
    ret = o * jax.nn.silu(g)
    return jnp.concatenate([ret, fourier_mix(f)], axis=-1) @ w_out

def conv_ffn(h, w_up, conv_w, conv_b, w_down, rows):
    bsz, length, _ = h.shape
    u = (h @ w_up).reshape(bsz, rows, length // rows, 2 * D_FF)
    up = jnp.pad(u, ((0, 0), (0, 0), (1, 1), (0, 0)))
    u = up[:, :, :-2] * conv_w[0] + up[:, :, 1:-1] * conv_w[1] + up[:, :, 2:] * conv_w[2] + conv_b
    a, b = jnp.split(u.reshape(bsz, length, 2 * D_FF), 2, axis=-1)
    return (jax.nn.silu(a) * b) @ w_down

def second_inputs(seed: int = 0) -> dict:
    key = jax.random.key(seed)
    ks = jax.random.split(key, 20)
    nrm = lambda k, shape, s: jax.random.normal(k, shape, jnp.float32) * s
    base = 1.0 - 2.0 ** (-5.0 - jnp.arange(RET_HEADS, dtype=jnp.float32))
    logit = jnp.log(base / (1.0 - base))
    return {
        "x": nrm(ks[0], (BATCH, SEQ, D_MODEL), 1.0),
        "c": nrm(ks[1], (BATCH, D_MODEL), 1.0),
        "ctx": nrm(ks[2], (BATCH, CTX_LEN, D_MODEL), 1.0),
        "c_ctx": nrm(ks[3], (D_MODEL,), 1.0),
        "w_ada": nrm(ks[4], (DEPTH_2, D_MODEL, N_MOD * D_MODEL), D_MODEL ** -0.5),
        "b_ada": nrm(ks[5], (DEPTH_2, N_MOD * D_MODEL), 0.02),
        "g_mix_pre": 1.0 + nrm(ks[6], (DEPTH_2, D_MODEL), 0.05),
        "g_mix_post": 1.0 + nrm(ks[7], (DEPTH_2, D_MODEL), 0.05),
        "g_ffn_pre": 1.0 + nrm(ks[8], (DEPTH_2, D_MODEL), 0.05),
        "g_ffn_post": 1.0 + nrm(ks[9], (DEPTH_2, D_MODEL), 0.05),
        "w_in": nrm(ks[10], (DEPTH_2, D_MODEL, IN_W), D_MODEL ** -0.5),
        "ret_decay_fwd": logit[None] + nrm(ks[11], (DEPTH_2, RET_HEADS), 0.1),
        "ret_decay_bwd": logit[None] + nrm(ks[12], (DEPTH_2, RET_HEADS), 0.1),
        "w_out": nrm(ks[13], (DEPTH_2, MIX_W, D_MODEL), MIX_W ** -0.5),
        "w_up": nrm(ks[14], (DEPTH_2, D_MODEL, 2 * D_FF), D_MODEL ** -0.5),
        "conv_w": nrm(ks[15], (DEPTH_2, CONV_WIDTH, 2 * D_FF), CONV_WIDTH ** -0.5),
        "conv_b": nrm(ks[16], (DEPTH_2, 2 * D_FF), 0.02),
        "w_down": nrm(ks[17], (DEPTH_2, D_FF, D_MODEL), D_FF ** -0.5),
    }

def second_block(x, c, ctx, c_ctx, w_ada, b_ada, g_mix_pre, g_mix_post, g_ffn_pre, g_ffn_post,
              w_in, ret_decay_fwd, ret_decay_bwd, w_out, w_up, conv_w, conv_b, w_down):
    seq_len = x.shape[1]
    rows = seq_len // GRID_W
    rope = axial_rope(seq_len)
    ctx_s = ctx
    for layer in range(DEPTH_2):
        lg_f = jax.nn.log_sigmoid(ret_decay_fwd[layer].astype(jnp.float32))
        lg_b = jax.nn.log_sigmoid(ret_decay_bwd[layer].astype(jnp.float32))
        sh_a, sc_a, gt_a, sh_f, sc_f, gt_f = [m[:, None, :] for m in adaln(c, w_ada[layer], b_ada[layer])]
        csh_a, csc_a, cgt_a, csh_f, csc_f, cgt_f = adaln(c_ctx, w_ada[layer], b_ada[layer])
        h_ctx = modulate(rms_norm(ctx_s, g_mix_pre[layer]), csh_a, csc_a)
        s_f, s_b = context_states(h_ctx, w_in[layer], lg_f, lg_b)
        h_lat = modulate(rms_norm(x, g_mix_pre[layer]), sh_a, sc_a)
        mix = token_mixer(h_lat, w_in[layer], w_out[layer], lg_f, lg_b, s_f, s_b, rope)
        x = x + gt_a * rms_norm(mix, g_mix_post[layer])
        h_ffn = modulate(rms_norm(x, g_ffn_pre[layer]), sh_f, sc_f)
        ffn = conv_ffn(h_ffn, w_up[layer], conv_w[layer], conv_b[layer], w_down[layer], rows)
        x = x + gt_f * rms_norm(ffn, g_ffn_post[layer])
        if layer + 1 < DEPTH_2:
            zero = jnp.zeros_like(s_f)
            mix_c = token_mixer(h_ctx, w_in[layer], w_out[layer], lg_f, lg_b, zero, zero, None)
            ctx_s = ctx_s + cgt_a * rms_norm(mix_c, g_mix_post[layer])
            h_cffn = modulate(rms_norm(ctx_s, g_ffn_pre[layer]), csh_f, csc_f)
            ffn_c = conv_ffn(h_cffn, w_up[layer], conv_w[layer], conv_b[layer], w_down[layer], 1)
            ctx_s = ctx_s + cgt_f * rms_norm(ffn_c, g_ffn_post[layer])
    return x


def setup_inputs(seed=0):
    out = dict(first_inputs(seed))
    for name, value in second_inputs(seed + 1).items():
        if name != "x":
            out[name + "_2"] = value
    return out


def reference(
    x, meta_tokens, norm_gain, w_in, forget_bias, lambda_q1, lambda_k1, lambda_q2, lambda_k2,
    subln_gain, w_out, final_gain, c_2, ctx_2, c_ctx_2, w_ada_2, b_ada_2, g_mix_pre_2,
    g_mix_post_2, g_ffn_pre_2, g_ffn_post_2, w_in_2, ret_decay_fwd_2, ret_decay_bwd_2, w_out_2,
    w_up_2, conv_w_2, conv_b_2, w_down_2,
):
    x = first_block(
        x, meta_tokens, norm_gain, w_in, forget_bias, lambda_q1, lambda_k1, lambda_q2,
        lambda_k2, subln_gain, w_out, final_gain,
    )
    return second_block(
        x, c_2, ctx_2, c_ctx_2, w_ada_2, b_ada_2, g_mix_pre_2, g_mix_post_2, g_ffn_pre_2,
        g_ffn_post_2, w_in_2, ret_decay_fwd_2, ret_decay_bwd_2, w_out_2, w_up_2, conv_w_2,
        conv_b_2, w_down_2,
    )


_drawn_inputs = setup_inputs


def setup_inputs(seed=0):
    import zlib

    import numpy as np

    out = dict(_drawn_inputs(seed))
    spreads = {}
    factors = {'forget_bias': 3.333, 'subln_gain': 5.236, 'conv_b_2': 5.707}
    for name, (base, spread) in spreads.items():
        noise = np.random.default_rng([zlib.crc32(name.encode()), seed]).standard_normal(out[name].shape)
        drawn = base * np.exp(spread * noise) if base else spread * noise
        out[name] = __import__('jax').numpy.asarray(drawn.astype(out[name].dtype))
    for name, factor in factors.items():
        out[name] = (out[name] * factor).astype(out[name].dtype)
    return out
```

```python
from contextlib import ExitStack

import numpy as np
import concourse.bass as bass
from concourse import mybir

F32 = mybir.dt.float32
F32R = mybir.dt.float32r
ALU = mybir.AluOpType
ACT = mybir.ActivationFunctionType
AX = mybir.AxisListType

SEQ = 1024
NM = 16
L = SEQ + NM
D = 1024
KT = 8
NT = 8
CH = [(0, 352), (352, 344), (696, 344)]
LAM_INIT = [0.8 - 0.6 * float(np.exp(-0.3 * l)) for l in range(2)]
NEG = -1e30
DFF = 2816
FT = DFF // 128


class Ins:

    def __init__(self, q, fn, after):
        self.q, self.fn, self.after = q, fn, after
        self.sig = False
        self.val = 0

    def need(self):
        self.sig = True


class Dma:

    def __init__(self, q, fn, after, chan):
        self.q, self.fn, self.after, self.chan = q, fn, after, chan
        chan.n += 1
        self.val = 16 * chan.n

    def need(self):
        pass


class Chan:
    def __init__(self, sem):
        self.sem, self.n = sem, 0


class Queue:

    def __init__(self, sem):
        self.sem, self.items = sem, []

    def add(self, fn, after=()):
        for a in after:
            a.need()
        i = Ins(self, fn, list(after))
        self.items.append(i)
        return i

    def dma(self, chan, out, in_, after=(), **kw):
        for a in after:
            a.need()
        i = Dma(self, lambda e: e.dma_start(out, in_, **kw), list(after), chan)
        self.items.append(i)
        return i

    def number(self):
        n = 0
        for i in self.items:
            if isinstance(i, Ins) and i.sig:
                n += 1
                i.val = n
        return n

    def emit(self, eng):
        seen = {}
        for i in self.items:
            want = {}
            for a in i.after:
                s = a.chan.sem if isinstance(a, Dma) else a.q.sem
                if a.val > seen.get(id(s), 0):
                    seen[id(s)] = a.val
                    want[id(s)] = (s, a.val)
            for s, v in want.values():
                eng.wait_ge(s, v)
            if i.fn is None:
                continue
            x = i.fn(eng)
            if isinstance(i, Dma):
                x.then_inc(i.chan.sem, 16)
            elif i.sig:
                x.then_inc(self.sem, 1)


class Ring:

    def __init__(self, n, base=0):
        self.n, self.i, self.base = n, 0, base
        self.rel = [[] for _ in range(n)]
        self.busy = [False] * n

    def ready(self):
        return not self.busy[self.i]

    def take(self):
        i = self.i
        assert not self.busy[i]
        self.busy[i] = True
        self.i = (i + 1) % self.n
        return i, self.rel[i]

    def free(self, i, ins):
        self.rel[i] = list(ins)
        self.busy[i] = False


def pieces(a, b, step=512):
    out = []
    while a < b:
        e = min(b, (a // step + 1) * step)
        out.append((a, e))
        a = e
    return out


def build(nc, A, S, O, dbg=None, stage=9):
    ctx = ExitStack()
    with ctx:
        def sb(name, shape, dt=F32):
            return ctx.enter_context(nc.sbuf_tensor(name, shape, dt))

        def sem(name):
            return ctx.enter_context(nc.semaphore(name))

        pe, act, dve, pool, sp = (Queue(sem(n)) for n in ("q_pe", "q_act", "q_dve", "q_pool", "q_sp"))
        chans = {}

        def ch(name):
            if name not in chans:
                chans[name] = Chan(sem("d_" + name))
            return chans[name]

        PS = ctx.enter_context(nc.psum_tensor("PS", [128, 8, 512], F32))
        PSf = PS[:, :, :].rearrange("p a b -> p (a b)")
        AH = sb("AH", [128, KT, L], F32R)
        AL = sb("AL", [128, KT, L], F32R)
        W32 = sb("W32", [128, 3, 1024])
        NW = 4
        WH = sb("WH", [128, NW, 1024], F32R)
        WL = sb("WL", [128, NW, 1024], F32R)
        identr = sb("identr", [128, 128], F32R)
        maskr = sb("maskr", [128, 2, 128], F32R)
        selr = sb("selr", [128, 8, 128], F32R)
        C2 = sb("C2", [128, L], F32R)
        RW = 22144
        R = sb("R", [128, RW])
        at = [0]

        def carve(n):
            v = R[:, at[0]:at[0] + n]
            at[0] += n
            assert at[0] <= RW, at[0]
            return v

        def c3(a, b):
            return carve(a * b).rearrange("p (a b) -> p a b", a=a)

        ident = carve(128)
        ones = carve(128)
        SM = carve(64)
        COLS = carve(96)
        persist = at[0]

        def mm(out, lhsT, rhs, start=True, stop=True, after=()):
            return pe.add(lambda e: e.matmul(out, lhsT, rhs, start=start, stop=stop, skip_group_check=True), after)

        def mm3(out, wh, wl, xh, xl, start, stop, after=()):
            mm(out, wh, xh, start, False, after)
            mm(out, wh, xl, False, False)
            return mm(out, wl, xh, False, stop)

        def tr(out, in_, after=()):
            k = in_.shape[0]
            return pe.add(lambda e: e.transpose(out, in_, ident[0:k, 0:k]), after)

        def ac(out, in_, func=ACT.Copy, after=(), scale=1.0, bias=None, accum=None):
            kw = {"scale": scale}
            if bias is not None:
                kw["bias"] = bias
            if accum is not None:
                kw["accum_out"] = accum
            return act.add(lambda e: e.activation(out, in_, func, **kw), after)

        def tt(out, a, b, op, after=(), q=None):
            return (q or dve).add(lambda e: e.tensor_tensor(out, a, b, op), after)

        def ts(out, a, s1, s2, op0, op1=None, after=(), q=None):
            if op1 is None:
                return (q or dve).add(lambda e: e.tensor_scalar(out, a, s1, None, op0), after)
            return (q or dve).add(lambda e: e.tensor_scalar(out, a, s1, s2, op0, op1), after)

        def stt(out, a, s, b, op0, op1, after=()):
            return dve.add(lambda e: e.scalar_tensor_tensor(out, a, s, b, op0, op1), after)

        def cp(out, a, after=(), q=None):
            return (q or dve).add(lambda e: e.tensor_copy(out, a), after)

        def rmax_neg(out, a, after=()):
            return dve.add(lambda e: e.tensor_reduce(out, a, AX.X, ALU.max, negate=True), after)

        def recip(out, a, after=()):
            return dve.add(lambda e: e.reciprocal(out, a), after)

        def f(x):
            return x.bitcast(F32)

        def barrier():
            last = []
            for q in (pe, act, dve, pool):
                real = [i for i in q.items[-40:] if i.fn is not None]
                last += real[-1:]
            for q in (pe, act, dve, pool, sp):
                q.add(None, [x for x in last if x.q is not q] + pend)
            del pend[:]
        pend = []

        banks = Ring(3, 5)
        w32 = Ring(3)
        wr = Ring(NW)

        def bank(i):
            return PS[:, banks.base + i, :]

        dve.add(lambda e: e.memset(ones, 1.0))
        cm = w32.take()[0]
        c0 = [sp.dma(ch("c0"), ident, A["k_ident"]),
              sp.dma(ch("c0"), W32[:, cm, 0:256], A["k_mask"]),
              sp.dma(ch("c0"), COLS[:, 0:32], A["k_cols"])]
        cn = w32.take()[0]
        c0.append(sp.dma(ch("c0"), W32[:, cn, :], A["k_sel"]))
        x1 = ac(identr[:, :], ident, after=c0)
        x2 = ac(maskr[:, :, :].rearrange("p a b -> p (a b)"), W32[:, cm, 0:256])
        x3 = ac(selr[:, :, :].rearrange("p a b -> p (a b)"), W32[:, cn, :])
        w32.free(cm, [x3])
        w32.free(cn, [x3])
        cz = dve.add(lambda e: e.memset(f(C2[:, :]), 0.0))
        consts = [x3, cz]

        def load_w(src, width):
            s, rel = w32.take()
            a = src.shape[1]
            d = sp.dma(ch(f"w{s}"), W32[:, s, :].rearrange("p (a b) -> p a b", a=a), src, rel)
            t, rel = wr.take()
            h = ac(WH[:, t, :], W32[:, s, :], after=[d] + rel)
            lo = tt(WL[:, t, :], W32[:, s, :], f(WH[:, t, :]), ALU.subtract, [h])
            w32.free(s, [lo])
            return t, lo

        def wslice(w, c, n=128):
            return w[:, c:c + n].rearrange("(k p) n -> p k n", p=128)

        def gemm_f(wsrc, nch, evac, ready):
            while not (w32.ready() and wr.ready()):
                yield
            t, lo = load_w(wsrc, 128)
            yield
            wh = WH[:, t, :].rearrange("p (k m) -> p k m", k=KT)
            wl = WL[:, t, :].rearrange("p (k m) -> p k m", k=KT)
            for c, n in nch:
                while not banks.ready():
                    yield
                b, rel = banks.take()
                o = bank(b)[:, 0:n]
                for k in range(KT):
                    m = mm3(o, wh[:, k, :], wl[:, k, :], AH[:, k, c:c + n], AL[:, k, c:c + n],
                            k == 0, k == KT - 1, [lo] + ready + rel if k == 0 else [])
                last = m
                r = evac(o, c, n, m)
                banks.free(b, r)
                yield
            wr.free(t, [last])

        def run(*gens):
            gens = [g for g in gens if g is not None]
            idle = 0
            while gens:
                n0 = sum(len(q.items) for q in (pe, act, dve, pool, sp))
                for g in list(gens):
                    try:
                        next(g)
                    except StopIteration:
                        gens.remove(g)
                n1 = sum(len(q.items) for q in (pe, act, dve, pool, sp))
                idle = idle + 1 if n1 == n0 else 0
                assert idle < 50, "stuck"

        cosT = carve(L)
        sinT = carve(L)
        rotm = carve(128)
        V = carve(2 * 9 * 128).rearrange("p (s t n) -> p s t n", s=2, t=9)
        QT = c3(2, L)
        KTt = c3(2, L)
        GT = c3(2, L)
        OTt = c3(1, L)
        TMP = c3(1, L)
        b1base = at[0]
        P = c3(4, L)
        PT = carve(2 * 9 * 256).rearrange("p (s t n) -> p s t n", s=2, t=9)
        ST = carve(64).rearrange("p (s n) -> p s n", s=8)
        HB = R[:, b1base:b1base + 4 * 1024].rearrange("p (a b) -> p a b", a=4)
        SQJ = PT[:, 0, :, :].rearrange("p t n -> p (t n)")[:, 0:1024]
        ctab = [sp.dma(ch("c1"), cosT, A["k_cos"]), sp.dma(ch("c1"), sinT, A["k_sin"]),
                sp.dma(ch("c1"), rotm, A["k_rot"])]
        consts = consts + ctab + c0

        LB = SM[:, 0:2]
        RSTD = SM[:, 8:26]
        lt = P[:, 0, 0:512].rearrange("p (l a n) -> p l a n", l=2, a=4)
        dl = sp.dma(ch("c2"), P[:, 0, 0:512], A["k_lam"])
        for l in range(2):
            pr = P[:, 1, 0:128].rearrange("p (a n) -> p a n", a=2)
            x = tt(pr, lt[:, l, 0:4:2, :], lt[:, l, 1:4:2, :], ALU.mult, [dl] if l == 0 else [y])
            y = dve.add(lambda e, o=SM[:, 2:4], a=pr: e.tensor_reduce(o, a, AX.X, ALU.add), [x] + ([z] if l else []))
            z = ac(SM[:, 4:6], SM[:, 2:4], ACT.Exp, [y] + ([y2] if l else []))
            y1 = tt(SM[:, 6:7], SM[:, 5:6], SM[:, 4:5], ALU.subtract, [z])
            y2 = ts(LB[:, l:l + 1], SM[:, 6:7], -LAM_INIT[l], None, ALU.add, after=[y1])
            y = y2
        pend.extend(ctab + c0)
        barrier()

        hs = S["hs"]
        os_ = S["os"]

        def norm_phase(src_tiles, rows, gain, bias, store=None):
            groups = [list(range(i, min(i + 4, len(src_tiles)))) for i in range(0, len(src_tiles), 4)]
            hrel = [[] for _ in range(4)]
            jr = []
            for gi, g in enumerate(groups):
                tl = {}
                for t in g:
                    src, rows_, col = src_tiles[t]
                    s = t % 4
                    d = sp.dma(ch(f"h{s}"), HB[0:rows_, s, :], src, hrel[s] + pend_hs)
                    q = ac(SQJ[0:rows_, :], HB[0:rows_, s, :], ACT.Square, [d] + jr, accum=RSTD[0:rows_, t:t + 1])
                    jr = [q]
                    l1 = ts(RSTD[0:rows_, t:t + 1], RSTD[0:rows_, t:t + 1], 1.0 / D, 1e-6, ALU.mult, ALU.add, [q])
                    l2 = ac(RSTD[0:rows_, t:t + 1], RSTD[0:rows_, t:t + 1], ACT.Ln, [l1])
                    l3 = ac(RSTD[0:rows_, t:t + 1], RSTD[0:rows_, t:t + 1], ACT.Exp, [l2], scale=-0.5)
                    n = ts(HB[0:rows_, s, :], HB[0:rows_, s, :], RSTD[0:rows_, t:t + 1], None, ALU.mult, after=[l3])
                    tl[t] = n
                c_lo = src_tiles[g[0]][2]
                tot = sum(src_tiles[t][1] for t in g)
                for k in range(KT):
                    b, rel = banks.take()
                    o = 0
                    for t in g:
                        _, rows_, col = src_tiles[t]
                        m = tr(bank(b)[:, o:o + rows_], HB[0:rows_, t % 4, 128 * k:128 * k + 128], [tl[t]] + rel)
                        o += rows_
                    dst_h, dst_l = AH[:, k, c_lo:c_lo + tot], AL[:, k, c_lo:c_lo + tot]
                    if bias is None:
                        h = ac(dst_h, bank(b)[:, 0:tot], ACT.Copy, [m], scale=gain(k))
                        lo = stt(dst_l, bank(b)[:, 0:tot], gain(k), f(dst_h), ALU.mult, ALU.subtract, [h])
                        banks.free(b, [lo])
                    else:
                        tb, trel = tmpr.take()
                        tv = TB[:, tb, 0:tot]
                        h = ac(tv, bank(b)[:, 0:tot], ACT.Identity, [m] + trel, scale=gain(k), bias=bias(k))
                        banks.free(b, [h])
                        h2 = cp(dst_h, tv, [h])
                        lo = tt(dst_l, tv, f(dst_h), ALU.subtract, [h2])
                        tmpr.free(tb, [lo])
                for t in g:
                    hrel[t % 4] = [m]
            return [lo]
        pend_hs = []

        vring, qring, gring = Ring(2), Ring(2), Ring(2)
        qgr = {}
        sA, sB = Ring(1), Ring(1)
        pring, ptring, oring, tring = Ring(4), Ring(2), Ring(1), Ring(1)
        C0 = {"q": (0, 2048), "k": (512, 2560), "v": (1024, 3072), "g": (1536, 3592)}

        def wcol(kind, g):
            return C0[kind][g // 4] + 128 * (g % 4)

        def ff_phase(l, ready):
            zt = TMP[:, 0, :]
            e1 = GT[:, 0, :]
            e2 = GT[:, 1, :]
            last = []

            def evac(o, c, n, m):
                x = ac(zt[0:8, c:c + n], o[0:8, :], ACT.Identity, [m], bias=COLS[0:8, 18 + l:19 + l])
                last.append(x)
                return [x]
            yield from gemm_f(wslice(A["w_in"][l], 3584), CH, evac, ready)
            z, a, u = zt[0:8, :], e1[0:8, :], e2[0:8, :]
            m1 = ts(a, z, -1.0, None, ALU.mult, after=last)
            m1 = tt(a, a, z, ALU.max, [m1])
            m2 = ac(a, a, ACT.Exp, [m1], scale=-1.0)
            m3 = ts(u, a, 1.0, None, ALU.add, after=[m2])
            m4 = ts(z, z, 0.0, None, ALU.min)
            m5 = stt(a, u, -1.0, a, ALU.add, ALU.subtract, [m3])
            m6 = tt(z, z, a, ALU.add, [m4, m5])
            m7 = ac(u, u, ACT.Ln, [m3, m5])
            m8 = tt(z, z, u, ALU.subtract, [m6, m7])
            m9 = dve.add(lambda e: e.memset(u, 1.0), [m8])
            m10 = dve.add(lambda e: e.tensor_tensor_scan(a, u, z, 0.0, ALU.mult, ALU.add), [m9])
            h = ac(C2[0:8, :], a, ACT.Copy, [m10])
            lo = tt(C2[32:40, :], a, f(C2[0:8, :]), ALU.subtract, [h])
            ffdone[:] = [lo]
            tring.rel[0] = [lo]

        ffdone = []

        def proj(l, g, ready):
            fox = g >= 4
            w = A["w_in"][l]
            while not (qring.ready() and vring.ready() and gring.ready()):
                yield
            s, qrel = qring.take()
            vs, vrel = vring.take()
            gs, grel = gring.take()
            qgr[(l, g)] = (s, vs, gs)
            fin = {"q": [], "k": [], "g": [], "v": []}
            for kind, dst in (("q", QT), ("k", KTt)):
                sc = 0.125 if kind == "q" else 1.0
                if fox:
                    def evac(o, c, n, m, dst=dst, sc=sc, kind=kind):
                        x = ac(dst[:, s, c:c + n], o, ACT.Copy, [m] + qrel, scale=sc)
                        fin[kind].append(x)
                        return [x]
                    yield from gemm_f(wslice(w, wcol(kind, g)), CH, evac, ready)
                else:
                    while not tring.ready():
                        yield
                    ti, trel = tring.take()
                    part = []

                    def evac(o, c, n, m, sc=sc):
                        x = ac(TMP[:, ti, c:c + n], o, ACT.Copy, [m] + trel, scale=sc)
                        part.append((c, n, x))
                        return [x]
                    yield from gemm_f(wslice(w, wcol(kind, g)), CH, evac, ready)
                    for c, n, x in part:
                        while not banks.ready():
                            yield
                        b, rel = banks.take()
                        m = mm(bank(b)[:, 0:n], rotm, TMP[:, ti, c:c + n], True, True, [x] + rel)
                        y = tt(dst[:, s, c:c + n], bank(b)[:, 0:n], sinT[:, c:c + n], ALU.mult, [m] + qrel)
                        banks.free(b, [y])
                        y2 = tt(TMP[:, ti, c:c + n], TMP[:, ti, c:c + n], cosT[:, c:c + n], ALU.mult, [m], q=pool)
                        y3 = tt(dst[:, s, c:c + n], dst[:, s, c:c + n], TMP[:, ti, c:c + n], ALU.add, [y, y2])
                        fin[kind].append(y3)
                        yield
                    tring.free(ti, [fin[kind][-1]])
            while not tring.ready():
                yield
            ti, trel = tring.take()
            part = []

            def evac(o, c, n, m):
                x = ac(TMP[:, ti, c:c + n], o, ACT.Copy, [m] + trel)
                part.append(x)
                return [x]
            yield from gemm_f(wslice(w, wcol("v", g)), CH, evac, ready)
            for quad in ((0, 1, 2, 3), (4, 5, 6, 7), (8,)):
                while not banks.ready():
                    yield
                b, rel = banks.take()
                for i, t in enumerate(quad):
                    cc, n = (16 + 128 * t, 128) if t < 8 else (0, 16)
                    m = tr(bank(b)[0:n, 128 * i:128 * i + 128], TMP[:, ti, cc:cc + n], [part[-1]] + rel)
                if quad[0] < 8:
                    x = cp(V[:, vs, quad[0]:quad[0] + 4, :], bank(b)[:, 0:512].rearrange("p (a b) -> p a b", a=4), [m] + vrel)
                else:
                    x = cp(V[0:16, vs, 8, :], bank(b)[0:16, 0:128], [m] + vrel)
                banks.free(b, [x])
                fin["v"].append(x)
                yield
            tring.free(ti, [m])

            def evac(o, c, n, m):
                x = ac(GT[:, gs, c:c + n], o, ACT.Tanh, [m] + grel + ffdone, scale=0.5)
                y = stt(GT[:, gs, c:c + n], GT[:, gs, c:c + n], 1.0, o, ALU.add, ALU.mult, [x])
                fin["g"].append(y)
                return [y]
            yield from gemm_f(wslice(w, wcol("g", g)), CH, evac, ready)
            qgr[(l, g)] = (s, vs, gs, fin)

        stn = [0]
        strel = [[] for _ in range(8)]

        def attention(l, g):
            fox = g >= 4
            s, vs, gs, fin = qgr[(l, g)]
            qk = [fin["q"][-1], fin["k"][-1]]
            while not oring.ready():
                yield
            oi, orel = oring.take()
            blocks = [(6, 7), (4, 5), (2, 3), (0, 1)] + ([(8,)] if l == 0 else [])
            pv_done = []
            o_done = []
            s_last = [None]

            def scores(j, m, use_a):
                ring, b0 = (sA, 0) if use_a else (sB, 3)
                while not (ring.ready() and pring.ready()):
                    yield
                _, rel = ring.take()
                pi, prel = pring.take()
                meta = j == 8
                q0 = 0 if meta else NM + 128 * j
                W = NM if meta else NM + 128 * (j + 1)
                off = 512 * b0
                rows = NM if meta else 128
                dm0 = 0 if meta else W - 128
                r0 = 64 * m
                for i, (a, b) in enumerate(pieces(0, W)):
                    x = mm(PSf[:, off + a:off + b], QT[r0:r0 + 64, s, q0:q0 + 128], KTt[r0:r0 + 64, s, a:b], True, False,
                           qk + rel if i == 0 else [])
                    if fox:
                        x = mm(PSf[:, off + a:off + b], selr[:, 2 * (g - 4) + m, :], C2[:, a:b], False, False, ffdone)
                if fox or not meta:
                    for a, b in pieces(dm0, W):
                        x = mm(PSf[:, off + a:off + b], identr[:, :], maskr[:, int(fox), a - dm0:b - dm0], False, True)
                s_last[0] = x
                si = stn[0] % 8
                stn[0] += 1
                st = ST[0:rows, si, :]
                w = PSf[0:rows, off:off + W]
                n = rmax_neg(st[:, 0:1], w, [x] + strel[si])
                p = P[0:rows, pi, 0:W]
                e = ac(p, w, ACT.Exp, [n] + prel, bias=st[:, 0:1], accum=st[:, 1:2])
                ring.free(0, [e])
                r = recip(st[:, 2:3], st[:, 1:2], [e])
                if fox or m == 0:
                    y = ts(p, p, st[:, 2:3], None, ALU.mult, after=[r])
                else:
                    y = ts(st[:, 3:4], st[:, 2:3], LB[0:rows, l:l + 1], None, ALU.mult, after=[r])
                strel[si] = [y]
                res.append((j, m, pi, rows, W, y, si))

            def block_scores(bi):
                blk = blocks[bi]
                for m in range(2):
                    for j in reversed(blk):
                        yield from scores(j, m, j % 2 == 1)
                        yield

            def tail(bi, mine):
                blk = blocks[bi]
                by = {(j, m): x for (j, m, *x) in mine}
                if not fox:
                    for j in blk:
                        p0, rows, W, y0, _ = by[(j, 0)]
                        p1, _, _, y1, si = by[(j, 1)]
                        z = stt(P[0:rows, p0, 0:W], P[0:rows, p1, 0:W], ST[0:rows, si, 3:4], P[0:rows, p0, 0:W],
                                ALU.mult, ALU.add, [y0, y1])
                        strel[si] = [z]
                        pring.free(p1, [z])
                        by[(j, 0)] = [p0, rows, W, z, si]
                meta = blk == (8,)
                nq = NM if meta else 256
                q0 = 0 if meta else NM + 128 * blk[0]
                tiles = [8] if meta else [8] + list(range(blk[1] + 1))
                pts = []
                for m in (range(2) if fox else range(1)):
                    while not ptring.ready():
                        yield
                    pt, ptrel = ptring.take()
                    evs = []
                    todo = [tiles[0:1]] + [tiles[i:i + 2] for i in range(1, len(tiles), 2)]
                    for grp in todo:
                        while not banks.ready():
                            yield
                        b, rel = banks.take()
                        kr = NM if grp[0] == 8 else 128
                        for i, t in enumerate(grp):
                            for jj, j in enumerate(blk):
                                if t < 8 and t > j:
                                    continue
                                p0, rows, W, y, _ = by[(j, m)]
                                ka = 0 if t == 8 else NM + 128 * t
                                x = tr(bank(b)[0:kr, 256 * i + 128 * jj:256 * i + 128 * jj + rows],
                                       P[0:rows, p0, ka:ka + kr], [y] + rel)
                        if grp[0] == 8:
                            ev = [evac_pt(PT[0:kr, pt, 8, 0:nq], bank(b)[0:kr, 0:nq], [x] + ptrel)]
                        elif grp[-1] == blk[-1]:
                            ev = [cp(PT[:, pt, grp[0], :], bank(b)[:, 0:256], [x] + ptrel),
                                  cp(PT[:, pt, grp[1], 128:256], bank(b)[:, 384:512], [x])]
                        else:
                            ev = [evac_pt(PT[:, pt, grp[0]:grp[0] + 2, :].rearrange("p a b -> p (a b)"),
                                          bank(b)[:, 0:512], [x] + ptrel)]
                        banks.free(b, ev)
                        evs += ev
                        yield
                    for j in blk:
                        pring.free(by[(j, m)][0], [x])
                    pts.append((pt, evs))
                while not banks.ready():
                    yield
                ab, arel = banks.take()
                for m, (pt, evs) in enumerate(pts):
                    mr = (64 * m, 64) if fox else (0, 128)
                    vc = slice(64 * m, 64 * m + 64) if fox else slice(0, 128)
                    for i, t in enumerate(tiles):
                        kr = NM if t == 8 else 128
                        qa = 128 if (not meta and t == blk[1]) else 0
                        x = mm(bank(ab)[mr[0]:mr[0] + mr[1], qa:nq], V[0:kr, vs, t, vc], PT[0:kr, pt, t, qa:nq],
                               i == 0, i == len(tiles) - 1, evs + fin["v"] + arel if i == 0 else [])
                    ptring.free(pt, [x])
                pv_done[:] = [x]
                yield
                y = cp(OTt[:, oi, q0:q0 + nq], bank(ab)[:, 0:nq], [x] + orel)
                banks.free(ab, [y])
                o_done.append(y)

            def evac_pt(o, a, after):
                epar[0] ^= 1
                return ac(o, a, ACT.Copy, after) if epar[0] else cp(o, a, after)

            res = []
            for bi in range(len(blocks)):
                res = []
                yield from block_scores(bi)
                mine = res
                yield from tail(bi, mine)
            qring.free(s, [s_last[0]])
            vring.free(vs, pv_done)
            o = OTt[:, oi, :]
            cs = CH if l == 0 else [(NM, 352), (NM + 352, 336), (NM + 688, 336)]
            if not fox:
                while not tring.ready():
                    yield
                ti, trel = tring.take()
                t = TMP[:, ti, :]
                for c, n in cs:
                    while not banks.ready():
                        yield
                    b, rel = banks.take()
                    q = ac(t[:, c:c + n], o[:, c:c + n], ACT.Square, [o_done[-1]] + trel)
                    x = mm(bank(b)[:, 0:n], ones, t[:, c:c + n], True, True, [q] + rel)
                    v = ts(t[:, c:c + n], bank(b)[:, 0:n], 1.0 / 128, 1e-5, ALU.mult, ALU.add, [x])
                    banks.free(b, [v])
                    v = ac(t[:, c:c + n], t[:, c:c + n], ACT.Ln, [v])
                    v = ac(t[:, c:c + n], t[:, c:c + n], ACT.Exp, [v], scale=-0.5)
                    v = stt(o[:, c:c + n], o[:, c:c + n], COLS[:, 16 + l:17 + l], t[:, c:c + n], ALU.mult, ALU.mult, [v])
                    yield
                tring.free(ti, [v])
                sc = 0.5 * (1.0 - LAM_INIT[l])
            else:
                v = o_done[-1]
                sc = 0.5
            c, n = (0, L) if l == 0 else (NM, SEQ)
            y = stt(o[:, c:c + n], o[:, c:c + n], sc, GT[:, gs, c:c + n], ALU.mult, ALU.mult, [v, fin["g"][-1]])
            gring.free(gs, [y])
            dst = sp.dma(ch("os"), os_[g][:, c:c + n], o[:, c:c + n], [y] + os_rel)
            oring.free(oi, [dst])
            os_done.append(dst)
            yield
        epar = [0]
        os_rel = []
        os_done = []

        def chain(*gs):
            for g in gs:
                yield from g

        def lazy(fn, *a):
            yield from fn(*a)

        def split_into(k, src, n, d):
            h = ac(AH[:, k, 0:n], src, ACT.Copy, d)
            return tt(AL[:, k, 0:n], src, f(AH[:, k, 0:n]), ALU.subtract, [h])

        def out_proj(w, tiles, evac, ready):
            last = None
            for half in range(2):
                ws = []
                for kk in range(4):
                    src = w[256 * kk:256 * kk + 256, 512 * half:512 * half + 512].rearrange("(k p) n -> p k n", p=128)
                    ws.append(load_w(src, 512))
                for t, col, rows in tiles:
                    b, rel = banks.take()
                    for k in range(KT):
                        ti, lo = ws[k // 2]
                        wv = slice(512 * (k % 2), 512 * (k % 2) + 512)
                        a = (AH[:, k, col:col + 128], AL[:, k, col:col + 128])
                        mm(bank(b), a[0], WH[:, ti, wv], k == 0, False, [lo] + (ready + rel if k == 0 else []))
                        mm(bank(b), a[0], WL[:, ti, wv], False, False)
                        last = mm(bank(b), a[1], WH[:, ti, wv], False, k == KT - 1)
                    banks.free(b, evac(bank(b), t, rows, half, last))
                for ti, lo in ws:
                    wr.free(ti, [last])

        def layer(l):
            if l == 0:
                tiles = [(A["x"][0][128 * t:128 * t + 128, :], 128, NM + 128 * t) for t in range(8)]
                tiles.append((A["meta_tokens"], 16, 0))
            else:
                tiles = [(hs[NM + 128 * t:NM + 128 * t + 128, :], 128, NM + 128 * t) for t in range(8)]
                tiles.append((hs[0:16, :], 16, 0))
            ready = norm_phase(tiles, None, lambda k: COLS[:, 8 * l + k:8 * l + k + 1], None)
            barrier()
            run(chain(ff_phase(l, ready), proj(l, 0, ready)))
            for g in range(8):
                run(attention(l, g), proj(l, g + 1, ready) if g < 7 else None)
            barrier()
            n = L if l == 0 else SEQ
            c = 0 if l == 0 else NM
            orr = Ring(2)
            for g in range(8):
                i, rel = orr.take()
                d = sp.dma(ch(f"o{i}"), OTt2[:, i, c:c + n], os_[g][:, c:c + n], rel + os_done)
                h = ac(AH[:, g, c:c + n], OTt2[:, i, c:c + n], ACT.Copy, [d])
                rd = tt(AL[:, g, c:c + n], OTt2[:, i, c:c + n], f(AH[:, g, c:c + n]), ALU.subtract, [h])
                orr.free(i, [rd])
            hr = Ring(4)
            stores = []

            def evac(b, t, rows, half, last):
                i, rel = hr.take()
                if l == 0:
                    src = A["x"][0][128 * t:128 * t + 128, 512 * half:512 * half + 512] if t < 8 else \
                        A["meta_tokens"][:, 512 * half:512 * half + 512]
                else:
                    src = hs[NM + 128 * t:NM + 128 * t + 128, 512 * half:512 * half + 512]
                r0 = NM + 128 * t if t < 8 else 0
                hv = HB[0:rows, i, 0:512]
                d = sp.dma(ch(f"r{i}"), hv, src, rel)
                y = tt(hv, hv, b[0:rows, :], ALU.add, [d, last])
                s = sp.dma(ch(f"s{i}"), hs[r0:r0 + rows, 512 * half:512 * half + 512], hv, [y])
                hr.free(i, [s])
                stores.append(s)
                return [y]
            tl = [(t, NM + 128 * t, 128) for t in range(8)] + ([(8, 0, 16)] if l == 0 else [])
            out_proj(A["w_out"][l], tl, evac, [rd])
            pend.extend(stores[-4:])
            del os_done[:]
            barrier()

        OTt2 = GT
        layer(0)
        if stage >= 2:
            layer(1)

        xs, gs_ = S["xs"], S["gs"]

        def phase(n=0):
            barrier()
            at[0] = persist + n

        def r3(a, b):
            return carve(a * b).rearrange("p (a b) -> p a b", a=a)

        banks.n, banks.base, banks.i = 8, 0, 0
        banks.rel = [[] for _ in range(8)]
        banks.busy = [False] * 8
        CH2 = [(0, 512), (512, 512)]

        G1 = SM[:, 30:54].rearrange("p (a k) -> p a k", a=3)
        B1 = COLS[:, 32:56].rearrange("p (a k) -> p a k", a=3)
        LG = SM[:, 54:62]

        def ada_phase():
            phase()
            CS = r3(8, 2)
            CT = r3(8, 2)
            CB = r3(8, 128)
            AD = r3(32, 2)
            BD = r3(32, 2)
            K2 = carve(24)
            BR = carve(2048)
            GP = r3(2, 1024)
            GO = r3(2, 512)
            d = [sp.dma(ch("a0"), CS, A["k_c"].rearrange("p (k c) -> p k c", k=8)),
                 sp.dma(ch("a0"), BD, A["k_bada"].rearrange("p (k c) -> p k c", k=32)),
                 sp.dma(ch("a0"), K2, A["k_cols2"]),
                 sp.dma(ch("a0"), BR[0:1, :], A["k_brow"]),
                 sp.dma(ch("a0"), GP, A["k_gpost"].rearrange("p (k c) -> p k c", k=2))]
            x = ac(CT, CS, ACT.Exp, d, scale=-1.0)
            x = ts(CT, CT, 1.0, None, ALU.add, after=[x])
            x = recip(CT, CT, [x])
            csd = tt(CS, CS, CT, ALU.mult, [x])
            cbd = cp(CB, CS[:, :, 0:1].broadcast_to([128, 8, 128]), [csd])
            z, a, u = K2[:, 0:8], K2[:, 8:16], K2[:, 16:24]
            zz = LG
            x = ts(a, z, -1.0, None, ALU.mult, after=d)
            x = tt(a, a, z, ALU.max, [x])
            x = ac(a, a, ACT.Exp, [x], scale=-1.0)
            x3_ = ts(u, a, 1.0, None, ALU.add, after=[x])
            x4 = ts(zz, z, 0.0, None, ALU.min)
            x5 = stt(a, u, -1.0, a, ALU.add, ALU.subtract, [x3_])
            x6 = tt(zz, zz, a, ALU.add, [x4, x5])
            x7 = ac(u, u, ACT.Ln, [x3_, x5])
            tt(zz, zz, u, ALU.subtract, [x6, x7])
            w = A["w_ada_2"][0]
            b, rel = banks.take()
            order = [0, 1, 3, 4]
            for i in range(32):
                c0_ = 1024 * order[i // 8] + 128 * (i % 8)
                s, wrel = w32.take()
                dd = sp.dma(ch(f"w{s}"), W32[:, s, :].rearrange("p (a b) -> p a b", a=8), wslice(w, c0_), wrel)
                for k in range(KT):
                    m = mm(bank(b)[:, 2 * i:2 * i + 2], W32[:, s, 128 * k:128 * k + 128], CS[:, k, :],
                           k == 0, k == KT - 1, [dd, csd] + rel)
                w32.free(s, [m])
            x = tt(AD, bank(b)[:, 0:64].rearrange("p (k c) -> p k c", k=32), BD, ALU.add, [m])
            banks.free(b, [x])
            gm = A["k_gpre"]
            GQ = carve(16).rearrange("p (a k) -> p a k", a=2)
            dg = sp.dma(ch("a1"), GQ, gm.rearrange("p (a k) -> p a k", a=2))
            for i, (sc_, cc, gg) in enumerate(((8, 0, 0), (8, 1, 0), (24, 0, 1))):
                y = stt(G1[:, i, :], AD[:, sc_:sc_ + 8, cc], 1.0, GQ[:, gg, :], ALU.add, ALU.mult, [x, dg])
                y = cp(B1[:, i, :], AD[:, sc_ - 8:sc_, cc], [x])
            gor = Ring(2)
            for gi in range(2):
                for half in range(2):
                    b, rel = banks.take()
                    for kk in range(4):
                        s, wrel = w32.take()
                        c0_ = 1024 * (2 + 3 * gi) + 512 * half
                        dd = sp.dma(ch(f"w{s}"), W32[:, s, :].rearrange("p (a b) -> p a b", a=2),
                                    w[256 * kk:256 * kk + 256, c0_:c0_ + 512].rearrange("(k p) n -> p k n", p=128), wrel)
                        for k in range(2):
                            m = mm(bank(b), CB[:, 2 * kk + k, :], W32[:, s, 512 * k:512 * k + 512],
                                   kk + k == 0, False, [dd, cbd] + rel)
                        w32.free(s, [m])
                    m = mm(bank(b), ones[0:1, :], BR[0:1, 1024 * gi + 512 * half:1024 * gi + 512 * half + 512], False, True)
                    gi_, grel = gor.take()
                    y = tt(GO[:, gi_, :], bank(b), GP[:, gi, 512 * half:512 * half + 512], ALU.mult, [m] + grel)
                    banks.free(b, [y])
                    dd = sp.dma(ch(f"g{gi_}"), gs_[gi][:, 512 * half:512 * half + 512], GO[:, gi_, :], [y])
                    gor.free(gi_, [dd])
                    pend.append(dd)

        def rstd_of(col, rows, scale, eps, after):
            v = ts(col, col, scale, eps, ALU.mult, ALU.add, after=after)
            v = ac(col, col, ACT.Ln, [v])
            return ac(col, col, ACT.Exp, [v], scale=-0.5)

        def fill_a(tiles, src, ready, gi, tb):
            lo = None
            tr_ = Ring(2)
            last = None
            for g0 in range(0, len(tiles), 4):
                g = tiles[g0:g0 + 4]
                n = 128 * len(g)
                for k in range(KT):
                    b, rel = banks.take()
                    for i, t in enumerate(g):
                        last = tr(bank(b)[:, 128 * i:128 * i + 128], src(t)[:, 128 * k:128 * k + 128], [ready[t]] + rel)
                    ti, trel = tr_.take()
                    tv = tb[:, ti, 0:n]
                    c = 128 * g0
                    h = ac(tv, bank(b)[:, 0:n], ACT.Identity, [last] + trel, scale=G1[:, gi, k:k + 1], bias=B1[:, gi, k:k + 1])
                    banks.free(b, [h])
                    h2 = cp(AH[:, k, c:c + n], tv, [h])
                    lo = tt(AL[:, k, c:c + n], tv, f(AH[:, k, c:c + n]), ALU.subtract, [h2])
                    tr_.free(ti, [lo])
            return lo, last

        def prep_x(keep):
            phase(keep)
            X = r3(8, 1024)
            FG = carve(1024)
            J = carve(1024)
            TB = r3(2, 512)
            d0 = sp.dma(ch("b0"), FG, A["k_fg"])
            jr = []
            ready = {}
            for t in range(8):
                x = X[:, t, :]
                r1, r2 = RSTD[:, t:t + 1], RSTD[:, 8 + t:9 + t]
                d = sp.dma(ch(f"h{t % 4}"), x, hs[NM + 128 * t:NM + 128 * t + 128, :], xr[t - 4:t - 3] if t > 3 else [])
                q = ac(J, x, ACT.Square, [d] + jr, accum=r1)
                jr = [q]
                v = rstd_of(r1, 128, 1.0 / D, 1e-6, [q])
                y = stt(x, x, r1, FG, ALU.mult, ALU.mult, [v, d0])
                st_ = sp.dma(ch(f"s{t % 4}"), xs[128 * t:128 * t + 128, :], x, [y])
                xr.append(y)
                pend.append(st_)
                q = ac(J, x, ACT.Square, [y] + jr, accum=r2)
                jr = [q]
                v = rstd_of(r2, 128, 1.0 / D, 1e-6, [q])
                ready[t] = ts(x, x, r2, None, ALU.mult, after=[v, st_])
            return fill_a(list(range(8)), lambda t: X[:, t, :], ready, 0, TB)[0]
        xr = []

        FM = [0]

        def ctx_phase():
            phase()
            SC = r3(4, 256)
            XI = carve(1024).rearrange("p (h d c) -> p h d c", h=4, d=2)
            DM = r3(4, 128)
            ZE = r3(8, 4)
            FM[0] = at[0] - persist
            X = r3(2, 1024)
            J = carve(1024)
            TB = r3(2, 512)
            KC, VC = r3(2, 512), r3(2, 512)
            TT = carve(256)
            CT = carve(8 + 4 * 128 + 256)
            E1, E2 = carve(128), carve(128)
            d0 = sp.dma(ch("b1"), CT, A["k_dec"])
            jr = []
            ready = {}
            for t in range(2):
                x, r1 = X[:, t, :], RSTD[:, t:t + 1]
                d = sp.dma(ch(f"h{t}"), x, A["ctx_2"][0][128 * t:128 * t + 128, :])
                q = ac(J, x, ACT.Square, [d] + jr, accum=r1)
                jr = [q]
                v = rstd_of(r1, 128, 1.0 / D, 1e-6, [q])
                ready[t] = ts(x, x, r1, None, ALU.mult, after=[v])
            lo, _ = fill_a([0, 1], lambda t: X[:, t, :], ready, 1, TB)
            x = None
            for dr in range(2):
                for h in range(4):
                    lg = LG[:, 4 * dr + h:4 * dr + h + 1]
                    x = ac(ZE[:, 4 * dr + h, :], CT[:, 4 * dr:4 * dr + 4], ACT.Exp, [d0], scale=lg)
                    x = ac(XI[:, h, dr, :], CT[:, 8 + 128 * dr:136 + 128 * dr], ACT.Exp, [], scale=lg)
            y = None
            for h in range(4):
                x = ac(E1, CT[:, 264:392], ACT.Exp, [y] if y else [], scale=LG[:, h:h + 1])
                x2_ = ac(E2, CT[:, 392:520], ACT.Exp, [], scale=LG[:, 4 + h:5 + h])
                y = tt(DM[:, h, :], E1, CT[:, 520:648], ALU.mult, [x])
                y2_ = tt(E2, E2, CT[:, 648:776], ALU.mult, [x2_])
                y = tt(DM[:, h, :], DM[:, h, :], E2, ALU.add, [y, y2_])

            def evac(b, t, rows, half, last):
                if half == 0:
                    z = ac(KC[:, t, :], b, ACT.Copy, [last], scale=float(128 ** -0.5))
                else:
                    z = ac(VC[:, t, :], b, ACT.Copy, [last])
                fin.append(z)
                return [z]
            fin = []
            out_proj(A["w_in_2"][0][:, 512:1536], [(0, 0, 128), (1, 128, 128)], evac, [lo])
            tr_ = Ring(1)
            for h in range(4):
                b, rel = banks.take()
                for t in range(2):
                    _, trel = tr_.take()
                    y1_ = ts(TT[:, 0:128], VC[:, t, 128 * h:128 * h + 128], ZE[:, h, t:t + 1], None, ALU.mult, after=[fin[-1], x] + trel)
                    y2_ = ts(TT[:, 128:256], VC[:, t, 128 * h:128 * h + 128], ZE[:, 4 + h, t:t + 1], None, ALU.mult)
                    m = mm(bank(b)[:, 0:256], KC[:, t, 128 * h:128 * h + 128], TT[:, 0:256], t == 0, t == 1, [y2_] + rel)
                    tr_.free(0, [m])
                y = cp(SC[:, h, :], bank(b)[:, 0:256], [m])
                banks.free(b, [y])
            return SC, XI, DM, ZE

        def mixer(SC, XI, DM, ZE, ready):
            phase(FM[0])
            CO, SI = carve(1024), carve(1024)
            QH, KH, GH_, OH = carve(1024), carve(1024), carve(1024), carve(1024)
            T1, T2 = r3(2, 512), r3(2, 512)
            VM, KM = r3(8, 128), r3(8, 128)
            VZ = r3(8, 256)
            PV = r3(8, 256)
            QX = r3(2, 1024)
            SS = r3(8, 128)
            dt = [sp.dma(ch("b2"), CO, A["k_cos2"]), sp.dma(ch("b2"), SI, A["k_sin2"])]
            w = A["w_in_2"][0]
            tr_ = Ring(2)
            prev = {"q": [], "k": [], "v": [], "g": [], "o": []}

            def go(gen):
                for _ in gen:
                    pass

            def gemm2(c, evac):
                go(gemm_f(wslice(w, c), CH2, evac, ready))

            for h in range(4):
                done = {"q": [], "k": [], "v": [], "g": []}
                for kind, dst, sc_ in (("q", QH, 1.0), ("k", KH, float(128 ** -0.5))):
                    def evac(o, c, n, m):
                        ti, trel = tr_.take()
                        x = ac(T1[:, ti, :], o, ACT.Copy, [m] + trel, scale=sc_)
                        y1 = tt(dst[:, c:c + n], T1[:, ti, :], CO[:, c:c + n], ALU.mult, [x] + dt + prev[kind])
                        y2 = tt(T2[0:64, ti, :], T1[64:128, ti, :], SI[64:128, c:c + n], ALU.mult)
                        y3 = tt(T2[64:128, ti, :], T1[0:64, ti, :], SI[0:64, c:c + n], ALU.mult)
                        y4 = tt(dst[:, c:c + n], dst[:, c:c + n], T2[:, ti, :], ALU.add, [y3])
                        tr_.free(ti, [y4])
                        done[kind].append(y4)
                        return [x]
                    gemm2(512 * (kind == "k") + 128 * h, evac)

                def evac(o, c, n, m):
                    ti, trel = tr_.take()
                    x = ac(T1[:, ti, :], o, ACT.Copy, [m] + trel)
                    b, rel = banks.take()
                    for i in range(4):
                        m = tr(bank(b)[:, 128 * i:128 * i + 128], T1[:, ti, 128 * i:128 * i + 128], [x] + rel)
                    tr_.free(ti, [m])
                    y = cp(VM[:, c // 128:c // 128 + 4, :], bank(b).rearrange("p (a b) -> p a b", a=4), [m] + prev["v"])
                    banks.free(b, [y])
                    done["v"].append(y)
                    return [x]
                gemm2(1024 + 128 * h, evac)

                def evac(o, c, n, m):
                    x = ac(GH_[:, c:c + n], o, ACT.Tanh, [m] + prev["g"], scale=0.5)
                    y = stt(GH_[:, c:c + n], GH_[:, c:c + n], 1.0, o, ALU.add, ALU.mult, [x])
                    done["g"].append(y)
                    return [y]
                gemm2(1536 + 128 * h, evac)
                for half in range(2):
                    b, rel = banks.take()
                    for i in range(4):
                        c = 512 * half + 128 * i
                        m = tr(bank(b)[:, 128 * i:128 * i + 128], KH[:, c:c + 128], done["k"] + rel)
                    y = cp(KM[:, 4 * half:4 * half + 4, :], bank(b).rearrange("p (a b) -> p a b", a=4), [m] + prev["k"])
                    banks.free(b, [y])
                z1 = ts(VZ[:, :, 0:128], VM, ZE[:, h, 2:3], None, ALU.mult, after=done["v"] + prev["k"])
                z2 = ts(VZ[:, :, 128:256], VM, ZE[:, 4 + h, 2:3], None, ALU.mult)
                kb = []
                for n in range(4):
                    b, rel = banks.take()
                    for i in range(2):
                        m = mm(bank(b)[:, 256 * i:256 * i + 256], KM[:, 2 * n + i, :], VZ[:, 2 * n + i, :], True, True, [z2, y] + rel)
                    kb.append((b, m))
                m_kv = m
                u = cp(PV[:, 0, 0:128], SC[:, h, 0:128], prev["o"])
                v = cp(PV[:, 7, 128:256], SC[:, h, 128:256], prev["o"])
                for n in range(7):
                    b, m = kb[n // 2]
                    u = stt(PV[:, n + 1, 0:128], PV[:, n, 0:128], ZE[:, h, 3:4], bank(b)[:, 256 * (n % 2):256 * (n % 2) + 128],
                            ALU.mult, ALU.add, [u, m])
                    n2 = 7 - n
                    b, m = kb[n2 // 2]
                    v = stt(PV[:, n2 - 1, 128:256], PV[:, n2, 128:256], ZE[:, 4 + h, 3:4],
                            bank(b)[:, 256 * (n2 % 2) + 128:256 * (n2 % 2) + 256], ALU.mult, ALU.add, [v, m])
                for b, m in kb:
                    banks.free(b, [u, v])
                for dr in range(2):
                    qx = tt(QX[:, dr, :].rearrange("p (a b) -> p a b", a=8), QH.rearrange("p (a b) -> p a b", a=8),
                            XI[:, h, dr, :].unsqueeze(1).broadcast_to([128, 8, 128]), ALU.mult, done["q"] + prev["o"])
                sd = []
                for half in range(2):
                    b, rel = banks.take()
                    for i in range(4):
                        c = 512 * half + 128 * i
                        m = mm(bank(b)[:, 128 * i:128 * i + 128], KH[:, c:c + 128], QH[:, c:c + 128], True, True, done["q"] + rel)
                    y = tt(SS[:, 4 * half:4 * half + 4, :], bank(b).rearrange("p (a b) -> p a b", a=4),
                           DM[:, h, :].unsqueeze(1).broadcast_to([128, 4, 128]), ALU.mult, [m] + prev["o"])
                    banks.free(b, [y])
                    sd.append(y)
                prev["q"] = [m, qx]
                for half in range(2):
                    b, rel = banks.take()
                    for i in range(4):
                        n = 4 * half + i
                        o = bank(b)[:, 128 * i:128 * i + 128]
                        mm(o, VM[:, n, :], SS[:, n, :], True, False, [sd[half], u, v, qx] + rel)
                        mm(o, PV[:, n, 0:128], QX[:, 0, 128 * n:128 * n + 128], False, False)
                        m = mm(o, PV[:, n, 128:256], QX[:, 1, 128 * n:128 * n + 128], False, True)
                    c = 512 * half
                    oh = OH[:, c:c + 512]
                    y = cp(oh, bank(b), [m] + prev["g"] + oh_rel)
                    ti, trel = tr_.take()
                    q = ac(T1[:, ti, :], bank(b), ACT.Square, [y] + trel)
                    banks.free(b, [q])
                    b, rel = banks.take()
                    m2 = mm(bank(b), ones, T1[:, ti, :], True, True, [q] + rel)
                    v_ = ts(T2[:, ti, :], bank(b), 1.0 / 128, 1e-6, ALU.mult, ALU.add, after=[m2])
                    banks.free(b, [v_])
                    v_ = ac(T2[:, ti, :], T2[:, ti, :], ACT.Ln, [v_])
                    v_ = ac(T2[:, ti, :], T2[:, ti, :], ACT.Exp, [v_], scale=-0.5)
                    v_ = stt(oh, oh, 0.5, T2[:, ti, :], ALU.mult, ALU.mult, [v_])
                    tr_.free(ti, [v_])
                    v_ = tt(oh, oh, GH_[:, c:c + 512], ALU.mult, [v_] + done["g"])
                prev["o"], prev["v"] = [m], [m, z2]
                prev["k"] = [m_kv]
                prev["g"] = [v_]
                dd = sp.dma(ch("os2"), os_[h][:, 0:SEQ], OH, [v_])
                oh_rel[:] = [dd]
                pend.append(dd)
        oh_rel = []

        def fourier(ready):
            phase(FM[0])
            FTt = r3(4, 1024)
            CD = carve(256)
            OB = r3(2, 512)
            Y = r3(2, 512)
            d0 = sp.dma(ch("b3"), CD, A["k_cd"])
            w = A["w_in_2"][0]
            fin = []
            for g in range(4):
                def evac(o, c, n, m):
                    x = ac(FTt[:, g, c:c + n], o, ACT.Copy, [m])
                    fin.append(x)
                    return [x]
                for _ in gemm_f(wslice(w, 2048 + 128 * g), CH2, evac, ready):
                    pass
            alldone = pe.items[-1]
            AHf = AH[:, :, :].rearrange("p a b -> p (a b)")[:, 0:8192].rearrange("p (m g c) -> p m g c", m=8, g=4)
            ALf = AL[:, :, :].rearrange("p a b -> p (a b)")[:, 0:8192].rearrange("p (m g c) -> p m g c", m=8, g=4)
            for g in range(4):
                for mt in range(0, 8, 2):
                    b, rel = banks.take()
                    for i in range(2):
                        c = 128 * (mt + i)
                        m = mm(bank(b)[:, 256 * i:256 * i + 256], FTt[:, g, c:c + 128], CD, True, True, [d0, fin[2 * g + 1]] + rel)
                    src = bank(b).rearrange("p (a b) -> p a b", a=2)
                    h = ac(AHf[:, mt:mt + 2, g, :], src, ACT.Copy, [m, alldone])
                    lo = tt(ALf[:, mt:mt + 2, g, :], src, f(AHf[:, mt:mt + 2, g, :]), ALU.subtract, [h])
                    banks.free(b, [lo])
            bs = [banks.take() for _ in range(8)]
            for j in range(16):
                mt, cs = j // 2, j % 2
                t, wl_ = load_w(A["k_dft"][:, 1024 * j:1024 * j + 1024].rearrange("p (a b) -> p a b", a=1), 1024)
                for g in range(4):
                    yh = AHf[:, mt, g, 128 * cs:128 * cs + 128]
                    yl = ALf[:, mt, g, 128 * cs:128 * cs + 128]
                    for half in range(2):
                        b, rel = bs[2 * g + half]
                        wv = slice(512 * half, 512 * half + 512)
                        m = mm3(bank(b), yh, yl, WH[:, t, wv], WL[:, t, wv], j == 0, j == 15, [lo, wl_] + rel)
                wr.free(t, [m])
            orr = Ring(2)
            for g in range(4):
                for half in range(2):
                    b, _ = bs[2 * g + half]
                    i, rel = orr.take()
                    y = (ac if half else cp)(OB[:, i, :], bank(b), after=[m] + rel)
                    banks.free(b, [y])
                    dd = sp.dma(ch(f"g{i}"), os_[4 + g][:, 512 * half:512 * half + 512], OB[:, i, :], [y])
                    orr.free(i, [dd])
                    pend.append(dd)

        def mix_out():
            phase()
            MX = r3(8, 1024)
            OL = r3(2, 1024)
            GA = carve(1024)
            XL = r3(2, 1024)
            J = carve(1024)
            TB = r3(2, 512)
            S2 = carve(16)
            orr = Ring(2)
            for g in range(8):
                i, rel = orr.take()
                d = sp.dma(ch(f"o{i}"), OL[:, i, :], os_[g][:, 0:SEQ], rel)
                h = ac(AH[:, g, 0:SEQ], OL[:, i, :], ACT.Copy, [d])
                rd = tt(AL[:, g, 0:SEQ], OL[:, i, :], f(AH[:, g, 0:SEQ]), ALU.subtract, [h])
                orr.free(i, [rd])
            dg = sp.dma(ch("b4"), GA, gs_[0])

            def evac(b, t, rows, half, last):
                y = (ac if t % 2 else cp)(MX[:, t, 512 * half:512 * half + 512], b, after=[last])
                fin.append(y)
                return [y]
            fin = []
            out_proj(A["w_out_2"][0], [(t, 128 * t, 128) for t in range(8)], evac, [rd])
            ready = {}
            jr = []
            xrr = Ring(2)
            for t in range(8):
                x, r1, r2 = MX[:, t, :], RSTD[:, t:t + 1], RSTD[:, 8 + t:9 + t]
                q = ac(J, x, ACT.Square, [fin[t], fin[8 + t]] + jr, accum=r1)
                v = rstd_of(r1, 128, 1.0 / D, 1e-6, [q])
                y = stt(x, x, r1, GA, ALU.mult, ALU.mult, [v, dg, fin[8 + t]])
                i, rel = xrr.take()
                d = sp.dma(ch(f"r{i}"), XL[:, i, :], xs[128 * t:128 * t + 128, :], rel)
                y = tt(x, x, XL[:, i, :], ALU.add, [y, d])
                xrr.free(i, [y])
                st_ = sp.dma(ch(f"s{t % 4}"), xs[128 * t:128 * t + 128, :], x, [y])
                pend.append(st_)
                q = ac(J, x, ACT.Square, [y, q], accum=r2)
                jr = [q]
                v = rstd_of(r2, 128, 1.0 / D, 1e-6, [q])
                ready[t] = ts(x, x, r2, None, ALU.mult, after=[v, st_])
            return fill_a(list(range(8)), lambda t: MX[:, t, :], ready, 2, TB)[0]

        def ffn(ready):
            phase()
            CW = carve(4 * 44).rearrange("p (a b) -> p a b", a=4)
            NR = 15
            CV = r3(2, 1024)
            CU = r3(2, 1024)
            TH = r3(2, 1024)
            G = r3(NR, 1024)
            gsp = S["gsp"]
            d0 = sp.dma(ch("b5"), CW, A["k_conv"].rearrange("p (a b) -> p a b", a=4))
            w = A["w_up_2"][0]
            cvr, thr = Ring(2), Ring(2)

            def conv(o, dst, c, j, after):
                x = ac(dst[:, c:c + 512], o, ACT.Identity, after + [d0], scale=CW[:, 1, j:j + 1], bias=CW[:, 3, j:j + 1])
                d3 = dst[:, c:c + 512].rearrange("p (r t) -> p r t", t=64)
                o3 = o.rearrange("p (r t) -> p r t", t=64)
                y = stt(d3[:, :, 1:64], o3[:, :, 0:63], CW[:, 0, j:j + 1], d3[:, :, 1:64], ALU.mult, ALU.add, [x])
                return stt(d3[:, :, 0:63], o3[:, :, 1:64], CW[:, 2, j:j + 1], d3[:, :, 0:63], ALU.mult, ALU.add, [y])
            gdone = []
            for j in range(FT):
                ci, crel = cvr.take()
                ti, trel = thr.take()
                va, vb, th = CV[:, ci, :], CU[:, ci, :], TH[:, ti, :]
                ya, yb = [], []

                def evac(o, c, n, m):
                    y = conv(o, va, c, j, [m] + crel)
                    ya.append(y)
                    return [y]
                for _ in gemm_f(wslice(w, 128 * j), CH2, evac, ready):
                    pass
                t_ = ac(th, va, ACT.Tanh, ya + trel, scale=0.5)

                def evac(o, c, n, m):
                    y = conv(o, vb, c, FT + j, [m] + crel)
                    yb.append(y)
                    return [y]
                for _ in gemm_f(wslice(w, DFF + 128 * j), CH2, evac, ready):
                    pass
                a1 = stt(va, th, 1.0, va, ALU.add, ALU.mult, [t_])
                thr.free(ti, [a1])
                if j < NR:
                    a2 = stt(G[:, j, :], va, 0.5, vb, ALU.mult, ALU.mult, [a1, yb[-1]])
                    cvr.free(ci, [a2])
                else:
                    a2 = stt(va, va, 0.5, vb, ALU.mult, ALU.mult, [a1, yb[-1]])
                    a2 = sp.dma(ch(f"s{ci}"), gsp[j - NR], va, [a2])
                    cvr.free(ci, [a2])
                    pend.append(a2)
                gdone.append(a2)
            barrier()
            GL_ = CU
            wd = A["w_down_2"][0]
            glr, ar = Ring(2), Ring(8)
            F = {}
            fdone = {}
            for half in range(2):
                bs = [banks.take() for _ in range(8)]
                wt = None
                for k in range(FT):
                    if k % 2 == 0:
                        src = wd[128 * k:128 * k + 256, 512 * half:512 * half + 512].rearrange("(k p) n -> p k n", p=128)
                        wt, wlo = load_w(src, 512)
                    ai, arel = ar.take()
                    if k < NR:
                        src, dep = G[:, k, :], []
                    else:
                        gi_, grel = glr.take()
                        d = sp.dma(ch(f"g{gi_}"), GL_[:, gi_, :], gsp[k - NR], grel)
                        src, dep = GL_[:, gi_, :], [d]
                    h = ac(AH[:, ai, 0:SEQ], src, ACT.Copy, dep + arel)
                    lo = tt(AL[:, ai, 0:SEQ], src, f(AH[:, ai, 0:SEQ]), ALU.subtract, [h])
                    if k >= NR:
                        glr.free(gi_, [lo])
                    wv = slice(512 * (k % 2), 512 * (k % 2) + 512)
                    for t in range(8):
                        b, rel = bs[t]
                        m = mm3(bank(b), AH[:, ai, 128 * t:128 * t + 128], AL[:, ai, 128 * t:128 * t + 128],
                                WH[:, wt, wv], WL[:, wt, wv], k == 0, k == FT - 1, [lo, wlo] + (rel if k == 0 else []))
                        if k == FT - 1:
                            if half == 0:
                                dst = (CV if t < 4 else TH)[:, (t // 2) % 2, 512 * (t % 2):512 * (t % 2) + 512]
                            else:
                                dst = G[:, t, 0:512]
                            F[(t, half)] = dst
                            y = (ac if t % 2 else cp)(dst, bank(b), after=[m])
                            fdone[(t, half)] = y
                            banks.free(b, [y])
                    ar.free(ai, [m])
                    if k % 2 == 1:
                        wr.free(wt, [m])
            GA, XL, J = G[:, 8, :], G[:, 9:11, :], G[:, 11, :]
            last_mm = m
            dg = sp.dma(ch("b6"), GA, gs_[1], [lo])
            xrr = Ring(2)
            jr = []
            for t in range(8):
                r = RSTD[:, t:t + 1]
                r2 = RSTD[:, 8 + t:9 + t]
                q1 = ac(J[:, 0:512], F[(t, 0)], ACT.Square, [lo, fdone[(t, 0)]] + jr, accum=r)
                q = ac(J[:, 512:1024], F[(t, 1)], ACT.Square, [fdone[(t, 1)]], accum=r2)
                jr = [q]
                v = tt(r, r, r2, ALU.add, [q])
                v = rstd_of(r, 128, 1.0 / D, 1e-6, [v])
                i, rel = xrr.take()
                d = sp.dma(ch(f"r{i}"), XL[:, i, :], xs[128 * t:128 * t + 128, :], rel + [lo])
                for half in range(2):
                    hv = slice(512 * half, 512 * half + 512)
                    y = stt(F[(t, half)], F[(t, half)], r, GA[:, hv], ALU.mult, ALU.mult, [v, dg])
                    y = tt(XL[:, i, hv], XL[:, i, hv], F[(t, half)], ALU.add, [y, d])
                st_ = sp.dma(ch(f"s{i}"), O["out"][0][128 * t:128 * t + 128, :], XL[:, i, :], [y])
                xrr.free(i, [st_])

        if stage >= 3:
            ada_phase()
            tabs = ctx_phase()
            lo = prep_x(FM[0])
            mixer(*tabs, [lo])
            fourier([lo])
            lo = mix_out()
            ffn([lo])

        if dbg is not None:
            dbg(locals(), hs, os_, sp, ch, O)
        finish = [c for c in chans.values()]

        for q in (pe, act, dve, pool, sp):
            n = q.number()
        block = ctx.enter_context(nc.Block())

        @block.tensor
        def _(e):
            pe.emit(e)

        @block.scalar
        def _(e):
            act.emit(e)

        @block.vector
        def _(e):
            dve.emit(e)

        @block.gpsimd
        def _(e):
            pool.emit(e)

        @block.sync
        def _(e):
            sp.emit(e)
            for c in finish:
                e.wait_ge(c.sem, 16 * c.n)


def host_constants():
    f = np.float32
    c = {}
    c["k_ident"] = np.eye(128, dtype=f)
    q = np.arange(128)
    m = np.zeros((128, 2, 128), f)
    m[:, 0] = np.where((q[None, :] // 64) <= (q[:, None] // 64), 0.0, NEG)
    m[:, 1] = np.where(q[None, :] <= q[:, None], 0.0, NEG)
    c["k_mask"] = m.reshape(128, 256)
    s = np.zeros((128, 8, 128), f)
    for h in range(8):
        s[h, h] = -1.0
        s[32 + h, h] = -1.0
    c["k_sel"] = s.reshape(128, 1024)
    pos = np.arange(L, dtype=f)
    inv = (1.0 / (np.float32(500000.0) ** (np.arange(0, 16, 2, dtype=f) / np.float32(16)))).astype(f)
    ang = pos[None, :] * inv[:, None]
    cos, sin = np.ones((128, L), f), np.zeros((128, L), f)
    rot = np.zeros((128, 128), f)
    for b in (0, 64):
        cos[b:b + 8] = np.cos(ang)
        cos[b + 8:b + 16] = np.cos(ang)
        sin[b:b + 8] = -np.sin(ang)
        sin[b + 8:b + 16] = np.sin(ang)
        for i in range(8):
            rot[b + 8 + i, b + i] = 1.0
            rot[b + i, b + 8 + i] = 1.0
    c["k_cos"], c["k_sin"], c["k_rot"] = cos, sin, rot
    p = np.arange(128, dtype=f)
    dec = np.zeros((128, 776), f)
    dec[:, 0], dec[:, 1], dec[:, 2], dec[:, 3] = 255 - p, 127 - p, 127 - p, 128
    dec[:, 4], dec[:, 5], dec[:, 6], dec[:, 7] = p, 128 + p, p, 128
    dec[:, 8:136] = p[None, :] + 1
    dec[:, 136:264] = 128 - p[None, :]
    dec[:, 264:392] = np.maximum(p[None, :] - p[:, None], 0)
    dec[:, 392:520] = np.maximum(p[:, None] - p[None, :], 0)
    dec[:, 520:648] = (p[:, None] <= p[None, :])
    dec[:, 648:776] = (p[:, None] > p[None, :])
    c["k_dec"] = dec
    t = np.arange(SEQ)
    fr = (np.float32(10000.0) ** (-np.arange(32, dtype=f) / np.float32(32))).astype(f)
    ang = np.concatenate([(t // 64).astype(f)[:, None] * fr, (t % 64).astype(f)[:, None] * fr], 1).T
    c["k_cos2"] = np.concatenate([np.cos(ang), np.cos(ang)]).astype(f)
    c["k_sin2"] = np.concatenate([np.sin(ang), -np.sin(ang)]).astype(f)
    i = np.arange(128, dtype=np.int64)
    a = 2 * np.pi * ((i[:, None] * i[None, :]) % 128) / 128.0
    c["k_cd"] = (np.concatenate([np.cos(a), np.sin(a)], 1) / np.sqrt(1024.0 * 128.0)).astype(f)
    n = np.arange(SEQ, dtype=np.int64)
    a = 2 * np.pi * ((n[:, None] * n[None, :]) % SEQ) / float(SEQ)
    both = np.stack([np.cos(a), -np.sin(a)], 0).reshape(2, 8, 128, SEQ)
    c["k_dft"] = np.ascontiguousarray(both.transpose(2, 1, 0, 3).reshape(128, 16 * SEQ)).astype(f)
    return c


def layout(inputs):
    f = {k: np.asarray(v) for k, v in inputs.items()}
    a = dict(host_constants())
    for n in ("x", "meta_tokens", "w_in", "w_out"):
        a[n] = f[n]
    cols = np.zeros((128, 32), np.float32)
    for l in range(2):
        cols[:, 8 * l:8 * l + 8] = f["norm_gain"][l].reshape(8, 128).T
        cols[:, 16 + l] = f["subln_gain"][l]
        cols[0:8, 18 + l] = f["forget_bias"][l]
    a["k_cols"] = cols
    for n in ("ctx_2", "w_ada_2", "w_in_2", "w_out_2", "w_up_2", "w_down_2"):
        a[n] = f[n]

    def col(v):
        return v.reshape(-1, 128).T

    def rows(v, n=128):
        return np.repeat(v.reshape(1, -1), n, axis=0)
    a["k_c"] = np.stack([col(f["c_2"][0]), col(f["c_ctx_2"])], 2).reshape(128, 16)
    b = col(f["b_ada_2"][0])
    b = np.concatenate([b[:, 0:16], b[:, 24:40]], 1)
    a["k_bada"] = np.repeat(b[:, :, None], 2, 2).reshape(128, 64)
    a["k_brow"] = np.concatenate([f["b_ada_2"][0, 2048:3072], f["b_ada_2"][0, 5120:6144]]).reshape(1, 2048)
    a["k_gpre"] = np.concatenate([col(f["g_mix_pre_2"][0]), col(f["g_ffn_pre_2"][0])], 1)
    a["k_gpost"] = np.concatenate([rows(f["g_mix_post_2"][0]), rows(f["g_ffn_post_2"][0])], 1)
    k2 = np.zeros((128, 24), np.float32)
    k2[:, 0:4], k2[:, 4:8] = rows(f["ret_decay_fwd_2"][0]), rows(f["ret_decay_bwd_2"][0])
    a["k_cols2"] = k2
    a["k_fg"] = rows(f["final_gain"])
    cw = np.concatenate([f["conv_w_2"][0], f["conv_b_2"]], 0)
    a["k_conv"] = cw.reshape(4, 44, 128).transpose(2, 0, 1).reshape(128, 176)
    lam = np.stack([f["lambda_q1"], f["lambda_k1"], f["lambda_q2"], f["lambda_k2"]], 1).reshape(1, 512)
    a["k_lam"] = np.repeat(lam, 128, axis=0)
    return {k: np.ascontiguousarray(v) for k, v in a.items()}


SCRATCH = {"hs": (L, D), "os": (8, 128, L), "xs": (SEQ, D), "gs": (2, 128, D), "gsp": (FT - 15, 128, SEQ)}


def kernel(**inputs):
    import concourse.bacc as _bacc
    from concourse.bass_utils import run_bass_kernel_spmd as _run

    arrays = layout(inputs)
    nc = _bacc.Bacc("TRN2", target_bir_lowering=False, num_devices=1)
    A = {n: nc.dram_tensor(f"in_{n}", a.shape, mybir.dt.from_np(a.dtype), kind="ExternalInput").ap()
         for n, a in arrays.items()}
    S = {n: nc.dram_tensor(f"s_{n}", s, F32, kind="Internal").ap() for n, s in SCRATCH.items()}
    O = {"out": nc.dram_tensor("out_0", (1, SEQ, D), F32, kind="ExternalOutput").ap()}
    build(nc, A, S, O)
    r = _run(nc, [{f"in_{n}": a for n, a in arrays.items()}], core_ids=[0])
    return r.results[0]["out_0"]
```

```python
from contextlib import ExitStack

import numpy as np
import concourse.bass as bass
from concourse import mybir

F32 = mybir.dt.float32
F32R = mybir.dt.float32r
ALU = mybir.AluOpType
ACT = mybir.ActivationFunctionType
AX = mybir.AxisListType

SEQ = 1024
NM = 16
L = SEQ + NM
D = 1024
KT = 8
NT = 8
CH = [(0, 352), (352, 344), (696, 344)]
LAM_INIT = [0.8 - 0.6 * float(np.exp(-0.3 * l)) for l in range(2)]
NEG = -1e30
DFF = 2816
FT = DFF // 128


class Ins:

    def __init__(self, q, fn, after):
        self.q, self.fn, self.after = q, fn, after
        self.sig = False
        self.val = 0

    def need(self):
        self.sig = True


class Dma:

    def __init__(self, q, fn, after, chan):
        self.q, self.fn, self.after, self.chan = q, fn, after, chan
        chan.n += 1
        self.val = 16 * chan.n

    def need(self):
        pass


class Chan:
    def __init__(self, sem):
        self.sem, self.n = sem, 0


class Queue:

    def __init__(self, sem):
        self.sem, self.items = sem, []

    def add(self, fn, after=()):
        for a in after:
            a.need()
        i = Ins(self, fn, list(after))
        self.items.append(i)
        return i

    def dma(self, chan, out, in_, after=(), **kw):
        for a in after:
            a.need()
        i = Dma(self, lambda e: e.dma_start(out, in_, **kw), list(after), chan)
        self.items.append(i)
        return i

    def number(self):
        n = 0
        for i in self.items:
            if isinstance(i, Ins) and i.sig:
                n += 1
                i.val = n
        return n

    def emit(self, eng):
        seen = {}
        for i in self.items:
            want = {}
            for a in i.after:
                s = a.chan.sem if isinstance(a, Dma) else a.q.sem
                if a.val > seen.get(id(s), 0):
                    seen[id(s)] = a.val
                    want[id(s)] = (s, a.val)
            for s, v in want.values():
                eng.wait_ge(s, v)
            if i.fn is None:
                continue
            x = i.fn(eng)
            if isinstance(i, Dma):
                x.then_inc(i.chan.sem, 16)
            elif i.sig:
                x.then_inc(self.sem, 1)


class Ring:

    def __init__(self, n, base=0):
        self.n, self.i, self.base = n, 0, base
        self.rel = [[] for _ in range(n)]
        self.busy = [False] * n

    def ready(self):
        return not self.busy[self.i]

    def take(self):
        i = self.i
        assert not self.busy[i]
        self.busy[i] = True
        self.i = (i + 1) % self.n
        return i, self.rel[i]

    def free(self, i, ins):
        self.rel[i] = list(ins)
        self.busy[i] = False


def pieces(a, b, step=512):
    out = []
    while a < b:
        e = min(b, (a // step + 1) * step)
        out.append((a, e))
        a = e
    return out


def build(nc, A, S, O, dbg=None, stage=9):
    ctx = ExitStack()
    with ctx:
        def sb(name, shape, dt=F32):
            return ctx.enter_context(nc.sbuf_tensor(name, shape, dt))

        def sem(name):
            return ctx.enter_context(nc.semaphore(name))

        pe, act, dve, pool, sp = (Queue(sem(n)) for n in ("q_pe", "q_act", "q_dve", "q_pool", "q_sp"))
        chans = {}

        def ch(name):
            if name not in chans:
                chans[name] = Chan(sem("d_" + name))
            return chans[name]

        PS = ctx.enter_context(nc.psum_tensor("PS", [128, 8, 512], F32))
        PSf = PS[:, :, :].rearrange("p a b -> p (a b)")
        AH = sb("AH", [128, KT, L], F32R)
        AL = sb("AL", [128, KT, L], F32R)
        W32 = sb("W32", [128, 3, 1024])
        NW = 3
        WH = sb("WH", [128, NW, 1024], F32R)
        WL = sb("WL", [128, NW, 1024], F32R)
        identr = sb("identr", [128, 128], F32R)
        maskr = sb("maskr", [128, 2, 128], F32R)
        selr = sb("selr", [128, 8, 128], F32R)
        C2 = sb("C2", [128, L], F32R)
        RW = 24192
        R = sb("R", [128, RW])
        at = [0]

        def carve(n):
            v = R[:, at[0]:at[0] + n]
            at[0] += n
            assert at[0] <= RW, at[0]
            return v

        def c3(a, b):
            return carve(a * b).rearrange("p (a b) -> p a b", a=a)

        ident = carve(128)
        ones = carve(128)
        SM = carve(64)
        COLS = carve(96)
        persist = at[0]

        def mm(out, lhsT, rhs, start=True, stop=True, after=()):
            return pe.add(lambda e: e.matmul(out, lhsT, rhs, start=start, stop=stop, skip_group_check=True), after)

        def mm3(out, wh, wl, xh, xl, start, stop, after=()):
            mm(out, wh, xh, start, False, after)
            mm(out, wh, xl, False, False)
            return mm(out, wl, xh, False, stop)

        def tr(out, in_, after=()):
            k = in_.shape[0]
            return pe.add(lambda e: e.transpose(out, in_, ident[0:k, 0:k]), after)

        def ac(out, in_, func=ACT.Copy, after=(), scale=1.0, bias=None, accum=None):
            kw = {"scale": scale}
            if bias is not None:
                kw["bias"] = bias
            if accum is not None:
                kw["accum_out"] = accum
            return act.add(lambda e: e.activation(out, in_, func, **kw), after)

        def tt(out, a, b, op, after=(), q=None):
            return (q or dve).add(lambda e: e.tensor_tensor(out, a, b, op), after)

        def ts(out, a, s1, s2, op0, op1=None, after=(), q=None):
            if op1 is None:
                return (q or dve).add(lambda e: e.tensor_scalar(out, a, s1, None, op0), after)
            return (q or dve).add(lambda e: e.tensor_scalar(out, a, s1, s2, op0, op1), after)

        def stt(out, a, s, b, op0, op1, after=()):
            return dve.add(lambda e: e.scalar_tensor_tensor(out, a, s, b, op0, op1), after)

        def cp(out, a, after=(), q=None):
            return (q or dve).add(lambda e: e.tensor_copy(out, a), after)

        def rmax_neg(out, a, after=()):
            return dve.add(lambda e: e.tensor_reduce(out, a, AX.X, ALU.max, negate=True), after)

        def recip(out, a, after=()):
            return dve.add(lambda e: e.reciprocal(out, a), after)

        def f(x):
            return x.bitcast(F32)

        def barrier():
            last = []
            for q in (pe, act, dve, pool):
                real = [i for i in q.items[-200:] if i.fn is not None and isinstance(i, Ins)]
                last += real[-1:]
            for q in (pe, act, dve, pool):
                q.add(None, [x for x in last if x.q is not q] + pend)
            del pend[:]
        pend = []

        banks = Ring(3, 5)
        sA, sB = Ring(1), Ring(1)
        w32 = Ring(3)
        wr = Ring(NW)

        def banks_set(n, base):
            assert not any(banks.busy)
            rel = sum(banks.rel, []) + sA.rel[0] + sB.rel[0]
            banks.n, banks.base, banks.i = n, base, 0
            banks.rel = [list(rel) for _ in range(n)]
            banks.busy = [False] * n
            sA.rel[0] = list(rel)
            sB.rel[0] = list(rel)

        def banks_all():
            banks_set(8, 0)

        def banks_few():
            banks_set(3, 5)

        def bank(i):
            return PS[:, banks.base + i, :]

        dve.add(lambda e: e.memset(ones, 1.0))
        cm = w32.take()[0]
        c0 = [sp.dma(ch("c0"), ident, A["k_ident"]),
              sp.dma(ch("c0"), W32[:, cm, 0:256], A["k_mask"]),
              sp.dma(ch("c0"), COLS[:, 0:32], A["k_cols"])]
        cn = w32.take()[0]
        c0.append(sp.dma(ch("c0"), W32[:, cn, :], A["k_sel"]))
        x1 = ac(identr[:, :], ident, after=c0)
        x2 = ac(maskr[:, :, :].rearrange("p a b -> p (a b)"), W32[:, cm, 0:256])
        x3 = ac(selr[:, :, :].rearrange("p a b -> p (a b)"), W32[:, cn, :])
        w32.free(cm, [x3])
        w32.free(cn, [x3])
        cz = dve.add(lambda e: e.memset(f(C2[:, :]), 0.0))
        consts = [x3, cz]

        def wslice(w, c, n=128):
            return w[:, c:c + n].rearrange("(k p) n -> p k n", p=128)

        class Weights:
            AHEAD = 1

            def __init__(self, plan):
                self.plan = list(plan)
                self.loaded, self.split, self.used = 0, 0, 0
                self.dmas, self.parts = {}, {}

            def load(self):
                while self.loaded < len(self.plan) and w32.ready():
                    src, _ = self.plan[self.loaded]
                    s, rel = w32.take()
                    d = sp.dma(ch(f"w{s}"), W32[:, s, :].rearrange("p (a b) -> p a b", a=src.shape[1]), src, rel)
                    self.dmas[self.loaded] = (s, d)
                    self.loaded += 1

            def prepare(self, upto):
                self.load()
                while self.split <= min(upto, len(self.plan) - 1):
                    i = self.split
                    if not self.plan[i][1]:
                        if i >= self.used:
                            return
                        self.split += 1
                        continue
                    if i not in self.dmas or not wr.ready():
                        return
                    s, d = self.dmas[i]
                    t, rel = wr.take()
                    h = ac(WH[:, t, :], W32[:, s, :], after=[d] + rel)
                    lo = tt(WL[:, t, :], W32[:, s, :], f(WH[:, t, :]), ALU.subtract, [h])
                    w32.free(s, [lo])
                    self.parts[i] = (t, lo)
                    self.split += 1
                    self.load()

            def next(self, split=True):
                i = self.used
                assert self.plan[i][1] == split
                if split:
                    self.prepare(i + self.AHEAD)
                    self.used += 1
                    return self.parts[i]
                self.load()
                self.used += 1
                return self.dmas[i]

        def out_srcs(w):
            for q in range(4):
                for kk in range(2):
                    yield (w[512 * kk:512 * kk + 512, 256 * q:256 * q + 256].rearrange("(k p) n -> p k n", p=128), True)

        C0 = {"q": (0, 2048), "k": (512, 2560), "v": (1024, 3072), "g": (1536, 3592)}

        def wcol(kind, g):
            return C0[kind][g // 4] + 128 * (g % 4)

        def ada_srcs(i0):
            for i in range(i0, i0 + 4):
                for kk in range(4):
                    yield (A["w_ada_2"][0][256 * kk:256 * kk + 256, 512 * i:512 * i + 512]
                           .rearrange("(k p) n -> p k n", p=128), False)

        def weight_plan():
            yield from ada_srcs(0)
            for l in range(2):
                yield (wslice(A["w_in"][l], 3584), True)
                for g in range(8):
                    for kind in "qkvg":
                        yield (wslice(A["w_in"][l], wcol(kind, g)), True)
                yield from out_srcs(A["w_out"][l])
                yield from ada_srcs(4 * l + 4)
            w = A["w_in_2"][0]
            yield from out_srcs(w[:, 512:1536])
            for h in range(4):
                for kind in range(4):
                    yield (wslice(w, 512 * kind + 128 * h), True)
            for g in range(4):
                yield (wslice(w, 2048 + 128 * g), True)
            for j in range(16):
                yield (A["k_dft"][:, 1024 * j:1024 * j + 1024].rearrange("p (a b) -> p a b", a=1), True)
            yield from out_srcs(A["w_out_2"][0])
            w = A["w_up_2"][0]
            for j in range(FT):
                yield (wslice(w, 128 * j), True)
                yield (wslice(w, DFF + 128 * j), True)
            wd = A["w_down_2"][0]
            for half in range(2):
                for k in range(0, FT, 2):
                    yield (wd[128 * k:128 * k + 256, 512 * half:512 * half + 512].rearrange("(k p) n -> p k n", p=128), True)

        weights = Weights(weight_plan())

        def gemm_f(nch, evac, ready):
            t, lo = weights.next()
            wh = WH[:, t, :].rearrange("p (k m) -> p k m", k=KT)
            wl = WL[:, t, :].rearrange("p (k m) -> p k m", k=KT)
            for c, n in nch:
                while not banks.ready():
                    yield
                b, rel = banks.take()
                o = bank(b)[:, 0:n]
                for k in range(KT):
                    m = mm3(o, wh[:, k, :], wl[:, k, :], AH[:, k, c:c + n], AL[:, k, c:c + n],
                            k == 0, k == KT - 1, [lo] + ready + rel if k == 0 else [])
                last = m
                r = evac(o, c, n, m)
                banks.free(b, r)
                if c == nch[-1][0]:
                    wr.free(t, [last])
                yield 24 * n / 2360.0

        cosT = carve(L)
        sinT = carve(L)
        rotm = carve(128)
        V = carve(2 * 9 * 128).rearrange("p (s t n) -> p s t n", s=2, t=9)
        QT = c3(2, L)
        KTt = c3(2, L)
        GT = c3(2, L)
        OTt = c3(1, L)
        TMP = c3(1, L)
        CS = c3(8, 2)
        CT = c3(8, 2)
        ADB = c3(2, 512)
        b1base = at[0]
        P = c3(4, L)
        PT = carve(2 * 9 * 256).rearrange("p (s t n) -> p s t n", s=2, t=9)
        ST = carve(64).rearrange("p (s n) -> p s n", s=8)
        HB = R[:, b1base:b1base + 4 * 1024].rearrange("p (a b) -> p a b", a=4)
        SQJ = PT[:, 0, :, :].rearrange("p t n -> p (t n)")[:, 0:1024]
        ctab = [sp.dma(ch("c1"), cosT, A["k_cos"]), sp.dma(ch("c1"), sinT, A["k_sin"]),
                sp.dma(ch("c1"), rotm, A["k_rot"])]
        consts = consts + ctab + c0

        LB = SM[:, 0:2]
        RSTD = SM[:, 8:26]
        lt = P[:, 0, 0:512].rearrange("p (l a n) -> p l a n", l=2, a=4)
        dl = sp.dma(ch("c2"), P[:, 0, 0:512], A["k_lam"])
        for l in range(2):
            pr = P[:, 1, 0:128].rearrange("p (a n) -> p a n", a=2)
            x = tt(pr, lt[:, l, 0:4:2, :], lt[:, l, 1:4:2, :], ALU.mult, [dl] if l == 0 else [y])
            y = dve.add(lambda e, o=SM[:, 2:4], a=pr: e.tensor_reduce(o, a, AX.X, ALU.add), [x] + ([z] if l else []))
            z = ac(SM[:, 4:6], SM[:, 2:4], ACT.Exp, [y] + ([y2] if l else []))
            y1 = tt(SM[:, 6:7], SM[:, 5:6], SM[:, 4:5], ALU.subtract, [z])
            y2 = ts(LB[:, l:l + 1], SM[:, 6:7], -LAM_INIT[l], None, ALU.add, after=[y1])
            y = y2
        x = pool.dma(ch("a0"), CS, A["k_c"].rearrange("p (k c) -> p k c", k=8))
        x = ac(CT, CS, ACT.Exp, [x], scale=-1.0)
        x = ts(CT, CT, 1.0, None, ALU.add, after=[x])
        x = recip(CT, CT, [x])
        csd = tt(CS, CS, CT, ALU.mult, [x])
        pend.extend(ctab + c0)
        barrier()

        hs = S["hs"]
        os_ = S["os"]

        def stats(srcs, cols, eps, junk):
            q = None
            for i, (x, after) in enumerate(srcs):
                r = x.shape[0]
                q = ac(junk[0:r, :], x, ACT.Square, after + ([q] if q else []), accum=cols[0:r, i:i + 1])
            v = ts(cols[0:r, :], cols[0:r, :], 1.0 / D, eps, ALU.mult, ALU.add, [q])
            v = ac(cols[0:r, :], cols[0:r, :], ACT.Ln, [v])
            return ac(cols[0:r, :], cols[0:r, :], ACT.Exp, [v], scale=-0.5)

        def fill_a(tiles, ready, gain, bias=None, tb=None):
            tr_ = Ring(2)
            groups_ = [tiles[i:i + 4] for i in range(0, len(tiles), 4)]
            at_ = 0
            for g in groups_:
                tot = sum(x.shape[0] for x, _ in g)
                c = g[0][1]
                for k in range(KT):
                    b, rel = banks.take()
                    o = 0
                    for i, (x, _) in enumerate(g):
                        r = x.shape[0]
                        m = tr(bank(b)[:, o:o + r], x[:, 128 * k:128 * k + 128], [ready[at_ + i]] + rel)
                        o += r
                    dst_h, dst_l = AH[:, k, c:c + tot], AL[:, k, c:c + tot]
                    if bias is None:
                        h = ac(dst_h, bank(b)[:, 0:tot], ACT.Copy, [m], scale=gain(k))
                        lo = stt(dst_l, bank(b)[:, 0:tot], gain(k), f(dst_h), ALU.mult, ALU.subtract, [h])
                        banks.free(b, [lo])
                    else:
                        ti, trel = tr_.take()
                        tv = tb[:, ti, 0:tot]
                        h = ac(tv, bank(b)[:, 0:tot], ACT.Identity, [m] + trel, scale=gain(k), bias=bias(k))
                        banks.free(b, [h])
                        h2 = cp(dst_h, tv, [h])
                        lo = tt(dst_l, tv, f(dst_h), ALU.subtract, [h2])
                        tr_.free(ti, [lo])
                at_ += len(g)
            return lo, m

        vring, qring, gring = Ring(2), Ring(2), Ring(2)
        groups = {}
        pring, ptring, oring, tring = Ring(4), Ring(2), Ring(1), Ring(1)
        def ff_phase(l, ready):
            zt = TMP[:, 0, :]
            e1 = GT[:, 0, :]
            e2 = GT[:, 1, :]
            last = []

            def evac(o, c, n, m):
                x = ac(zt[0:8, c:c + n], o[0:8, :], ACT.Identity, [m], bias=COLS[0:8, 18 + l:19 + l])
                last.append(x)
                return [x]
            yield from gemm_f(CH, evac, ready)
            z, a, u = zt[0:8, :], e1[0:8, :], e2[0:8, :]
            m1 = ts(a, z, -1.0, None, ALU.mult, after=last)
            m1 = tt(a, a, z, ALU.max, [m1])
            m2 = ac(a, a, ACT.Exp, [m1], scale=-1.0)
            m3 = ts(u, a, 1.0, None, ALU.add, after=[m2])
            m4 = ts(z, z, 0.0, None, ALU.min)
            m5 = stt(a, u, -1.0, a, ALU.add, ALU.subtract, [m3])
            m6 = tt(z, z, a, ALU.add, [m4, m5])
            m7 = ac(u, u, ACT.Ln, [m3, m5])
            m8 = tt(z, z, u, ALU.subtract, [m6, m7])
            m9 = dve.add(lambda e: e.memset(u, 1.0), [m8])
            m10 = dve.add(lambda e: e.tensor_tensor_scan(a, u, z, 0.0, ALU.mult, ALU.add), [m9])
            h = ac(C2[0:8, :], a, ACT.Copy, [m10])
            lo = tt(C2[32:40, :], a, f(C2[0:8, :]), ALU.subtract, [h])
            ffdone[:] = [lo]
            tring.rel[0] = [lo]

        ffdone = []

        def proj(l, g, ready):
            fox = g >= 4
            while not qring.ready():
                yield 0
            s, qrel = qring.take()
            fin = {"q": [], "k": [], "g": [], "v": []}
            me = {"s": s, "fin": fin, "have": set()}
            groups[(l, g)] = me
            for kind, dst in (("q", QT), ("k", KTt)):
                sc = 0.125 if kind == "q" else 1.0
                if fox:
                    def evac(o, c, n, m, dst=dst, sc=sc, kind=kind):
                        x = ac(dst[:, s, c:c + n], o, ACT.Copy, [m] + qrel, scale=sc)
                        fin[kind].append(x)
                        return [x]
                    yield from gemm_f(CH, evac, ready)
                else:
                    while not tring.ready():
                        yield
                    ti, trel = tring.take()
                    part = []

                    def evac(o, c, n, m, sc=sc):
                        x = ac(TMP[:, ti, c:c + n], o, ACT.Copy, [m] + trel, scale=sc)
                        part.append((c, n, x))
                        return [x]
                    yield from gemm_f(CH, evac, ready)
                    for c, n, x in part:
                        while not banks.ready():
                            yield
                        b, rel = banks.take()
                        m = mm(bank(b)[:, 0:n], rotm, TMP[:, ti, c:c + n], True, True, [x] + rel)
                        y = tt(dst[:, s, c:c + n], bank(b)[:, 0:n], sinT[:, c:c + n], ALU.mult, [m] + qrel)
                        banks.free(b, [y])
                        y2 = tt(TMP[:, ti, c:c + n], TMP[:, ti, c:c + n], cosT[:, c:c + n], ALU.mult, [m], q=pool)
                        y3 = tt(dst[:, s, c:c + n], dst[:, s, c:c + n], TMP[:, ti, c:c + n], ALU.add, [y, y2])
                        fin[kind].append(y3)
                        yield 0.6
                    tring.free(ti, [fin[kind][-1]])
                me["have"].add(kind)
            while not (tring.ready() and vring.ready()):
                yield 0
            vs, vrel = vring.take()
            me["vs"] = vs
            ti, trel = tring.take()
            part = []

            def evac(o, c, n, m):
                x = ac(TMP[:, ti, c:c + n], o, ACT.Copy, [m] + trel)
                part.append(x)
                return [x]
            yield from gemm_f(CH, evac, ready)
            for quad in ((0, 1, 2, 3), (4, 5, 6, 7), (8,)):
                while not banks.ready():
                    yield
                b, rel = banks.take()
                for i, t in enumerate(quad):
                    cc, n = (16 + 128 * t, 128) if t < 8 else (0, 16)
                    m = tr(bank(b)[0:n, 128 * i:128 * i + 128], TMP[:, ti, cc:cc + n], [part[-1]] + rel)
                if quad[0] < 8:
                    x = cp(V[:, vs, quad[0]:quad[0] + 4, :], bank(b)[:, 0:512].rearrange("p (a b) -> p a b", a=4), [m] + vrel)
                else:
                    x = cp(V[0:16, vs, 8, :], bank(b)[0:16, 0:128], [m] + vrel)
                banks.free(b, [x])
                fin["v"].append(x)
                yield 0.5
            tring.free(ti, [m])
            me["have"].add("v")
            while not gring.ready():
                yield 0
            gs, grel = gring.take()
            me["gs"] = gs

            def evac(o, c, n, m):
                x = ac(GT[:, gs, c:c + n], o, ACT.Tanh, [m] + grel + ffdone, scale=0.5)
                y = stt(GT[:, gs, c:c + n], GT[:, gs, c:c + n], 1.0, o, ALU.add, ALU.mult, [x])
                fin["g"].append(y)
                return [y]
            yield from gemm_f(CH, evac, ready)
            me["have"].add("g")
            yield 0

        stn = [0]
        strel = [[] for _ in range(8)]

        class Attention:

            def __init__(self, l, g):
                self.l, self.g, self.fox = l, g, g >= 4
                self.blocks = [(6, 7), (4, 5), (2, 3), (0, 1)] + ([(8,)] if l == 0 else [])
                self.by, self.pts, self.o_done = {}, {}, []

            def units(self, bi):
                return [(j, m) for m in range(2) for j in reversed(self.blocks[bi])]

            def scores(self, j, m):
                fox, l, g, me = self.fox, self.l, self.g, groups[(self.l, self.g)]
                s = me["s"]
                qk = [me["fin"]["q"][-1], me["fin"]["k"][-1]]
                ring, b0 = (sA, 0) if j % 2 == 1 else (sB, 3)
                _, rel = ring.take()
                pi, prel = pring.take()
                meta = j == 8
                q0 = 0 if meta else NM + 128 * j
                W = NM if meta else NM + 128 * (j + 1)
                off = 512 * b0
                rows = NM if meta else 128
                dm0 = 0 if meta else W - 128
                r0 = 64 * m
                for i, (a, b) in enumerate(pieces(0, W)):
                    x = mm(PSf[:, off + a:off + b], QT[r0:r0 + 64, s, q0:q0 + 128], KTt[r0:r0 + 64, s, a:b], True, False,
                           qk + rel if i == 0 else [])
                    if fox:
                        x = mm(PSf[:, off + a:off + b], selr[:, 2 * (g - 4) + m, :], C2[:, a:b], False, False, ffdone)
                if fox or not meta:
                    for a, b in pieces(dm0, W):
                        x = mm(PSf[:, off + a:off + b], identr[:, :], maskr[:, int(fox), a - dm0:b - dm0], False, True)
                si = stn[0] % 8
                stn[0] += 1
                st = ST[0:rows, si, :]
                w = PSf[0:rows, off:off + W]
                n = rmax_neg(st[:, 0:1], w, [x] + strel[si])
                p = P[0:rows, pi, 0:W]
                e = ac(p, w, ACT.Exp, [n] + prel, bias=st[:, 0:1], accum=st[:, 1:2])
                ring.free(0, [e])
                if (j, m) == self.units(len(self.blocks) - 1)[-1]:
                    qring.free(s, [x])
                self.by[(j, m)] = (pi, rows, W, e, si)

            def normalise(self, bi):
                blk = self.blocks[bi]
                for j, m in self.units(bi):
                    pi, rows, W, e, si = self.by[(j, m)]
                    st = ST[0:rows, si, :]
                    p = P[0:rows, pi, 0:W]
                    r = recip(st[:, 2:3], st[:, 1:2], [e])
                    if self.fox or m == 0:
                        y = ts(p, p, st[:, 2:3], None, ALU.mult, after=[r])
                    else:
                        y = ts(st[:, 3:4], st[:, 2:3], LB[0:rows, self.l:self.l + 1], None, ALU.mult, after=[r])
                        p0 = self.by[(j, 0)][0]
                        y = stt(P[0:rows, p0, 0:W], p, st[:, 3:4], P[0:rows, p0, 0:W], ALU.mult, ALU.add, [y, self.by[(j, 0)][3]])
                        pring.free(pi, [y])
                        self.by[(j, 0)] = (p0, rows, W, y, self.by[(j, 0)][4])
                    strel[si] = [y]
                    if self.fox or m == 0:
                        self.by[(j, m)] = (pi, rows, W, y, si)

            def transposes(self, bi):
                blk = self.blocks[bi]
                meta = blk == (8,)
                nq = NM if meta else 256
                tiles = [8] if meta else [8] + list(range(blk[1] + 1))
                pts = []
                for m in (range(2) if self.fox else range(1)):
                    pt, ptrel = ptring.take()
                    evs = []
                    todo = [tiles[0:1]] + [tiles[i:i + 2] for i in range(1, len(tiles), 2)]
                    for grp in todo:
                        b, rel = banks.take()
                        kr = NM if grp[0] == 8 else 128
                        for i, t in enumerate(grp):
                            for jj, j in enumerate(blk):
                                if t < 8 and t > j:
                                    continue
                                p0, rows, W, y, _ = self.by[(j, m)]
                                ka = 0 if t == 8 else NM + 128 * t
                                x = tr(bank(b)[0:kr, 256 * i + 128 * jj:256 * i + 128 * jj + rows],
                                       P[0:rows, p0, ka:ka + kr], [y] + rel)
                        if grp[0] == 8:
                            ev = [evac_pt(PT[0:kr, pt, 8, 0:nq], bank(b)[0:kr, 0:nq], [x] + ptrel)]
                        elif grp[-1] == blk[-1]:
                            ev = [cp(PT[:, pt, grp[0], :], bank(b)[:, 0:256], [x] + ptrel),
                                  cp(PT[:, pt, grp[1], 128:256], bank(b)[:, 384:512], [x])]
                        else:
                            ev = [evac_pt(PT[:, pt, grp[0]:grp[0] + 2, :].rearrange("p a b -> p (a b)"),
                                          bank(b)[:, 0:512], [x] + ptrel)]
                        banks.free(b, ev)
                        evs += ev
                    for j in blk:
                        pring.free(self.by[(j, m)][0], [x])
                    pts.append((pt, evs))
                self.pts[bi] = (pts, tiles, nq, meta)

            def values(self, bi):
                me = groups[(self.l, self.g)]
                blk = self.blocks[bi]
                fox, vs, fin = self.fox, me["vs"], me["fin"]
                pts, tiles, nq, meta = self.pts[bi]
                q0 = 0 if meta else NM + 128 * blk[0]
                if bi == 0:
                    self.oi, self.orel = oring.take()
                ab, arel = banks.take()
                for i, t in enumerate(tiles):
                    for m, (pt, evs) in enumerate(pts):
                        mr = (64 * m, 64) if fox else (0, 128)
                        vc = slice(64 * m, 64 * m + 64) if fox else slice(0, 128)
                        kr = NM if t == 8 else 128
                        qa = 128 if (not meta and t == blk[1]) else 0
                        x = mm(bank(ab)[mr[0]:mr[0] + mr[1], qa:nq], V[0:kr, vs, t, vc], PT[0:kr, pt, t, qa:nq],
                               i == 0, i == len(tiles) - 1, evs + fin["v"] + arel if i == 0 else [])
                for pt, _ in pts:
                    ptring.free(pt, [x])
                y = cp(OTt[:, self.oi, q0:q0 + nq], bank(ab)[:, 0:nq], [x] + self.orel)
                banks.free(ab, [y])
                self.o_done.append(y)
                if bi == len(self.blocks) - 1:
                    vring.free(vs, [x])

            def finish(self):
                l, g, me = self.l, self.g, groups[(self.l, self.g)]
                gs, fin, oi = me["gs"], me["fin"], self.oi
                o = OTt[:, oi, :]
                cs = CH if l == 0 else [(NM, 352), (NM + 352, 336), (NM + 688, 336)]
                a, b_ = cs[0][0], cs[-1][0] + cs[-1][1]
                if not self.fox:
                    while not tring.ready():
                        yield
                    ti, trel = tring.take()
                    t = TMP[:, ti, :]
                    q = ac(t[:, a:b_], o[:, a:b_], ACT.Square, [self.o_done[-1]] + trel)
                    yield
                    vv = []
                    for c, n in cs:
                        b, rel = banks.take()
                        x = mm(bank(b)[:, 0:n], ones, t[:, c:c + n], True, True, [q] + rel)
                        v = ts(t[:, c:c + n], bank(b)[:, 0:n], 1.0 / 128, 1e-5, ALU.mult, ALU.add, [x])
                        banks.free(b, [v])
                        vv.append(v)
                    v = ac(t[:, a:b_], t[:, a:b_], ACT.Ln, vv)
                    v = ac(t[:, a:b_], t[:, a:b_], ACT.Exp, [v], scale=-0.5)
                    v = stt(o[:, a:b_], o[:, a:b_], COLS[:, 16 + l:17 + l], t[:, a:b_], ALU.mult, ALU.mult, [v])
                    tring.free(ti, [v])
                    sc = 0.5 * (1.0 - LAM_INIT[l])
                else:
                    v = self.o_done[-1]
                    sc = 0.5
                c, n = (0, L) if l == 0 else (NM, SEQ)
                y = stt(o[:, c:c + n], o[:, c:c + n], sc, GT[:, gs, c:c + n], ALU.mult, ALU.mult, [v, fin["g"][-1]])
                gring.free(gs, [y])
                self.gated = y
                if g == 7:
                    oring.free(oi, [y])
                else:
                    dst = pool.dma(ch(f"os{g % 2}"), os_[g][:, c:c + n], o[:, c:c + n], [y])
                    oring.free(oi, [dst])
                    os_done.append(dst)
                yield

        def evac_pt(o, a, after):
            epar[0] ^= 1
            return ac(o, a, ACT.Copy, after) if epar[0] else cp(o, a, after)

        BUDGET = [13.0, 12.0, 10.0, 8.0, 2.0]

        def attention_phase(l, ready):
            filler = chain(*[proj(l, g, ready) for g in range(8)])
            alive = [True]

            def fill(us):
                while us > 0 and alive[0]:
                    c = next(filler, None)
                    if c is None:
                        alive[0] = False
                    elif c == 0:
                        return
                    else:
                        us -= c

            def split_o(g, src, after):
                c, n = (0, L) if l == 0 else (NM, SEQ)
                h = ac(AH[:, g, c:c + n], src[:, c:c + n], ACT.Copy, after + lastproj)
                lo = tt(AL[:, g, c:c + n], src[:, c:c + n], f(AH[:, g, c:c + n]), ALU.subtract, [h])
                return lo

            def reload(n):
                for _ in range(n):
                    g = len(los)
                    if g >= 7 or g >= len(os_done):
                        return
                    if not lastproj:
                        lastproj.append([i for i in pe.items if i.fn is not None][-1])
                        sl = qring.i
                        stage_rel[:] = [qring.rel[sl], qring.rel[sl]]
                        stage[:] = [QT[:, sl, :], KTt[:, sl, :]]
                        assert qring.ready()
                    j = g % 2
                    c, n_ = (0, L) if l == 0 else (NM, SEQ)
                    d = pool.dma(ch(f"o{j}"), stage[j][:, c:c + n_], os_[g][:, c:c + n_], stage_rel[j] + [os_done[g]])
                    lo = split_o(g, stage[j], [d])
                    stage_rel[j] = [lo]
                    los.append(lo)
            lastproj, stage, stage_rel, los = [], [], [[], []], []

            def have(g, kind):
                while kind not in groups.get((l, g), {"have": ()})["have"]:
                    n = len(pe.items)
                    assert next(filler, None) is not None or kind in groups[(l, g)]["have"]

            atts = [Attention(l, g) for g in range(8)]
            seq = [(a, bi) for a in atts for bi in range(len(a.blocks))]
            have(0, "k")
            for u in atts[0].units(0):
                atts[0].scores(*u)
            atts[0].normalise(0)
            fill(8)
            for i, (a, bi) in enumerate(seq):
                a.transposes(bi)
                nxt = seq[i + 1] if i + 1 < len(seq) else None
                us = []
                if nxt:
                    have(nxt[0].g, "k")
                    us = nxt[0].units(nxt[1])
                    for u in us[:2]:
                        nxt[0].scores(*u)
                have(a.g, "v")
                a.values(bi)
                for u in us[2:]:
                    nxt[0].scores(*u)
                if nxt:
                    nxt[0].normalise(nxt[1])
                last = bi == len(a.blocks) - 1
                if a.g == 7:
                    fill(1000)
                    assert not alive[0] or last is not None
                    if not alive[0]:
                        reload(2)
                b = BUDGET[bi]
                if last:
                    have(a.g, "g")
                    for _ in a.finish():
                        fill(3)
                        b -= 3
                fill(b)
            reload(7)
            assert len(los) == 7
            a = atts[7]
            y = a.gated
            los.append(split_o(7, OTt[:, a.oi, :], [y]))
            oring.rel[0] = [los[-1]]
            for r in (qring, vring, gring, tring):
                assert r.ready()
            qring.rel[0] = qring.rel[0] + los[-3:]
            qring.rel[1] = qring.rel[1] + los[-3:]
            del os_done[:]
            os_rel[:] = []
            return [los[-1]]

        epar = [0]
        os_rel = []
        os_done = []

        def chain(*gs):
            for g in gs:
                yield from g

        def out_proj(tiles, evac, ready):
            nb = (len(tiles) + 1) // 2
            for q in range(4):
                bs = [banks.take() for _ in range(nb)]
                for kk in range(2):
                    ti, lo = weights.next()
                    for t, col in enumerate(tiles):
                        b, rel = bs[t // 2]
                        o = bank(b)[:, 256 * (t % 2):256 * (t % 2) + 256]
                        for k in range(4):
                            wv = slice(256 * k, 256 * k + 256)
                            kt = 4 * kk + k
                            m = mm3(o, AH[:, kt, col:col + 128], AL[:, kt, col:col + 128], WH[:, ti, wv], WL[:, ti, wv],
                                    kt == 0 and t % 2 == 0, kt == 7, [lo] + (ready + rel if kt == 0 else []) if k == 0 else [])
                        if kk == 1 and (t % 2 == 1 or t == len(tiles) - 1):
                            n = t % 2 + 1
                            banks.free(b, evac(bank(b)[:, 0:256 * n].rearrange("p (a b) -> p a b", a=n), t - n + 1, n, q, m))
                    wr.free(ti, [m])

        HT = R[:, b1base:b1base + 8192].rearrange("p (a b) -> p a b", a=8)
        HM = OTt[:, 0, 0:1024]
        JK = TMP[:, 0, 0:1024]
        ada = S["ada"]
        ar_ = Ring(2)

        def ada_unit(i):
            j, rel = ar_.take()
            d0 = pool.dma(ch(f"ab{j}"), ADB[0:2, j, :], A["k_brow"][:, 512 * i:512 * i + 512], rel)
            b, rel = banks.take()
            for kk in range(4):
                s, dd = weights.next(False)
                for k in range(2):
                    m = mm(bank(b)[0:2, :], CS[:, 2 * kk + k, :], W32[:, s, 512 * k:512 * k + 512],
                           kk + k == 0, kk + k == 4, [dd, csd] + rel)
                w32.free(s, [m])
            y = tt(ADB[0:2, j, :], bank(b)[0:2, :], ADB[0:2, j, :], ALU.add, [m, d0])
            banks.free(b, [y])
            d = pool.dma(ch(f"as{j}"), ada[:, 512 * i:512 * i + 512], ADB[0:2, j, :], [y])
            ar_.free(j, [d])
            ada_done[j] = d
        ada_done = {}

        def layer_norm(l, tiles):
            ready = []
            for q0, n in ((0, 4), (4, 4), (8, 1)):
                g = tiles[q0:q0 + n]
                v = stats([(x, after) for x, _, after, _ in g], RSTD[:, q0:q0 + n], 1e-6, JK)
                for i, (x, _, _, after) in enumerate(g):
                    ready.append(ts(x, x, RSTD[0:x.shape[0], q0 + i:q0 + i + 1], None, ALU.mult, after=[v] + after))
            lo, m = fill_a([(x, c) for x, c, _, _ in tiles], ready, lambda k: COLS[:, 8 * l + k:8 * l + k + 1])
            for r in (pring, ptring, oring, tring):
                for i in range(r.n):
                    r.rel[i] = [m]
            gring.rel[0] = gring.rel[1] = [m]
            return [lo]

        def layer(l, ready):
            banks_few()
            for _ in ff_phase(l, ready):
                pass
            lastg = attention_phase(l, ready)
            banks_all()
            free = pring.rel[0] + pring.rel[1] + pring.rel[2] + pring.rel[3] + ptring.rel[0] + ptring.rel[1]
            x_rows = A["x"][0] if l == 0 else hs[NM:L, :]
            loads = []
            for t in range(8):
                loads.append(pool.dma(ch(f"h{t}"), HT[:, t, :], x_rows[128 * t:128 * t + 128, :], free))
            if l == 0:
                loads.append(pool.dma(ch("h8"), HM[0:NM, :], A["meta_tokens"], oring.rel[0]))
            done = {}

            def evac(b, t, n, q, last):
                c = slice(256 * q, 256 * q + 256)
                if t < 8:
                    y = tt(HT[:, t:t + 2, c], HT[:, t:t + 2, c], b, ALU.add, [last] + loads[t:t + 2])
                else:
                    y = tt(HM[0:NM, c], HM[0:NM, c], b[0:NM, 0, :], ALU.add, [last, loads[8]])
                if q == 3:
                    for i in range(t, t + n):
                        done[i] = y
                return [y]
            cols = [NM + 128 * t for t in range(8)] + ([0] if l == 0 else [])
            out_proj(cols, evac, lastg)
            for i in range(4 * l + 4, 4 * l + 8):
                ada_unit(i)
            return done

        loads = [pool.dma(ch(f"h{t}"), HT[:, t, :], A["x"][0][128 * t:128 * t + 128, :]) for t in range(8)]
        loads.append(pool.dma(ch("h8"), HM[0:NM, :], A["meta_tokens"]))
        banks_all()
        for i in range(4):
            ada_unit(i)
        tiles = [(HT[:, t, :], NM + 128 * t, [loads[t]], []) for t in range(8)] + [(HM[0:NM, :], 0, [loads[8]], [])]
        done = layer(0, layer_norm(0, tiles))
        stores = [pool.dma(ch(f"s{t}"), hs[NM + 128 * t:NM + 128 * t + 128, :], HT[:, t, :], [done[t]]) for t in range(8)]
        tiles = [(HT[:, t, :], NM + 128 * t, [done[t]], [stores[t]]) for t in range(8)] + [(HM[0:NM, :], 0, [done[8]], [])]
        done = layer(1, layer_norm(1, tiles))

        xs = S["xs"]

        def phase(n=0):
            barrier()
            at[0] = persist + n

        def r3(a, b):
            return carve(a * b).rearrange("p (a b) -> p a b", a=a)

        CH2 = [(0, 512), (512, 512)]

        banks_all()
        G1 = SM[:, 30:54].rearrange("p (a k) -> p a k", a=3)
        B1 = COLS[:, 32:56].rearrange("p (a k) -> p a k", a=3)
        LG = SM[:, 54:62]

        def ada_phase():
            phase()
            AD = r3(32, 2)
            K2 = carve(24)
            RW_ = r3(8, 512)
            GQ = carve(16).rearrange("p (a k) -> p a k", a=2)
            d2 = pool.dma(ch("a1"), K2, A["k_cols2"])
            d3 = pool.dma(ch("a2"), GQ, A["k_gpre"].rearrange("p (a k) -> p a k", a=2))
            ad = list(ada_done.values())
            d = [pool.dma(ch("a3"), RW_[0:2, 0:4, :], ada[:, 0:2048].rearrange("c (a b) -> c a b", a=4), ad),
                 pool.dma(ch("a4"), RW_[0:2, 4:8, :], ada[:, 3072:5120].rearrange("c (a b) -> c a b", a=4), ad)]
            z, a, u = K2[:, 0:8], K2[:, 8:16], K2[:, 16:24]
            zz = LG
            x = ts(a, z, -1.0, None, ALU.mult, after=[d2])
            x = tt(a, a, z, ALU.max, [x])
            x = ac(a, a, ACT.Exp, [x], scale=-1.0)
            x3_ = ts(u, a, 1.0, None, ALU.add, after=[x])
            x4 = ts(zz, z, 0.0, None, ALU.min)
            x5 = stt(a, u, -1.0, a, ALU.add, ALU.subtract, [x3_])
            x6 = tt(zz, zz, a, ALU.add, [x4, x5])
            x7 = ac(u, u, ACT.Ln, [x3_, x5])
            tt(zz, zz, u, ALU.subtract, [x6, x7])
            b2, rel2 = banks.take()
            for i in range(8):
                for k in range(4):
                    m = tr(bank(b2)[:, 8 * i + 2 * k:8 * i + 2 * k + 2], RW_[0:2, i, 128 * k:128 * k + 128], d + rel2)
            x = cp(AD, bank(b2)[:, 0:64].rearrange("p (k c) -> p k c", k=32), [m])
            banks.free(b2, [x])
            for i, (sc_, cc, gg) in enumerate(((8, 0, 0), (8, 1, 0), (24, 0, 1))):
                y = stt(G1[:, i, :], AD[:, sc_:sc_ + 8, cc], 1.0, GQ[:, gg, :], ALU.add, ALU.mult, [x, d3])
                y = cp(B1[:, i, :], AD[:, sc_ - 8:sc_, cc], [x])

        def rstd_of(col, rows, scale, eps, after):
            v = ts(col, col, scale, eps, ALU.mult, ALU.add, after=after)
            v = ac(col, col, ACT.Ln, [v])
            return ac(col, col, ACT.Exp, [v], scale=-0.5)

        def gate_rows(dst, tmp, i, c, after=()):
            d = [pool.dma(ch("ga"), dst, ada[0:1, 1024 * c:1024 * c + 1024].broadcast_to([128, 1024]), list(after)),
                 pool.dma(ch("gb"), tmp, A["k_gpost"][:, 1024 * i:1024 * i + 1024], list(after))]
            return tt(dst, dst, tmp, ALU.mult, d)

        def prep_x(keep):
            phase(keep)
            X = r3(8, 1024)
            FG = carve(1024)
            J = carve(1024)
            TB = r3(2, 512)
            d0 = pool.dma(ch("b0"), FG, A["k_fg"])
            jr = []
            ready = {}
            for t in range(8):
                x = X[:, t, :]
                r1, r2 = RSTD[:, t:t + 1], RSTD[:, 8 + t:9 + t]
                d = pool.dma(ch(f"h{t % 4}"), x, hs[NM + 128 * t:NM + 128 * t + 128, :], xr[t - 4:t - 3] if t > 3 else [])
                q = ac(J, x, ACT.Square, [d] + jr, accum=r1)
                jr = [q]
                v = rstd_of(r1, 128, 1.0 / D, 1e-6, [q])
                y = stt(x, x, r1, FG, ALU.mult, ALU.mult, [v, d0])
                st_ = pool.dma(ch(f"s{t % 4}"), xs[128 * t:128 * t + 128, :], x, [y])
                xr.append(y)
                pend.append(st_)
                q = ac(J, x, ACT.Square, [y] + jr, accum=r2)
                jr = [q]
                v = rstd_of(r2, 128, 1.0 / D, 1e-6, [q])
                ready[t] = ts(x, x, r2, None, ALU.mult, after=[v, st_])
            return fill_a([(X[:, t, :], 128 * t) for t in range(8)], ready, lambda k: G1[:, 0, k:k + 1], lambda k: B1[:, 0, k:k + 1], TB)[0]
        xr = []

        FM = [0]

        def ctx_phase():
            phase()
            SC = r3(4, 256)
            XI = carve(1024).rearrange("p (h d c) -> p h d c", h=4, d=2)
            DM = r3(4, 128)
            ZE = r3(8, 4)
            FM[0] = at[0] - persist
            X = r3(2, 1024)
            J = carve(1024)
            TB = r3(2, 512)
            KC, VC = r3(2, 512), r3(2, 512)
            TT = carve(256)
            CT = carve(8 + 4 * 128 + 256)
            E1, E2 = carve(128), carve(128)
            d0 = pool.dma(ch("b1"), CT, A["k_dec"])
            jr = []
            ready = {}
            for t in range(2):
                x, r1 = X[:, t, :], RSTD[:, t:t + 1]
                d = pool.dma(ch(f"h{t}"), x, A["ctx_2"][0][128 * t:128 * t + 128, :])
                q = ac(J, x, ACT.Square, [d] + jr, accum=r1)
                jr = [q]
                v = rstd_of(r1, 128, 1.0 / D, 1e-6, [q])
                ready[t] = ts(x, x, r1, None, ALU.mult, after=[v])
            lo, _ = fill_a([(X[:, t, :], 128 * t) for t in range(2)], ready, lambda k: G1[:, 1, k:k + 1], lambda k: B1[:, 1, k:k + 1], TB)
            x = None
            for dr in range(2):
                for h in range(4):
                    lg = LG[:, 4 * dr + h:4 * dr + h + 1]
                    x = ac(ZE[:, 4 * dr + h, :], CT[:, 4 * dr:4 * dr + 4], ACT.Exp, [d0], scale=lg)
                    x = ac(XI[:, h, dr, :], CT[:, 8 + 128 * dr:136 + 128 * dr], ACT.Exp, [], scale=lg)
            y = None
            for h in range(4):
                x = ac(E1, CT[:, 264:392], ACT.Exp, [y] if y else [], scale=LG[:, h:h + 1])
                x2_ = ac(E2, CT[:, 392:520], ACT.Exp, [], scale=LG[:, 4 + h:5 + h])
                y = tt(DM[:, h, :], E1, CT[:, 520:648], ALU.mult, [x])
                y2_ = tt(E2, E2, CT[:, 648:776], ALU.mult, [x2_])
                y = tt(DM[:, h, :], DM[:, h, :], E2, ALU.add, [y, y2_])

            def evac(b, t, n, q, last):
                c = 256 * (q % 2)
                if q < 2:
                    z = ac(KC[:, :, c:c + 256], b, ACT.Copy, [last], scale=float(128 ** -0.5))
                else:
                    z = ac(VC[:, :, c:c + 256], b, ACT.Copy, [last])
                fin.append(z)
                return [z]
            fin = []
            out_proj([0, 128], evac, [lo])
            tr_ = Ring(1)
            for h in range(4):
                b, rel = banks.take()
                for t in range(2):
                    _, trel = tr_.take()
                    y1_ = ts(TT[:, 0:128], VC[:, t, 128 * h:128 * h + 128], ZE[:, h, t:t + 1], None, ALU.mult, after=[fin[-1], x] + trel)
                    y2_ = ts(TT[:, 128:256], VC[:, t, 128 * h:128 * h + 128], ZE[:, 4 + h, t:t + 1], None, ALU.mult)
                    m = mm(bank(b)[:, 0:256], KC[:, t, 128 * h:128 * h + 128], TT[:, 0:256], t == 0, t == 1, [y2_] + rel)
                    tr_.free(0, [m])
                y = cp(SC[:, h, :], bank(b)[:, 0:256], [m])
                banks.free(b, [y])
            return SC, XI, DM, ZE

        def mixer(SC, XI, DM, ZE, ready):
            phase(FM[0])
            CO, SI = carve(1024), carve(1024)
            QH, KH, GH_, OH = carve(1024), carve(1024), carve(1024), carve(1024)
            T1, T2 = r3(2, 512), r3(2, 512)
            VM, KM = r3(8, 128), r3(8, 128)
            VZ = r3(8, 256)
            PV = r3(8, 256)
            QX = r3(2, 1024)
            SS = r3(8, 128)
            dt = [pool.dma(ch("b2"), CO, A["k_cos2"]), pool.dma(ch("b2"), SI, A["k_sin2"])]
            w = A["w_in_2"][0]
            tr_ = Ring(2)
            prev = {"q": [], "k": [], "v": [], "g": [], "o": []}

            def go(gen):
                for _ in gen:
                    pass

            def gemm2(evac):
                go(gemm_f(CH2, evac, ready))

            for h in range(4):
                done = {"q": [], "k": [], "v": [], "g": []}
                for kind, dst, sc_ in (("q", QH, 1.0), ("k", KH, float(128 ** -0.5))):
                    def evac(o, c, n, m):
                        ti, trel = tr_.take()
                        x = ac(T1[:, ti, :], o, ACT.Copy, [m] + trel, scale=sc_)
                        y1 = tt(dst[:, c:c + n], T1[:, ti, :], CO[:, c:c + n], ALU.mult, [x] + dt + prev[kind])
                        y2 = tt(T2[0:64, ti, :], T1[64:128, ti, :], SI[64:128, c:c + n], ALU.mult)
                        y3 = tt(T2[64:128, ti, :], T1[0:64, ti, :], SI[0:64, c:c + n], ALU.mult)
                        y4 = tt(dst[:, c:c + n], dst[:, c:c + n], T2[:, ti, :], ALU.add, [y3])
                        tr_.free(ti, [y4])
                        done[kind].append(y4)
                        return [x]
                    gemm2(evac)

                def evac(o, c, n, m):
                    ti, trel = tr_.take()
                    x = ac(T1[:, ti, :], o, ACT.Copy, [m] + trel)
                    b, rel = banks.take()
                    for i in range(4):
                        m = tr(bank(b)[:, 128 * i:128 * i + 128], T1[:, ti, 128 * i:128 * i + 128], [x] + rel)
                    tr_.free(ti, [m])
                    y = cp(VM[:, c // 128:c // 128 + 4, :], bank(b).rearrange("p (a b) -> p a b", a=4), [m] + prev["v"])
                    banks.free(b, [y])
                    done["v"].append(y)
                    return [x]
                gemm2(evac)

                def evac(o, c, n, m):
                    x = ac(GH_[:, c:c + n], o, ACT.Tanh, [m] + prev["g"], scale=0.5)
                    y = stt(GH_[:, c:c + n], GH_[:, c:c + n], 1.0, o, ALU.add, ALU.mult, [x])
                    done["g"].append(y)
                    return [y]
                gemm2(evac)
                for half in range(2):
                    b, rel = banks.take()
                    for i in range(4):
                        c = 512 * half + 128 * i
                        m = tr(bank(b)[:, 128 * i:128 * i + 128], KH[:, c:c + 128], done["k"] + rel)
                    y = cp(KM[:, 4 * half:4 * half + 4, :], bank(b).rearrange("p (a b) -> p a b", a=4), [m] + prev["k"])
                    banks.free(b, [y])
                z1 = ts(VZ[:, :, 0:128], VM, ZE[:, h, 2:3], None, ALU.mult, after=done["v"] + prev["k"])
                z2 = ts(VZ[:, :, 128:256], VM, ZE[:, 4 + h, 2:3], None, ALU.mult)
                kb = []
                for n in range(4):
                    b, rel = banks.take()
                    for i in range(2):
                        m = mm(bank(b)[:, 256 * i:256 * i + 256], KM[:, 2 * n + i, :], VZ[:, 2 * n + i, :], True, True, [z2, y] + rel)
                    kb.append((b, m))
                m_kv = m
                u = cp(PV[:, 0, 0:128], SC[:, h, 0:128], prev["o"])
                v = cp(PV[:, 7, 128:256], SC[:, h, 128:256], prev["o"])
                for n in range(7):
                    b, m = kb[n // 2]
                    u = stt(PV[:, n + 1, 0:128], PV[:, n, 0:128], ZE[:, h, 3:4], bank(b)[:, 256 * (n % 2):256 * (n % 2) + 128],
                            ALU.mult, ALU.add, [u, m])
                    n2 = 7 - n
                    b, m = kb[n2 // 2]
                    v = stt(PV[:, n2 - 1, 128:256], PV[:, n2, 128:256], ZE[:, 4 + h, 3:4],
                            bank(b)[:, 256 * (n2 % 2) + 128:256 * (n2 % 2) + 256], ALU.mult, ALU.add, [v, m])
                for b, m in kb:
                    banks.free(b, [u, v])
                for dr in range(2):
                    qx = tt(QX[:, dr, :].rearrange("p (a b) -> p a b", a=8), QH.rearrange("p (a b) -> p a b", a=8),
                            XI[:, h, dr, :].unsqueeze(1).broadcast_to([128, 8, 128]), ALU.mult, done["q"] + prev["o"])
                sd = []
                for half in range(2):
                    b, rel = banks.take()
                    for i in range(4):
                        c = 512 * half + 128 * i
                        m = mm(bank(b)[:, 128 * i:128 * i + 128], KH[:, c:c + 128], QH[:, c:c + 128], True, True, done["q"] + rel)
                    y = tt(SS[:, 4 * half:4 * half + 4, :], bank(b).rearrange("p (a b) -> p a b", a=4),
                           DM[:, h, :].unsqueeze(1).broadcast_to([128, 4, 128]), ALU.mult, [m] + prev["o"])
                    banks.free(b, [y])
                    sd.append(y)
                prev["q"] = [m, qx]
                for half in range(2):
                    b, rel = banks.take()
                    for i in range(4):
                        n = 4 * half + i
                        o = bank(b)[:, 128 * i:128 * i + 128]
                        mm(o, VM[:, n, :], SS[:, n, :], True, False, [sd[half], u, v, qx] + rel)
                        mm(o, PV[:, n, 0:128], QX[:, 0, 128 * n:128 * n + 128], False, False)
                        m = mm(o, PV[:, n, 128:256], QX[:, 1, 128 * n:128 * n + 128], False, True)
                    c = 512 * half
                    oh = OH[:, c:c + 512]
                    y = cp(oh, bank(b), [m] + prev["g"] + oh_rel)
                    ti, trel = tr_.take()
                    q = ac(T1[:, ti, :], bank(b), ACT.Square, [y] + trel)
                    banks.free(b, [q])
                    b, rel = banks.take()
                    m2 = mm(bank(b), ones, T1[:, ti, :], True, True, [q] + rel)
                    v_ = ts(T2[:, ti, :], bank(b), 1.0 / 128, 1e-6, ALU.mult, ALU.add, after=[m2])
                    banks.free(b, [v_])
                    v_ = ac(T2[:, ti, :], T2[:, ti, :], ACT.Ln, [v_])
                    v_ = ac(T2[:, ti, :], T2[:, ti, :], ACT.Exp, [v_], scale=-0.5)
                    v_ = stt(oh, oh, 0.5, T2[:, ti, :], ALU.mult, ALU.mult, [v_])
                    tr_.free(ti, [v_])
                    v_ = tt(oh, oh, GH_[:, c:c + 512], ALU.mult, [v_] + done["g"])
                prev["o"], prev["v"] = [m], [m, z2]
                prev["k"] = [m_kv]
                prev["g"] = [v_]
                dd = pool.dma(ch("os2"), os_[h][:, 0:SEQ], OH, [v_])
                oh_rel[:] = [dd]
                pend.append(dd)
        oh_rel = []

        def fourier(ready):
            phase(FM[0])
            FTt = r3(4, 1024)
            CD = carve(256)
            OB = r3(2, 512)
            Y = r3(2, 512)
            d0 = pool.dma(ch("b3"), CD, A["k_cd"])
            w = A["w_in_2"][0]
            fin = []
            for g in range(4):
                def evac(o, c, n, m):
                    x = ac(FTt[:, g, c:c + n], o, ACT.Copy, [m])
                    fin.append(x)
                    return [x]
                for _ in gemm_f(CH2, evac, ready):
                    pass
            alldone = pe.items[-1]
            AHf = AH[:, :, :].rearrange("p a b -> p (a b)")[:, 0:8192].rearrange("p (m g c) -> p m g c", m=8, g=4)
            ALf = AL[:, :, :].rearrange("p a b -> p (a b)")[:, 0:8192].rearrange("p (m g c) -> p m g c", m=8, g=4)
            for g in range(4):
                for mt in range(0, 8, 2):
                    b, rel = banks.take()
                    for i in range(2):
                        c = 128 * (mt + i)
                        m = mm(bank(b)[:, 256 * i:256 * i + 256], FTt[:, g, c:c + 128], CD, True, True, [d0, fin[2 * g + 1]] + rel)
                    src = bank(b).rearrange("p (a b) -> p a b", a=2)
                    h = ac(AHf[:, mt:mt + 2, g, :], src, ACT.Copy, [m, alldone])
                    lo = tt(ALf[:, mt:mt + 2, g, :], src, f(AHf[:, mt:mt + 2, g, :]), ALU.subtract, [h])
                    banks.free(b, [lo])
            bs = [banks.take() for _ in range(8)]
            for j in range(16):
                mt, cs = j // 2, j % 2
                t, wl_ = weights.next()
                for g in range(4):
                    yh = AHf[:, mt, g, 128 * cs:128 * cs + 128]
                    yl = ALf[:, mt, g, 128 * cs:128 * cs + 128]
                    for half in range(2):
                        b, rel = bs[2 * g + half]
                        wv = slice(512 * half, 512 * half + 512)
                        m = mm3(bank(b), yh, yl, WH[:, t, wv], WL[:, t, wv], j == 0, j == 15, [lo, wl_] + rel)
                wr.free(t, [m])
            orr = Ring(2)
            for g in range(4):
                for half in range(2):
                    b, _ = bs[2 * g + half]
                    i, rel = orr.take()
                    y = (ac if half else cp)(OB[:, i, :], bank(b), after=[m] + rel)
                    banks.free(b, [y])
                    dd = pool.dma(ch(f"g{i}"), os_[4 + g][:, 512 * half:512 * half + 512], OB[:, i, :], [y])
                    orr.free(i, [dd])
                    pend.append(dd)

        def mix_out():
            phase()
            MX = r3(8, 1024)
            OL = r3(2, 1024)
            GA = carve(1024)
            XL = r3(2, 1024)
            J = carve(1024)
            TB = r3(2, 512)
            S2 = carve(16)
            orr = Ring(2)
            for g in range(8):
                i, rel = orr.take()
                d = pool.dma(ch(f"o{i}"), OL[:, i, :], os_[g][:, 0:SEQ], rel)
                h = ac(AH[:, g, 0:SEQ], OL[:, i, :], ACT.Copy, [d])
                rd = tt(AL[:, g, 0:SEQ], OL[:, i, :], f(AH[:, g, 0:SEQ]), ALU.subtract, [h])
                orr.free(i, [rd])
            dg = gate_rows(GA, J, 0, 2)

            def evac(b, t, n, q, last):
                y = (ac if t % 4 else cp)(MX[:, t:t + n, 256 * q:256 * q + 256], b, after=[last])
                fin[t] = fin[t + 1] = fin.get(t, []) + [y]
                return [y]
            fin = {}
            out_proj([128 * t for t in range(8)], evac, [rd])
            ready = {}
            jr = []
            xrr = Ring(2)
            for t in range(8):
                x, r1, r2 = MX[:, t, :], RSTD[:, t:t + 1], RSTD[:, 8 + t:9 + t]
                q = ac(J, x, ACT.Square, fin[t] + jr + [dg], accum=r1)
                v = rstd_of(r1, 128, 1.0 / D, 1e-6, [q])
                y = stt(x, x, r1, GA, ALU.mult, ALU.mult, [v, dg])
                i, rel = xrr.take()
                d = pool.dma(ch(f"r{i}"), XL[:, i, :], xs[128 * t:128 * t + 128, :], rel)
                y = tt(x, x, XL[:, i, :], ALU.add, [y, d])
                xrr.free(i, [y])
                st_ = pool.dma(ch(f"s{t % 4}"), xs[128 * t:128 * t + 128, :], x, [y])
                pend.append(st_)
                q = ac(J, x, ACT.Square, [y, q], accum=r2)
                jr = [q]
                v = rstd_of(r2, 128, 1.0 / D, 1e-6, [q])
                ready[t] = ts(x, x, r2, None, ALU.mult, after=[v, st_])
            return fill_a([(MX[:, t, :], 128 * t) for t in range(8)], ready, lambda k: G1[:, 2, k:k + 1], lambda k: B1[:, 2, k:k + 1], TB)[0]

        def ffn(ready):
            phase()
            CW = carve(4 * 44).rearrange("p (a b) -> p a b", a=4)
            NR = 17
            CV = r3(2, 1024)
            CU = r3(2, 1024)
            TH = r3(2, 1024)
            G = r3(NR, 1024)
            gsp = S["gsp"]
            d0 = pool.dma(ch("b5"), CW, A["k_conv"].rearrange("p (a b) -> p a b", a=4))
            w = A["w_up_2"][0]
            cvr, thr = Ring(2), Ring(2)

            def conv(o, dst, c, j, after):
                x = ac(dst[:, c:c + 512], o, ACT.Identity, after + [d0], scale=CW[:, 1, j:j + 1], bias=CW[:, 3, j:j + 1])
                d3 = dst[:, c:c + 512].rearrange("p (r t) -> p r t", t=64)
                o3 = o.rearrange("p (r t) -> p r t", t=64)
                y = stt(d3[:, :, 1:64], o3[:, :, 0:63], CW[:, 0, j:j + 1], d3[:, :, 1:64], ALU.mult, ALU.add, [x])
                return stt(d3[:, :, 0:63], o3[:, :, 1:64], CW[:, 2, j:j + 1], d3[:, :, 0:63], ALU.mult, ALU.add, [y])
            gdone = []
            for j in range(FT):
                ci, crel = cvr.take()
                ti, trel = thr.take()
                va, vb, th = CV[:, ci, :], CU[:, ci, :], TH[:, ti, :]
                ya, yb = [], []

                def evac(o, c, n, m):
                    y = conv(o, va, c, j, [m] + crel)
                    ya.append(y)
                    return [y]
                for _ in gemm_f(CH2, evac, ready):
                    pass
                t_ = ac(th, va, ACT.Tanh, ya + trel, scale=0.5)

                def evac(o, c, n, m):
                    y = conv(o, vb, c, FT + j, [m] + crel)
                    yb.append(y)
                    return [y]
                for _ in gemm_f(CH2, evac, ready):
                    pass
                a1 = stt(va, th, 1.0, va, ALU.add, ALU.mult, [t_])
                thr.free(ti, [a1])
                if j < NR:
                    a2 = stt(G[:, j, :], va, 0.5, vb, ALU.mult, ALU.mult, [a1, yb[-1]])
                    cvr.free(ci, [a2])
                else:
                    a2 = stt(va, va, 0.5, vb, ALU.mult, ALU.mult, [a1, yb[-1]])
                    a2 = pool.dma(ch(f"s{ci}"), gsp[j - NR], va, [a2])
                    cvr.free(ci, [a2])
                    pend.append(a2)
                gdone.append(a2)
            barrier()
            GL_ = CU
            wd = A["w_down_2"][0]
            glr, ar = Ring(2), Ring(8)
            F = {}
            fdone = {}
            for half in range(2):
                bs = [banks.take() for _ in range(8)]
                wt = None
                for k in range(FT):
                    if k % 2 == 0:
                        wt, wlo = weights.next()
                    ai, arel = ar.take()
                    if k < NR:
                        src, dep = G[:, k, :], []
                    else:
                        gi_, grel = glr.take()
                        d = pool.dma(ch(f"g{gi_}"), GL_[:, gi_, :], gsp[k - NR], grel)
                        src, dep = GL_[:, gi_, :], [d]
                    h = ac(AH[:, ai, 0:SEQ], src, ACT.Copy, dep + arel)
                    lo = tt(AL[:, ai, 0:SEQ], src, f(AH[:, ai, 0:SEQ]), ALU.subtract, [h])
                    if k >= NR:
                        glr.free(gi_, [lo])
                    wv = slice(512 * (k % 2), 512 * (k % 2) + 512)
                    for t in range(8):
                        b, rel = bs[t]
                        m = mm3(bank(b), AH[:, ai, 128 * t:128 * t + 128], AL[:, ai, 128 * t:128 * t + 128],
                                WH[:, wt, wv], WL[:, wt, wv], k == 0, k == FT - 1, [lo, wlo] + (rel if k == 0 else []))
                        if k == FT - 1:
                            if half == 0:
                                dst = (CV if t < 4 else TH)[:, (t // 2) % 2, 512 * (t % 2):512 * (t % 2) + 512]
                            else:
                                dst = G[:, t, 0:512]
                            F[(t, half)] = dst
                            y = (ac if t % 2 else cp)(dst, bank(b), after=[m])
                            fdone[(t, half)] = y
                            banks.free(b, [y])
                    ar.free(ai, [m])
                    if k % 2 == 1:
                        wr.free(wt, [m])
            GA, XL, J = G[:, 8, :], G[:, 9:11, :], G[:, 11, :]
            last_mm = m
            dg = gate_rows(GA, J, 1, 5, [lo])
            xrr = Ring(2)
            jr = []
            for t in range(8):
                r = RSTD[:, t:t + 1]
                r2 = RSTD[:, 8 + t:9 + t]
                q1 = ac(J[:, 0:512], F[(t, 0)], ACT.Square, [lo, fdone[(t, 0)], dg] + jr, accum=r)
                q = ac(J[:, 512:1024], F[(t, 1)], ACT.Square, [fdone[(t, 1)]], accum=r2)
                jr = [q]
                v = tt(r, r, r2, ALU.add, [q])
                v = rstd_of(r, 128, 1.0 / D, 1e-6, [v])
                i, rel = xrr.take()
                d = pool.dma(ch(f"r{i}"), XL[:, i, :], xs[128 * t:128 * t + 128, :], rel + [lo])
                for half in range(2):
                    hv = slice(512 * half, 512 * half + 512)
                    y = stt(F[(t, half)], F[(t, half)], r, GA[:, hv], ALU.mult, ALU.mult, [v, dg])
                    y = tt(XL[:, i, hv], XL[:, i, hv], F[(t, half)], ALU.add, [y, d])
                st_ = pool.dma(ch(f"s{i}"), O["out"][0][128 * t:128 * t + 128, :], XL[:, i, :], [y])
                xrr.free(i, [st_])

        for t in range(8):
            pend.append(pool.dma(ch(f"s{t}"), hs[NM + 128 * t:NM + 128 * t + 128, :], HT[:, t, :], [done[t]]))
        if stage >= 3:
            ada_phase()
            tabs = ctx_phase()
            lo = prep_x(FM[0])
            mixer(*tabs, [lo])
            fourier([lo])
            lo = mix_out()
            ffn([lo])

        if dbg is not None:
            dbg(locals(), hs, os_, sp, ch, O)
        finish = [c for c in chans.values()]

        for q in (pe, act, dve, pool, sp):
            n = q.number()
        block = ctx.enter_context(nc.Block())

        @block.tensor
        def _(e):
            pe.emit(e)

        @block.scalar
        def _(e):
            act.emit(e)

        @block.vector
        def _(e):
            dve.emit(e)

        @block.gpsimd
        def _(e):
            pool.emit(e)

        @block.sync
        def _(e):
            sp.emit(e)
            for c in finish:
                e.wait_ge(c.sem, 16 * c.n)


def host_constants():
    f = np.float32
    c = {}
    c["k_ident"] = np.eye(128, dtype=f)
    q = np.arange(128)
    m = np.zeros((128, 2, 128), f)
    m[:, 0] = np.where((q[None, :] // 64) <= (q[:, None] // 64), 0.0, NEG)
    m[:, 1] = np.where(q[None, :] <= q[:, None], 0.0, NEG)
    c["k_mask"] = m.reshape(128, 256)
    s = np.zeros((128, 8, 128), f)
    for h in range(8):
        s[h, h] = -1.0
        s[32 + h, h] = -1.0
    c["k_sel"] = s.reshape(128, 1024)
    pos = np.arange(L, dtype=f)
    inv = (1.0 / (np.float32(500000.0) ** (np.arange(0, 16, 2, dtype=f) / np.float32(16)))).astype(f)
    ang = pos[None, :] * inv[:, None]
    cos, sin = np.ones((128, L), f), np.zeros((128, L), f)
    rot = np.zeros((128, 128), f)
    for b in (0, 64):
        cos[b:b + 8] = np.cos(ang)
        cos[b + 8:b + 16] = np.cos(ang)
        sin[b:b + 8] = -np.sin(ang)
        sin[b + 8:b + 16] = np.sin(ang)
        for i in range(8):
            rot[b + 8 + i, b + i] = 1.0
            rot[b + i, b + 8 + i] = 1.0
    c["k_cos"], c["k_sin"], c["k_rot"] = cos, sin, rot
    p = np.arange(128, dtype=f)
    dec = np.zeros((128, 776), f)
    dec[:, 0], dec[:, 1], dec[:, 2], dec[:, 3] = 255 - p, 127 - p, 127 - p, 128
    dec[:, 4], dec[:, 5], dec[:, 6], dec[:, 7] = p, 128 + p, p, 128
    dec[:, 8:136] = p[None, :] + 1
    dec[:, 136:264] = 128 - p[None, :]
    dec[:, 264:392] = np.maximum(p[None, :] - p[:, None], 0)
    dec[:, 392:520] = np.maximum(p[:, None] - p[None, :], 0)
    dec[:, 520:648] = (p[:, None] <= p[None, :])
    dec[:, 648:776] = (p[:, None] > p[None, :])
    c["k_dec"] = dec
    t = np.arange(SEQ)
    fr = (np.float32(10000.0) ** (-np.arange(32, dtype=f) / np.float32(32))).astype(f)
    ang = np.concatenate([(t // 64).astype(f)[:, None] * fr, (t % 64).astype(f)[:, None] * fr], 1).T
    c["k_cos2"] = np.concatenate([np.cos(ang), np.cos(ang)]).astype(f)
    c["k_sin2"] = np.concatenate([np.sin(ang), -np.sin(ang)]).astype(f)
    i = np.arange(128, dtype=np.int64)
    a = 2 * np.pi * ((i[:, None] * i[None, :]) % 128) / 128.0
    c["k_cd"] = (np.concatenate([np.cos(a), np.sin(a)], 1) / np.sqrt(1024.0 * 128.0)).astype(f)
    n = np.arange(SEQ, dtype=np.int64)
    a = 2 * np.pi * ((n[:, None] * n[None, :]) % SEQ) / float(SEQ)
    both = np.stack([np.cos(a), -np.sin(a)], 0).reshape(2, 8, 128, SEQ)
    c["k_dft"] = np.ascontiguousarray(both.transpose(2, 1, 0, 3).reshape(128, 16 * SEQ)).astype(f)
    return c


def layout(inputs):
    f = {k: np.asarray(v) for k, v in inputs.items()}
    a = dict(host_constants())
    for n in ("x", "meta_tokens", "w_in", "w_out"):
        a[n] = f[n]
    cols = np.zeros((128, 32), np.float32)
    for l in range(2):
        cols[:, 8 * l:8 * l + 8] = f["norm_gain"][l].reshape(8, 128).T
        cols[:, 16 + l] = f["subln_gain"][l]
        cols[0:8, 18 + l] = f["forget_bias"][l]
    a["k_cols"] = cols
    for n in ("ctx_2", "w_ada_2", "w_in_2", "w_out_2", "w_up_2", "w_down_2"):
        a[n] = f[n]

    def col(v):
        return v.reshape(-1, 128).T

    def rows(v, n=128):
        return np.repeat(v.reshape(1, -1), n, axis=0)
    a["k_c"] = np.stack([col(f["c_2"][0]), col(f["c_ctx_2"])], 2).reshape(128, 16)
    a["k_brow"] = np.repeat(f["b_ada_2"], 2, axis=0)
    a["k_gpre"] = np.concatenate([col(f["g_mix_pre_2"][0]), col(f["g_ffn_pre_2"][0])], 1)
    a["k_gpost"] = np.concatenate([rows(f["g_mix_post_2"][0]), rows(f["g_ffn_post_2"][0])], 1)
    k2 = np.zeros((128, 24), np.float32)
    k2[:, 0:4], k2[:, 4:8] = rows(f["ret_decay_fwd_2"][0]), rows(f["ret_decay_bwd_2"][0])
    a["k_cols2"] = k2
    a["k_fg"] = rows(f["final_gain"])
    cw = np.concatenate([f["conv_w_2"][0], f["conv_b_2"]], 0)
    a["k_conv"] = cw.reshape(4, 44, 128).transpose(2, 0, 1).reshape(128, 176)
    lam = np.stack([f["lambda_q1"], f["lambda_k1"], f["lambda_q2"], f["lambda_k2"]], 1).reshape(1, 512)
    a["k_lam"] = np.repeat(lam, 128, axis=0)
    return {k: np.ascontiguousarray(v) for k, v in a.items()}


SCRATCH = {"hs": (L, D), "os": (8, 128, L), "xs": (SEQ, D), "ada": (2, 6 * D), "gsp": (FT - 17, 128, SEQ)}


def kernel(**inputs):
    import concourse.bacc as _bacc
    from concourse.bass_utils import run_bass_kernel_spmd as _run

    arrays = layout(inputs)
    nc = _bacc.Bacc("TRN2", target_bir_lowering=False, num_devices=1)
    A = {n: nc.dram_tensor(f"in_{n}", a.shape, mybir.dt.from_np(a.dtype), kind="ExternalInput").ap()
         for n, a in arrays.items()}
    S = {n: nc.dram_tensor(f"s_{n}", s, F32, kind="Internal").ap() for n, s in SCRATCH.items()}
    O = {"out": nc.dram_tensor("out_0", (1, SEQ, D), F32, kind="ExternalOutput").ap()}
    build(nc, A, S, O)
    r = _run(nc, [{f"in_{n}": a for n, a in arrays.items()}], core_ids=[0])
    return r.results[0]["out_0"]
```

```python
from contextlib import ExitStack

import numpy as np
import concourse.bass as bass
from concourse import mybir

F32 = mybir.dt.float32
F32R = mybir.dt.float32r
ALU = mybir.AluOpType
ACT = mybir.ActivationFunctionType
AX = mybir.AxisListType

SEQ = 1024
NM = 16
L = SEQ + NM
D = 1024
KT = 8
NT = 8
CH = [(0, 352), (352, 344), (696, 344)]
LAM_INIT = [0.8 - 0.6 * float(np.exp(-0.3 * l)) for l in range(2)]
NEG = -1e30
DFF = 2816
FT = DFF // 128


class Ins:

    def __init__(self, q, fn, after):
        self.q, self.fn, self.after = q, fn, after
        self.sig = False
        self.val = 0

    def need(self):
        self.sig = True


class Dma:

    def __init__(self, q, fn, after, chan):
        self.q, self.fn, self.after, self.chan = q, fn, after, chan
        chan.n += 1
        self.val = 16 * chan.n

    def need(self):
        pass


class Chan:
    def __init__(self, sem):
        self.sem, self.n = sem, 0


class Queue:

    def __init__(self, sem):
        self.sem, self.items = sem, []

    def add(self, fn, after=()):
        for a in after:
            a.need()
        i = Ins(self, fn, list(after))
        self.items.append(i)
        return i

    def dma(self, chan, out, in_, after=(), **kw):
        for a in after:
            a.need()
        i = Dma(self, lambda e: e.dma_start(out, in_, **kw), list(after), chan)
        self.items.append(i)
        return i

    def number(self):
        n = 0
        for i in self.items:
            if isinstance(i, Ins) and i.sig:
                n += 1
                i.val = n
        return n

    def emit(self, eng):
        seen = {}
        for i in self.items:
            want = {}
            for a in i.after:
                s = a.chan.sem if isinstance(a, Dma) else a.q.sem
                if a.val > seen.get(id(s), 0):
                    seen[id(s)] = a.val
                    want[id(s)] = (s, a.val)
            for s, v in want.values():
                eng.wait_ge(s, v)
            if i.fn is None:
                continue
            x = i.fn(eng)
            if isinstance(i, Dma):
                x.then_inc(i.chan.sem, 16)
            elif i.sig:
                x.then_inc(self.sem, 1)


class Ring:

    def __init__(self, n, base=0):
        self.n, self.i, self.base = n, 0, base
        self.rel = [[] for _ in range(n)]
        self.busy = [False] * n

    def ready(self):
        return not self.busy[self.i]

    def take(self):
        i = self.i
        assert not self.busy[i]
        self.busy[i] = True
        self.i = (i + 1) % self.n
        return i, self.rel[i]

    def free(self, i, ins):
        self.rel[i] = list(ins)
        self.busy[i] = False


def pieces(a, b, step=512):
    out = []
    while a < b:
        e = min(b, (a // step + 1) * step)
        out.append((a, e))
        a = e
    return out


def build(nc, A, S, O):
    ctx = ExitStack()
    with ctx:
        def sb(name, shape, dt=F32):
            return ctx.enter_context(nc.sbuf_tensor(name, shape, dt))

        def sem(name):
            return ctx.enter_context(nc.semaphore(name))

        pe, act, dve, pool, sp = (Queue(sem(n)) for n in ("q_pe", "q_act", "q_dve", "q_pool", "q_sp"))
        chans = {}

        def ch(name):
            if name not in chans:
                chans[name] = Chan(sem("d_" + name))
            return chans[name]

        PS = ctx.enter_context(nc.psum_tensor("PS", [128, 8, 512], F32))
        PSf = PS[:, :, :].rearrange("p a b -> p (a b)")
        AH = sb("AH", [128, KT, L], F32R)
        AL = sb("AL", [128, KT, L], F32R)
        W32 = sb("W32", [128, 3, 1024])
        NW = 3
        WH = sb("WH", [128, NW, 1024], F32R)
        WL = sb("WL", [128, NW, 1024], F32R)
        identr = sb("identr", [128, 128], F32R)
        maskr = sb("maskr", [128, 2, 128], F32R)
        selr = sb("selr", [128, 8, 128], F32R)
        C2 = sb("C2", [128, L], F32R)
        RW = 24192
        R = sb("R", [128, RW])
        at = [0]

        def carve(n):
            v = R[:, at[0]:at[0] + n]
            at[0] += n
            assert at[0] <= RW, at[0]
            return v

        def c3(a, b):
            return carve(a * b).rearrange("p (a b) -> p a b", a=a)

        ident = carve(128)
        ones = carve(128)
        SM = carve(64)
        COLS = carve(96)
        persist = at[0]

        def mm(out, lhsT, rhs, start=True, stop=True, after=()):
            return pe.add(lambda e: e.matmul(out, lhsT, rhs, start=start, stop=stop, skip_group_check=True), after)

        def mm3(out, wh, wl, xh, xl, start, stop, after=()):
            mm(out, wh, xh, start, False, after)
            mm(out, wh, xl, False, False)
            return mm(out, wl, xh, False, stop)

        def tr(out, in_, after=()):
            k = in_.shape[0]
            return pe.add(lambda e: e.transpose(out, in_, ident[0:k, 0:k]), after)

        def ac(out, in_, func=ACT.Copy, after=(), scale=1.0, bias=None, accum=None):
            kw = {"scale": scale}
            if bias is not None:
                kw["bias"] = bias
            if accum is not None:
                kw["accum_out"] = accum
            return act.add(lambda e: e.activation(out, in_, func, **kw), after)

        def tt(out, a, b, op, after=(), q=None):
            return (q or dve).add(lambda e: e.tensor_tensor(out, a, b, op), after)

        def ts(out, a, s1, s2, op0, op1=None, after=(), q=None):
            if op1 is None:
                return (q or dve).add(lambda e: e.tensor_scalar(out, a, s1, None, op0), after)
            return (q or dve).add(lambda e: e.tensor_scalar(out, a, s1, s2, op0, op1), after)

        def stt(out, a, s, b, op0, op1, after=()):
            return dve.add(lambda e: e.scalar_tensor_tensor(out, a, s, b, op0, op1), after)

        def cp(out, a, after=(), q=None):
            return (q or dve).add(lambda e: e.tensor_copy(out, a), after)

        def rmax_neg(out, a, after=()):
            return dve.add(lambda e: e.tensor_reduce(out, a, AX.X, ALU.max, negate=True), after)

        def recip(out, a, after=()):
            return dve.add(lambda e: e.reciprocal(out, a), after)

        def f(x):
            return x.bitcast(F32)

        def barrier(qs=None):
            last = []
            for q in (pe, act, dve, pool):
                real = [i for i in q.items[-200:] if i.fn is not None and isinstance(i, Ins)]
                last += real[-1:]
            for q in qs or (pe, act, dve, pool):
                q.add(None, [x for x in last if x.q is not q] + pend)
            del pend[:]
        pend = []

        banks = Ring(3, 5)
        sA, sB = Ring(1), Ring(1)
        w32 = Ring(3)
        wr = Ring(NW)

        def banks_set(n, base):
            assert not any(banks.busy)
            rel = sum(banks.rel, []) + sA.rel[0] + sB.rel[0]
            banks.n, banks.base, banks.i = n, base, 0
            banks.rel = [list(rel) for _ in range(n)]
            banks.busy = [False] * n
            sA.rel[0] = list(rel)
            sB.rel[0] = list(rel)

        def banks_all():
            banks_set(8, 0)

        def banks_few():
            banks_set(3, 5)

        def bank(i):
            return PS[:, banks.base + i, :]

        dve.add(lambda e: e.memset(ones, 1.0))
        cm = w32.take()[0]
        c0 = [sp.dma(ch("c0"), ident, A["k_ident"]),
              sp.dma(ch("c0"), W32[:, cm, 0:256], A["k_mask"]),
              sp.dma(ch("c0"), COLS[:, 0:32], A["k_cols"])]
        cn = w32.take()[0]
        c0.append(sp.dma(ch("c0"), W32[:, cn, :], A["k_sel"]))
        x1 = ac(identr[:, :], ident, after=c0)
        x2 = ac(maskr[:, :, :].rearrange("p a b -> p (a b)"), W32[:, cm, 0:256])
        x3 = ac(selr[:, :, :].rearrange("p a b -> p (a b)"), W32[:, cn, :])
        w32.free(cm, [x3])
        w32.free(cn, [x3])
        cz = dve.add(lambda e: e.memset(f(C2[:, :]), 0.0))
        consts = [x3, cz]

        def wslice(w, c, n=128):
            return w[:, c:c + n].rearrange("(k p) n -> p k n", p=128)

        class Weights:
            AHEAD = 1

            def __init__(self, plan):
                self.plan = list(plan)
                self.loaded, self.split, self.used = 0, 0, 0
                self.dmas, self.parts = {}, {}

            def load(self):
                while self.loaded < len(self.plan) and w32.ready():
                    src, _ = self.plan[self.loaded]
                    s, rel = w32.take()
                    d = sp.dma(ch(f"w{s}"), W32[:, s, :].rearrange("p (a b) -> p a b", a=src.shape[1]), src, rel)
                    self.dmas[self.loaded] = (s, d)
                    self.loaded += 1

            def prepare(self, upto):
                self.load()
                while self.split <= min(upto, len(self.plan) - 1):
                    i = self.split
                    if not self.plan[i][1]:
                        if i >= self.used:
                            return
                        self.split += 1
                        continue
                    if i not in self.dmas or not wr.ready():
                        return
                    s, d = self.dmas[i]
                    t, rel = wr.take()
                    h = ac(WH[:, t, :], W32[:, s, :], after=[d] + rel)
                    lo = tt(WL[:, t, :], W32[:, s, :], f(WH[:, t, :]), ALU.subtract, [h])
                    w32.free(s, [lo])
                    self.parts[i] = (t, lo)
                    self.split += 1
                    self.load()

            def next(self, split=True):
                i = self.used
                assert self.plan[i][1] == split
                if split:
                    self.prepare(i + self.AHEAD)
                    self.used += 1
                    return self.parts[i]
                self.load()
                self.used += 1
                return self.dmas[i]

        def out_srcs(w):
            for q in range(4):
                for kk in range(2):
                    yield (w[512 * kk:512 * kk + 512, 256 * q:256 * q + 256].rearrange("(k p) n -> p k n", p=128), True)

        C0 = {"q": (0, 2048), "k": (512, 2560), "v": (1024, 3072), "g": (1536, 3592)}

        def wcol(kind, g):
            return C0[kind][g // 4] + 128 * (g % 4)

        def ada_srcs(i0):
            for i in range(i0, i0 + 4):
                for kk in range(4):
                    yield (A["w_ada_2"][0][256 * kk:256 * kk + 256, 512 * i:512 * i + 512]
                           .rearrange("(k p) n -> p k n", p=128), False)

        def weight_plan():
            yield from ada_srcs(0)
            for l in range(2):
                yield (wslice(A["w_in"][l], 3584), True)
                for g in range(8):
                    for kind in "qkvg":
                        yield (wslice(A["w_in"][l], wcol(kind, g)), True)
                yield from out_srcs(A["w_out"][l])
                yield from ada_srcs(4 * l + 4)
            w = A["w_in_2"][0]
            yield from out_srcs(w[:, 512:1536])
            for h in range(4):
                for kind in range(4):
                    yield (wslice(w, 512 * kind + 128 * h), True)
            for g in range(4):
                yield (wslice(w, 2048 + 128 * g), True)
            for j in range(16):
                yield (A["k_dft"][:, 1024 * j:1024 * j + 1024].rearrange("p (a b) -> p a b", a=1), True)
            yield from out_srcs(A["w_out_2"][0])
            w = A["w_up_2"][0]
            for j in range(FT):
                yield (wslice(w, 128 * j), True)
                yield (wslice(w, DFF + 128 * j), True)
            wd = A["w_down_2"][0]
            for half in range(2):
                for k in range(0, FT, 2):
                    yield (wd[128 * k:128 * k + 256, 512 * half:512 * half + 512].rearrange("(k p) n -> p k n", p=128), True)

        weights = Weights(weight_plan())

        def gemm_f(nch, evac, ready):
            t, lo = weights.next()
            wh = WH[:, t, :].rearrange("p (k m) -> p k m", k=KT)
            wl = WL[:, t, :].rearrange("p (k m) -> p k m", k=KT)
            for c, n in nch:
                while not banks.ready():
                    yield
                b, rel = banks.take()
                o = bank(b)[:, 0:n]
                for k in range(KT):
                    m = mm3(o, wh[:, k, :], wl[:, k, :], AH[:, k, c:c + n], AL[:, k, c:c + n],
                            k == 0, k == KT - 1, [lo] + ready + rel if k == 0 else [])
                last = m
                r = evac(o, c, n, m)
                banks.free(b, r)
                if c == nch[-1][0]:
                    wr.free(t, [last])
                yield 24 * n / 2360.0

        cosT = carve(L)
        sinT = carve(L)
        rotm = carve(128)
        V = carve(2 * 9 * 128).rearrange("p (s t n) -> p s t n", s=2, t=9)
        QT = c3(2, L)
        KTt = c3(2, L)
        GT = c3(2, L)
        OTt = c3(1, L)
        TMP = c3(1, L)
        CS = c3(8, 2)
        CT = c3(8, 2)
        ADB = c3(2, 512)
        b1base = at[0]
        P = c3(4, L)
        PT = carve(2 * 9 * 256).rearrange("p (s t n) -> p s t n", s=2, t=9)
        ST = carve(64).rearrange("p (s n) -> p s n", s=8)
        ctab = [sp.dma(ch("c1"), cosT, A["k_cos"]), sp.dma(ch("c1"), sinT, A["k_sin"]),
                sp.dma(ch("c1"), rotm, A["k_rot"])]
        consts = consts + ctab + c0

        LB = SM[:, 0:2]
        RSTD = SM[:, 8:26]
        lt = P[:, 0, 0:512].rearrange("p (l a n) -> p l a n", l=2, a=4)
        dl = sp.dma(ch("c2"), P[:, 0, 0:512], A["k_lam"])
        for l in range(2):
            pr = P[:, 1, 0:128].rearrange("p (a n) -> p a n", a=2)
            x = tt(pr, lt[:, l, 0:4:2, :], lt[:, l, 1:4:2, :], ALU.mult, [dl] if l == 0 else [y])
            y = dve.add(lambda e, o=SM[:, 2:4], a=pr: e.tensor_reduce(o, a, AX.X, ALU.add), [x] + ([z] if l else []))
            z = ac(SM[:, 4:6], SM[:, 2:4], ACT.Exp, [y] + ([y2] if l else []))
            y1 = tt(SM[:, 6:7], SM[:, 5:6], SM[:, 4:5], ALU.subtract, [z])
            y2 = ts(LB[:, l:l + 1], SM[:, 6:7], -LAM_INIT[l], None, ALU.add, after=[y1])
            y = y2
        x = pool.dma(ch("a0"), CS, A["k_c"].rearrange("p (k c) -> p k c", k=8))
        x = ac(CT, CS, ACT.Exp, [x], scale=-1.0)
        x = ts(CT, CT, 1.0, None, ALU.add, after=[x])
        x = recip(CT, CT, [x])
        csd = tt(CS, CS, CT, ALU.mult, [x])
        pend.extend(ctab + c0)
        barrier()

        hs = S["hs"]
        os_ = S["os"]

        def stats(srcs, cols, eps, junk):
            q = None
            for i, (x, after) in enumerate(srcs):
                r = x.shape[0]
                q = ac(junk[0:r, :], x, ACT.Square, after + ([q] if q else []), accum=cols[0:r, i:i + 1])
            v = ts(cols[0:r, :], cols[0:r, :], 1.0 / D, eps, ALU.mult, ALU.add, [q])
            v = ac(cols[0:r, :], cols[0:r, :], ACT.Ln, [v])
            return ac(cols[0:r, :], cols[0:r, :], ACT.Exp, [v], scale=-0.5)

        def fill_a(tiles, ready, gain, bias=None, tb=None):
            tr_ = Ring(2)
            groups_ = [tiles[i:i + 4] for i in range(0, len(tiles), 4)]
            at_ = 0
            for g in groups_:
                tot = sum(x.shape[0] for x, _ in g)
                c = g[0][1]
                for k in range(KT):
                    b, rel = banks.take()
                    o = 0
                    for i, (x, _) in enumerate(g):
                        r = x.shape[0]
                        m = tr(bank(b)[:, o:o + r], x[:, 128 * k:128 * k + 128], [ready[at_ + i]] + rel)
                        o += r
                    dst_h, dst_l = AH[:, k, c:c + tot], AL[:, k, c:c + tot]
                    if bias is None:
                        h = ac(dst_h, bank(b)[:, 0:tot], ACT.Copy, [m], scale=gain(k))
                        lo = stt(dst_l, bank(b)[:, 0:tot], gain(k), f(dst_h), ALU.mult, ALU.subtract, [h])
                        banks.free(b, [lo])
                    else:
                        ti, trel = tr_.take()
                        tv = tb[:, ti, 0:tot]
                        h = ac(tv, bank(b)[:, 0:tot], ACT.Identity, [m] + trel, scale=gain(k), bias=bias(k))
                        banks.free(b, [h])
                        h2 = cp(dst_h, tv, [h])
                        lo = tt(dst_l, tv, f(dst_h), ALU.subtract, [h2])
                        tr_.free(ti, [lo])
                at_ += len(g)
            return lo, m

        vring, qring, gring = Ring(2), Ring(2), Ring(2)
        groups = {}
        pring, ptring, oring, tring = Ring(4), Ring(2), Ring(1), Ring(1)
        def ff_phase(l, ready):
            zt = TMP[:, 0, :]
            e1 = GT[:, 0, :]
            e2 = GT[:, 1, :]
            last = []

            def evac(o, c, n, m):
                x = ac(zt[0:8, c:c + n], o[0:8, :], ACT.Identity, [m], bias=COLS[0:8, 18 + l:19 + l])
                last.append(x)
                return [x]
            yield from gemm_f(CH, evac, ready)
            z, a, u = zt[0:8, :], e1[0:8, :], e2[0:8, :]
            m1 = ts(a, z, -1.0, None, ALU.mult, after=last)
            m1 = tt(a, a, z, ALU.max, [m1])
            m2 = ac(a, a, ACT.Exp, [m1], scale=-1.0)
            m3 = ts(u, a, 1.0, None, ALU.add, after=[m2])
            m4 = ts(z, z, 0.0, None, ALU.min)
            m5 = stt(a, u, -1.0, a, ALU.add, ALU.subtract, [m3])
            m6 = tt(z, z, a, ALU.add, [m4, m5])
            m7 = ac(u, u, ACT.Ln, [m3, m5])
            m8 = tt(z, z, u, ALU.subtract, [m6, m7])
            m9 = dve.add(lambda e: e.memset(u, 1.0), [m8])
            m10 = dve.add(lambda e: e.tensor_tensor_scan(a, u, z, 0.0, ALU.mult, ALU.add), [m9])
            h = ac(C2[0:8, :], a, ACT.Copy, [m10])
            lo = tt(C2[32:40, :], a, f(C2[0:8, :]), ALU.subtract, [h])
            ffdone[:] = [lo]
            tring.rel[0] = [lo]

        ffdone = []

        def proj(l, g, ready):
            fox = g >= 4
            while not qring.ready():
                yield 0
            s, qrel = qring.take()
            fin = {"q": [], "k": [], "g": [], "v": []}
            me = {"s": s, "fin": fin, "have": set()}
            groups[(l, g)] = me
            for kind, dst in (("q", QT), ("k", KTt)):
                sc = 0.125 if kind == "q" else 1.0
                if fox:
                    def evac(o, c, n, m, dst=dst, sc=sc, kind=kind):
                        x = ac(dst[:, s, c:c + n], o, ACT.Copy, [m] + qrel, scale=sc)
                        fin[kind].append(x)
                        return [x]
                    yield from gemm_f(CH, evac, ready)
                else:
                    while not tring.ready():
                        yield
                    ti, trel = tring.take()
                    part = []

                    def evac(o, c, n, m, sc=sc):
                        x = ac(TMP[:, ti, c:c + n], o, ACT.Copy, [m] + trel, scale=sc)
                        part.append((c, n, x))
                        return [x]
                    yield from gemm_f(CH, evac, ready)
                    for c, n, x in part:
                        while not banks.ready():
                            yield
                        b, rel = banks.take()
                        m = mm(bank(b)[:, 0:n], rotm, TMP[:, ti, c:c + n], True, True, [x] + rel)
                        y = tt(dst[:, s, c:c + n], bank(b)[:, 0:n], sinT[:, c:c + n], ALU.mult, [m] + qrel)
                        banks.free(b, [y])
                        y2 = tt(TMP[:, ti, c:c + n], TMP[:, ti, c:c + n], cosT[:, c:c + n], ALU.mult, [m], q=pool)
                        y3 = tt(dst[:, s, c:c + n], dst[:, s, c:c + n], TMP[:, ti, c:c + n], ALU.add, [y, y2])
                        fin[kind].append(y3)
                        yield 0.6
                    tring.free(ti, [fin[kind][-1]])
                me["have"].add(kind)
            while not (tring.ready() and vring.ready()):
                yield 0
            vs, vrel = vring.take()
            me["vs"] = vs
            ti, trel = tring.take()
            part = []

            def evac(o, c, n, m):
                x = ac(TMP[:, ti, c:c + n], o, ACT.Copy, [m] + trel)
                part.append(x)
                return [x]
            yield from gemm_f(CH, evac, ready)
            for quad in ((0, 1, 2, 3), (4, 5, 6, 7), (8,)):
                while not banks.ready():
                    yield
                b, rel = banks.take()
                for i, t in enumerate(quad):
                    cc, n = (16 + 128 * t, 128) if t < 8 else (0, 16)
                    m = tr(bank(b)[0:n, 128 * i:128 * i + 128], TMP[:, ti, cc:cc + n], [part[-1]] + rel)
                if quad[0] < 8:
                    x = cp(V[:, vs, quad[0]:quad[0] + 4, :], bank(b)[:, 0:512].rearrange("p (a b) -> p a b", a=4), [m] + vrel)
                else:
                    x = cp(V[0:16, vs, 8, :], bank(b)[0:16, 0:128], [m] + vrel)
                banks.free(b, [x])
                fin["v"].append(x)
                yield 0.5
            tring.free(ti, [m])
            me["have"].add("v")
            while not gring.ready():
                yield 0
            gs, grel = gring.take()
            me["gs"] = gs

            def evac(o, c, n, m):
                x = ac(GT[:, gs, c:c + n], o, ACT.Tanh, [m] + grel + ffdone, scale=0.5)
                y = stt(GT[:, gs, c:c + n], GT[:, gs, c:c + n], 1.0, o, ALU.add, ALU.mult, [x])
                fin["g"].append(y)
                return [y]
            yield from gemm_f(CH, evac, ready)
            me["have"].add("g")
            yield 0

        stn = [0]
        strel = [[] for _ in range(8)]

        class Attention:

            def __init__(self, l, g):
                self.l, self.g, self.fox = l, g, g >= 4
                self.blocks = [(6, 7), (4, 5), (2, 3), (0, 1)] + ([(8,)] if l == 0 else [])
                self.by, self.pts, self.o_done = {}, {}, []

            def units(self, bi):
                return [(j, m) for m in range(2) for j in reversed(self.blocks[bi])]

            def scores(self, j, m):
                fox, l, g, me = self.fox, self.l, self.g, groups[(self.l, self.g)]
                s = me["s"]
                qk = [me["fin"]["q"][-1], me["fin"]["k"][-1]]
                ring, b0 = (sA, 0) if j % 2 == 1 else (sB, 3)
                _, rel = ring.take()
                pi, prel = pring.take()
                meta = j == 8
                q0 = 0 if meta else NM + 128 * j
                W = NM if meta else NM + 128 * (j + 1)
                off = 512 * b0
                rows = NM if meta else 128
                dm0 = 0 if meta else W - 128
                r0 = 64 * m
                for i, (a, b) in enumerate(pieces(0, W)):
                    x = mm(PSf[:, off + a:off + b], QT[r0:r0 + 64, s, q0:q0 + 128], KTt[r0:r0 + 64, s, a:b], True, False,
                           qk + rel if i == 0 else [])
                    if fox:
                        x = mm(PSf[:, off + a:off + b], selr[:, 2 * (g - 4) + m, :], C2[:, a:b], False, False, ffdone)
                if fox or not meta:
                    for a, b in pieces(dm0, W):
                        x = mm(PSf[:, off + a:off + b], identr[:, :], maskr[:, int(fox), a - dm0:b - dm0], False, True)
                si = stn[0] % 8
                stn[0] += 1
                st = ST[0:rows, si, :]
                w = PSf[0:rows, off:off + W]
                n = rmax_neg(st[:, 0:1], w, [x] + strel[si])
                p = P[0:rows, pi, 0:W]
                e = ac(p, w, ACT.Exp, [n] + prel, bias=st[:, 0:1], accum=st[:, 1:2])
                ring.free(0, [e])
                if (j, m) == self.units(len(self.blocks) - 1)[-1]:
                    qring.free(s, [x])
                self.by[(j, m)] = (pi, rows, W, e, si)

            def normalise(self, bi):
                blk = self.blocks[bi]
                for j, m in self.units(bi):
                    pi, rows, W, e, si = self.by[(j, m)]
                    st = ST[0:rows, si, :]
                    p = P[0:rows, pi, 0:W]
                    r = recip(st[:, 2:3], st[:, 1:2], [e])
                    if self.fox or m == 0:
                        y = ts(p, p, st[:, 2:3], None, ALU.mult, after=[r])
                    else:
                        y = ts(st[:, 3:4], st[:, 2:3], LB[0:rows, self.l:self.l + 1], None, ALU.mult, after=[r])
                        p0 = self.by[(j, 0)][0]
                        y = stt(P[0:rows, p0, 0:W], p, st[:, 3:4], P[0:rows, p0, 0:W], ALU.mult, ALU.add, [y, self.by[(j, 0)][3]])
                        pring.free(pi, [y])
                        self.by[(j, 0)] = (p0, rows, W, y, self.by[(j, 0)][4])
                    strel[si] = [y]
                    if self.fox or m == 0:
                        self.by[(j, m)] = (pi, rows, W, y, si)

            def transposes(self, bi):
                blk = self.blocks[bi]
                meta = blk == (8,)
                nq = NM if meta else 256
                tiles = [8] if meta else [8] + list(range(blk[1] + 1))
                pts = []
                for m in (range(2) if self.fox else range(1)):
                    pt, ptrel = ptring.take()
                    evs = []
                    todo = [tiles[0:1]] + [tiles[i:i + 2] for i in range(1, len(tiles), 2)]
                    for grp in todo:
                        b, rel = banks.take()
                        kr = NM if grp[0] == 8 else 128
                        for i, t in enumerate(grp):
                            for jj, j in enumerate(blk):
                                if t < 8 and t > j:
                                    continue
                                p0, rows, W, y, _ = self.by[(j, m)]
                                ka = 0 if t == 8 else NM + 128 * t
                                x = tr(bank(b)[0:kr, 256 * i + 128 * jj:256 * i + 128 * jj + rows],
                                       P[0:rows, p0, ka:ka + kr], [y] + rel)
                        if grp[0] == 8:
                            ev = [evac_pt(PT[0:kr, pt, 8, 0:nq], bank(b)[0:kr, 0:nq], [x] + ptrel)]
                        elif grp[-1] == blk[-1]:
                            ev = [cp(PT[:, pt, grp[0], :], bank(b)[:, 0:256], [x] + ptrel),
                                  cp(PT[:, pt, grp[1], 128:256], bank(b)[:, 384:512], [x])]
                        else:
                            ev = [evac_pt(PT[:, pt, grp[0]:grp[0] + 2, :].rearrange("p a b -> p (a b)"),
                                          bank(b)[:, 0:512], [x] + ptrel)]
                        banks.free(b, ev)
                        evs += ev
                    for j in blk:
                        pring.free(self.by[(j, m)][0], [x])
                    pts.append((pt, evs))
                self.pts[bi] = (pts, tiles, nq, meta)

            def values(self, bi):
                me = groups[(self.l, self.g)]
                blk = self.blocks[bi]
                fox, vs, fin = self.fox, me["vs"], me["fin"]
                pts, tiles, nq, meta = self.pts[bi]
                q0 = 0 if meta else NM + 128 * blk[0]
                if bi == 0:
                    self.oi, self.orel = oring.take()
                ab, arel = banks.take()
                for i, t in enumerate(tiles):
                    for m, (pt, evs) in enumerate(pts):
                        mr = (64 * m, 64) if fox else (0, 128)
                        vc = slice(64 * m, 64 * m + 64) if fox else slice(0, 128)
                        kr = NM if t == 8 else 128
                        qa = 128 if (not meta and t == blk[1]) else 0
                        x = mm(bank(ab)[mr[0]:mr[0] + mr[1], qa:nq], V[0:kr, vs, t, vc], PT[0:kr, pt, t, qa:nq],
                               i == 0, i == len(tiles) - 1, evs + fin["v"] + arel if i == 0 else [])
                for pt, _ in pts:
                    ptring.free(pt, [x])
                y = cp(OTt[:, self.oi, q0:q0 + nq], bank(ab)[:, 0:nq], [x] + self.orel)
                banks.free(ab, [y])
                self.o_done.append(y)
                if bi == len(self.blocks) - 1:
                    vring.free(vs, [x])

            def finish(self):
                l, g, me = self.l, self.g, groups[(self.l, self.g)]
                gs, fin, oi = me["gs"], me["fin"], self.oi
                o = OTt[:, oi, :]
                cs = CH if l == 0 else [(NM, 352), (NM + 352, 336), (NM + 688, 336)]
                a, b_ = cs[0][0], cs[-1][0] + cs[-1][1]
                if not self.fox:
                    while not tring.ready():
                        yield
                    ti, trel = tring.take()
                    t = TMP[:, ti, :]
                    q = ac(t[:, a:b_], o[:, a:b_], ACT.Square, [self.o_done[-1]] + trel)
                    yield
                    vv = []
                    for c, n in cs:
                        b, rel = banks.take()
                        x = mm(bank(b)[:, 0:n], ones, t[:, c:c + n], True, True, [q] + rel)
                        v = ts(t[:, c:c + n], bank(b)[:, 0:n], 1.0 / 128, 1e-5, ALU.mult, ALU.add, [x])
                        banks.free(b, [v])
                        vv.append(v)
                    v = ac(t[:, a:b_], t[:, a:b_], ACT.Ln, vv)
                    v = ac(t[:, a:b_], t[:, a:b_], ACT.Exp, [v], scale=-0.5)
                    v = stt(o[:, a:b_], o[:, a:b_], COLS[:, 16 + l:17 + l], t[:, a:b_], ALU.mult, ALU.mult, [v])
                    tring.free(ti, [v])
                    sc = 0.5 * (1.0 - LAM_INIT[l])
                else:
                    v = self.o_done[-1]
                    sc = 0.5
                c, n = (0, L) if l == 0 else (NM, SEQ)
                y = stt(o[:, c:c + n], o[:, c:c + n], sc, GT[:, gs, c:c + n], ALU.mult, ALU.mult, [v, fin["g"][-1]])
                gring.free(gs, [y])
                self.gated = y
                if g == 7:
                    oring.free(oi, [y])
                else:
                    dst = pool.dma(ch(f"os{g % 2}"), os_[g][:, c:c + n], o[:, c:c + n], [y])
                    oring.free(oi, [dst])
                    os_done.append(dst)
                yield

        def evac_pt(o, a, after):
            epar[0] ^= 1
            return ac(o, a, ACT.Copy, after) if epar[0] else cp(o, a, after)

        BUDGET = [13.0, 12.0, 10.0, 8.0, 2.0]

        def attention_phase(l, ready):
            filler = chain(*[proj(l, g, ready) for g in range(8)])
            alive = [True]

            def fill(us):
                while us > 0 and alive[0]:
                    c = next(filler, None)
                    if c is None:
                        alive[0] = False
                    elif c == 0:
                        return
                    else:
                        us -= c

            def split_o(g, src, after):
                c, n = (0, L) if l == 0 else (NM, SEQ)
                h = ac(AH[:, g, c:c + n], src[:, c:c + n], ACT.Copy, after + lastproj)
                lo = tt(AL[:, g, c:c + n], src[:, c:c + n], f(AH[:, g, c:c + n]), ALU.subtract, [h])
                return lo

            def reload(n):
                for _ in range(n):
                    g = len(los)
                    if g >= 7 or g >= len(os_done):
                        return
                    if not lastproj:
                        lastproj.append([i for i in pe.items if i.fn is not None][-1])
                        sl = qring.i
                        stage_rel[:] = [qring.rel[sl], qring.rel[sl]]
                        stage[:] = [QT[:, sl, :], KTt[:, sl, :]]
                        assert qring.ready()
                    j = g % 2
                    c, n_ = (0, L) if l == 0 else (NM, SEQ)
                    d = pool.dma(ch(f"o{j}"), stage[j][:, c:c + n_], os_[g][:, c:c + n_], stage_rel[j] + [os_done[g]])
                    lo = split_o(g, stage[j], [d])
                    stage_rel[j] = [lo]
                    los.append(lo)
            lastproj, stage, stage_rel, los = [], [], [[], []], []

            def have(g, kind):
                while kind not in groups.get((l, g), {"have": ()})["have"]:
                    n = len(pe.items)
                    assert next(filler, None) is not None or kind in groups[(l, g)]["have"]

            atts = [Attention(l, g) for g in range(8)]
            seq = [(a, bi) for a in atts for bi in range(len(a.blocks))]
            have(0, "k")
            for u in atts[0].units(0):
                atts[0].scores(*u)
            atts[0].normalise(0)
            fill(8)
            for i, (a, bi) in enumerate(seq):
                a.transposes(bi)
                nxt = seq[i + 1] if i + 1 < len(seq) else None
                us = []
                if nxt:
                    have(nxt[0].g, "k")
                    us = nxt[0].units(nxt[1])
                    for u in us[:2]:
                        nxt[0].scores(*u)
                have(a.g, "v")
                a.values(bi)
                for u in us[2:]:
                    nxt[0].scores(*u)
                if nxt:
                    nxt[0].normalise(nxt[1])
                last = bi == len(a.blocks) - 1
                if a.g == 7:
                    fill(1000)
                    if not alive[0]:
                        reload(2)
                b = BUDGET[bi]
                if last:
                    have(a.g, "g")
                    for _ in a.finish():
                        fill(3)
                        b -= 3
                fill(b)
            reload(7)
            assert len(los) == 7
            a = atts[7]
            y = a.gated
            los.append(split_o(7, OTt[:, a.oi, :], [y]))
            oring.rel[0] = [los[-1]]
            for r in (qring, vring, gring, tring):
                assert r.ready()
            qring.rel[0] = qring.rel[0] + los[-3:]
            qring.rel[1] = qring.rel[1] + los[-3:]
            del os_done[:]
            return [[x] for x in los]

        epar = [0]
        os_done = []

        def chain(*gs):
            for g in gs:
                yield from g

        def out_proj(tiles, evac, ready):
            nb = (len(tiles) + 1) // 2
            for q in range(4):
                bs = [banks.take() for _ in range(nb)]

                def part(kk, t, w):
                    ti, lo = w
                    b, rel = bs[t // 2]
                    o = bank(b)[:, 256 * (t % 2):256 * (t % 2) + 256]
                    for k in range(4):
                        wv = slice(256 * k, 256 * k + 256)
                        kt = 4 * kk + k
                        m = mm3(o, AH[:, kt, tiles[t]:tiles[t] + 128], AL[:, kt, tiles[t]:tiles[t] + 128], WH[:, ti, wv], WL[:, ti, wv],
                                kt == 0 and t % 2 == 0, kt == 7,
                                ([lo] if k == 0 else []) + (rel if kt == 0 else []) + (ready[kt] if q == 0 else []))
                    return m

                def close(t, m):
                    if t % 2 == 1 or t == len(tiles) - 1:
                        n = t % 2 + 1
                        b, _ = bs[t // 2]
                        banks.free(b, evac(bank(b)[:, 0:256 * n].rearrange("p (a b) -> p a b", a=n), t - n + 1, n, q, m))
                if q < 3:
                    for kk in range(2):
                        w = weights.next()
                        for t in range(len(tiles)):
                            m = part(kk, t, w)
                            if kk == 1:
                                close(t, m)
                        wr.free(w[0], [m])
                else:
                    ws = [weights.next(), weights.next()]
                    for t0 in range(0, len(tiles), 2):
                        pair = range(t0, min(t0 + 2, len(tiles)))
                        for kk in range(2):
                            for t in pair:
                                m = part(kk, t, ws[kk])
                                if kk == 1:
                                    close(t, m)
                    for w in ws:
                        wr.free(w[0], [m])

        HT = R[:, b1base:b1base + 8192].rearrange("p (a b) -> p a b", a=8)
        HM = OTt[:, 0, 0:1024]
        JK = TMP[:, 0, 0:1024]
        ada = S["ada"]
        ar_ = Ring(2)

        def ada_unit(i):
            j, rel = ar_.take()
            d0 = pool.dma(ch(f"ab{j}"), ADB[0:2, j, :], A["k_brow"][:, 512 * i:512 * i + 512], rel)
            b, rel = banks.take()
            for kk in range(4):
                s, dd = weights.next(False)
                for k in range(2):
                    m = mm(bank(b)[0:2, :], CS[:, 2 * kk + k, :], W32[:, s, 512 * k:512 * k + 512],
                           kk + k == 0, kk + k == 4, [dd, csd] + rel)
                w32.free(s, [m])
            y = tt(ADB[0:2, j, :], bank(b)[0:2, :], ADB[0:2, j, :], ALU.add, [m, d0])
            banks.free(b, [y])
            d = pool.dma(ch(f"as{j}"), ada[:, 512 * i:512 * i + 512], ADB[0:2, j, :], [y])
            ar_.free(j, [d])
            ada_done[j] = d
        ada_done = {}

        def layer_norm(l, tiles):
            ready = []
            for q0, n in ((0, 4), (4, 4), (8, 1)):
                g = tiles[q0:q0 + n]
                v = stats([(x, after) for x, _, after, _ in g], RSTD[:, q0:q0 + n], 1e-6, JK)
                for i, (x, _, _, after) in enumerate(g):
                    ready.append(ts(x, x, RSTD[0:x.shape[0], q0 + i:q0 + i + 1], None, ALU.mult, after=[v] + after))
            lo, m = fill_a([(x, c) for x, c, _, _ in tiles], ready, lambda k: COLS[:, 8 * l + k:8 * l + k + 1])
            for r in (pring, ptring, oring, tring):
                for i in range(r.n):
                    r.rel[i] = [m]
            gring.rel[0] = gring.rel[1] = [m]
            return [lo]

        def layer(l, ready):
            banks_few()
            for _ in ff_phase(l, ready):
                pass
            lastg = attention_phase(l, ready)
            banks_all()
            free = pring.rel[0] + pring.rel[1] + pring.rel[2] + pring.rel[3] + ptring.rel[0] + ptring.rel[1]
            x_rows = A["x"][0] if l == 0 else hs[NM:L, :]
            loads = []
            for t in range(8):
                loads.append(pool.dma(ch(f"h{t}"), HT[:, t, :], x_rows[128 * t:128 * t + 128, :], free))
            if l == 0:
                loads.append(pool.dma(ch("h8"), HM[0:NM, :], A["meta_tokens"], oring.rel[0]))
            done = {}

            def evac(b, t, n, q, last):
                c = slice(256 * q, 256 * q + 256)
                if t < 8:
                    y = tt(HT[:, t:t + 2, c], HT[:, t:t + 2, c], b, ALU.add, [last] + loads[t:t + 2])
                else:
                    y = tt(HM[0:NM, c], HM[0:NM, c], b[0:NM, 0, :], ALU.add, [last, loads[8]])
                if q == 3:
                    for i in range(t, t + n):
                        done[i] = y
                return [y]
            cols = [NM + 128 * t for t in range(8)] + ([0] if l == 0 else [])
            out_proj(cols, evac, lastg)
            return done

        def final_norm(done, ready):
            FG = KTt[:, 0, 0:1024]
            d0 = pool.dma(ch("b0"), FG, A["k_fg"], qring.rel[0] + qring.rel[1])
            dc = [pool.dma(ch(f"r{t}"), XC[t], A["ctx_2"][0][128 * t:128 * t + 128, :], gring.rel[t]) for t in range(2)]
            v = stats([(HT[:, t, :], [done[t]]) for t in range(8)], RSTD[:, 0:8], 1e-6, JK)
            ada_unit(8)
            ys, st_ = [], []
            for t in range(8):
                x = HT[:, t, :]
                ys.append(stt(x, x, RSTD[:, t:t + 1], FG, ALU.mult, ALU.mult, [v, d0]))
                st_.append(pool.dma(ch(f"s{t}"), xs[128 * t:128 * t + 128, :], x, [ys[-1]]))
            pend.extend(st_)
            ada_unit(9)
            v = stats([(XC[t], [dc[t]]) for t in range(2)], RSTD[:, 16:18], 1e-6, JK)
            for t in range(2):
                readyc[t] = ts(XC[t], XC[t], RSTD[:, 16 + t:17 + t], None, ALU.mult, after=[v])
            for i, t0 in enumerate((0, 4)):
                v = stats([(HT[:, t, :], [ys[t]]) for t in range(t0, t0 + 4)], RSTD[:, 8 + t0:12 + t0], 1e-6, JK)
                ada_unit(10 + i)
                for t in range(t0, t0 + 4):
                    x = HT[:, t, :]
                    ready[t] = ts(x, x, RSTD[:, 8 + t:9 + t], None, ALU.mult, after=[v, st_[t]])

        loads = [pool.dma(ch(f"h{t}"), HT[:, t, :], A["x"][0][128 * t:128 * t + 128, :]) for t in range(8)]
        loads.append(pool.dma(ch("h8"), HM[0:NM, :], A["meta_tokens"]))
        banks_all()
        for i in range(4):
            ada_unit(i)
        tiles = [(HT[:, t, :], NM + 128 * t, [loads[t]], []) for t in range(8)] + [(HM[0:NM, :], 0, [loads[8]], [])]
        done = layer(0, layer_norm(0, tiles))
        for i in range(4, 8):
            ada_unit(i)
        stores = [pool.dma(ch(f"s{t}"), hs[NM + 128 * t:NM + 128 * t + 128, :], HT[:, t, :], [done[t]]) for t in range(8)]
        tiles = [(HT[:, t, :], NM + 128 * t, [done[t]], [stores[t]]) for t in range(8)] + [(HM[0:NM, :], 0, [done[8]], [])]
        done = layer(1, layer_norm(1, tiles))
        xs = S["xs"]
        XC = [GT[:, t, 0:1024] for t in range(2)]
        readyx, readyc = {}, {}
        final_norm(done, readyx)


        def phase(n=0):
            barrier((act, dve, pool))
            at[0] = persist + n

        def r3(a, b):
            return carve(a * b).rearrange("p (a b) -> p a b", a=a)

        CH2 = [(0, 512), (512, 512)]

        banks_all()
        G1 = SM[:, 30:54].rearrange("p (a k) -> p a k", a=3)
        B1 = COLS[:, 32:56].rearrange("p (a k) -> p a k", a=3)
        LG = SM[:, 54:62]

        def ada_phase():
            phase()
            AD = r3(32, 2)
            K2 = carve(24)
            RW_ = r3(8, 512)
            GQ = carve(16).rearrange("p (a k) -> p a k", a=2)
            d2 = pool.dma(ch("a1"), K2, A["k_cols2"])
            d3 = pool.dma(ch("a2"), GQ, A["k_gpre"].rearrange("p (a k) -> p a k", a=2))
            ad = list(ada_done.values())
            d = [pool.dma(ch("a3"), RW_[0:2, 0:4, :], ada[:, 0:2048].rearrange("c (a b) -> c a b", a=4), ad),
                 pool.dma(ch("a4"), RW_[0:2, 4:8, :], ada[:, 3072:5120].rearrange("c (a b) -> c a b", a=4), ad)]
            z, a, u = K2[:, 0:8], K2[:, 8:16], K2[:, 16:24]
            zz = LG
            x = ts(a, z, -1.0, None, ALU.mult, after=[d2])
            x = tt(a, a, z, ALU.max, [x])
            x = ac(a, a, ACT.Exp, [x], scale=-1.0)
            x3_ = ts(u, a, 1.0, None, ALU.add, after=[x])
            x4 = ts(zz, z, 0.0, None, ALU.min)
            x5 = stt(a, u, -1.0, a, ALU.add, ALU.subtract, [x3_])
            x6 = tt(zz, zz, a, ALU.add, [x4, x5])
            x7 = ac(u, u, ACT.Ln, [x3_, x5])
            tt(zz, zz, u, ALU.subtract, [x6, x7])
            b2, rel2 = banks.take()
            for i in range(8):
                for k in range(4):
                    m = tr(bank(b2)[:, 8 * i + 2 * k:8 * i + 2 * k + 2], RW_[0:2, i, 128 * k:128 * k + 128], d + rel2)
            x = cp(AD, bank(b2)[:, 0:64].rearrange("p (k c) -> p k c", k=32), [m])
            banks.free(b2, [x])
            for i, (sc_, cc, gg) in enumerate(((8, 0, 0), (8, 1, 0), (24, 0, 1))):
                y = stt(G1[:, i, :], AD[:, sc_:sc_ + 8, cc], 1.0, GQ[:, gg, :], ALU.add, ALU.mult, [x, d3])
                y = cp(B1[:, i, :], AD[:, sc_ - 8:sc_, cc], [x])

        def rstd_of(col, rows, scale, eps, after):
            v = ts(col, col, scale, eps, ALU.mult, ALU.add, after=after)
            v = ac(col, col, ACT.Ln, [v])
            return ac(col, col, ACT.Exp, [v], scale=-0.5)

        def gate_rows(dst, tmp, i, c, after=()):
            d = [pool.dma(ch("ga"), dst, ada[0:1, 1024 * c:1024 * c + 1024].broadcast_to([128, 1024]), list(after)),
                 pool.dma(ch("gb"), tmp, A["k_gpost"][:, 1024 * i:1024 * i + 1024], list(after))]
            return tt(dst, dst, tmp, ALU.mult, d)

        def prep_x(keep):
            phase(keep)
            TB = r3(2, 512)
            return fill_a([(HT[:, t, :], 128 * t) for t in range(8)], readyx, lambda k: G1[:, 0, k:k + 1], lambda k: B1[:, 0, k:k + 1], TB)[0]

        FM = [0]

        def ctx_phase():
            phase()
            SC = r3(4, 256)
            XI = carve(1024).rearrange("p (h d c) -> p h d c", h=4, d=2)
            DM = r3(4, 128)
            ZE = r3(8, 4)
            FM[0] = at[0] - persist
            TB = r3(2, 512)
            KC, VC = r3(2, 512), r3(2, 512)
            TT = carve(256)
            CT = carve(8 + 4 * 128 + 256)
            E1, E2 = carve(128), carve(128)
            d0 = pool.dma(ch("b1"), CT, A["k_dec"])
            lo, _ = fill_a([(XC[t], 128 * t) for t in range(2)], readyc, lambda k: G1[:, 1, k:k + 1], lambda k: B1[:, 1, k:k + 1], TB)
            x = None
            for dr in range(2):
                for h in range(4):
                    lg = LG[:, 4 * dr + h:4 * dr + h + 1]
                    x = ac(ZE[:, 4 * dr + h, :], CT[:, 4 * dr:4 * dr + 4], ACT.Exp, [d0], scale=lg)
                    x = ac(XI[:, h, dr, :], CT[:, 8 + 128 * dr:136 + 128 * dr], ACT.Exp, [], scale=lg)
            y = None
            for h in range(4):
                x = ac(E1, CT[:, 264:392], ACT.Exp, [y] if y else [], scale=LG[:, h:h + 1])
                x2_ = ac(E2, CT[:, 392:520], ACT.Exp, [], scale=LG[:, 4 + h:5 + h])
                y = tt(DM[:, h, :], E1, CT[:, 520:648], ALU.mult, [x])
                y2_ = tt(E2, E2, CT[:, 648:776], ALU.mult, [x2_])
                y = tt(DM[:, h, :], DM[:, h, :], E2, ALU.add, [y, y2_])

            def evac(b, t, n, q, last):
                c = 256 * (q % 2)
                if q < 2:
                    z = ac(KC[:, :, c:c + 256], b, ACT.Copy, [last], scale=float(128 ** -0.5))
                else:
                    z = ac(VC[:, :, c:c + 256], b, ACT.Copy, [last])
                fin.append(z)
                return [z]
            fin = []
            out_proj([0, 128], evac, [[lo]] + [[]] * 7)
            tr_ = Ring(1)
            for h in range(4):
                b, rel = banks.take()
                for t in range(2):
                    _, trel = tr_.take()
                    y1_ = ts(TT[:, 0:128], VC[:, t, 128 * h:128 * h + 128], ZE[:, h, t:t + 1], None, ALU.mult, after=[fin[-1], x] + trel)
                    y2_ = ts(TT[:, 128:256], VC[:, t, 128 * h:128 * h + 128], ZE[:, 4 + h, t:t + 1], None, ALU.mult)
                    m = mm(bank(b)[:, 0:256], KC[:, t, 128 * h:128 * h + 128], TT[:, 0:256], t == 0, t == 1, [y2_] + rel)
                    tr_.free(0, [m])
                y = cp(SC[:, h, :], bank(b)[:, 0:256], [m])
                banks.free(b, [y])
            return SC, XI, DM, ZE

        def mixer(SC, XI, DM, ZE, ready):
            phase(FM[0])
            CO, SI = carve(1024), carve(1024)
            QH, KH, GH_, OH = carve(1024), carve(1024), carve(1024), carve(1024)
            T1, T2 = r3(2, 512), r3(2, 512)
            VM, KM = r3(8, 128), r3(8, 128)
            VZ = r3(8, 256)
            PV = r3(8, 256)
            QX = r3(2, 1024)
            SS = r3(8, 128)
            T3, T4 = r3(2, 512), r3(2, 512)
            dt = [pool.dma(ch("b2"), CO, A["k_cos2"]), pool.dma(ch("b2"), SI, A["k_sin2"])]
            tr_ = Ring(2)
            t3r = [[], []]
            prev = {"q": [], "k": [], "v": [], "g": [], "o": [], "km": []}
            dones = [{"q": [], "k": [], "v": [], "g": []} for _ in range(4)]

            def go(gen):
                for _ in gen:
                    pass

            def project(h, kind):
                done = dones[h]
                if kind in "qk":
                    dst, sc_ = (QH, 1.0) if kind == "q" else (KH, float(128 ** -0.5))

                    def evac(o, c, n, m):
                        ti, trel = tr_.take()
                        x = ac(T1[:, ti, :], o, ACT.Copy, [m] + trel, scale=sc_)
                        y1 = tt(dst[:, c:c + n], T1[:, ti, :], CO[:, c:c + n], ALU.mult, [x] + dt + prev[kind])
                        y2 = tt(T2[0:64, ti, :], T1[64:128, ti, :], SI[64:128, c:c + n], ALU.mult)
                        y3 = tt(T2[64:128, ti, :], T1[0:64, ti, :], SI[0:64, c:c + n], ALU.mult)
                        y4 = tt(dst[:, c:c + n], dst[:, c:c + n], T2[:, ti, :], ALU.add, [y3])
                        tr_.free(ti, [y4])
                        done[kind].append(y4)
                        return [x]
                elif kind == "v":
                    def evac(o, c, n, m):
                        ti, trel = tr_.take()
                        x = ac(T1[:, ti, :], o, ACT.Copy, [m] + trel)
                        done["v"].append((ti, c, x))
                        return [x]
                else:
                    def evac(o, c, n, m):
                        x = ac(GH_[:, c:c + n], o, ACT.Tanh, [m] + prev["g"], scale=0.5)
                        y = stt(GH_[:, c:c + n], GH_[:, c:c + n], 1.0, o, ALU.add, ALU.mult, [x])
                        done["g"].append(y)
                        return [y]
                return gemm_f(CH2, evac, ready)

            def turn_v(h):
                out = []
                for ti, c, x in dones[h]["v"]:
                    b, rel = banks.take()
                    for i in range(4):
                        m = tr(bank(b)[:, 128 * i:128 * i + 128], T1[:, ti, 128 * i:128 * i + 128], [x] + rel)
                    tr_.free(ti, [m])
                    y = cp(VM[:, c // 128:c // 128 + 4, :], bank(b).rearrange("p (a b) -> p a b", a=4), [m] + prev["v"])
                    banks.free(b, [y])
                    out.append(y)
                dones[h]["v"] = out

            go(project(0, "q"))
            go(project(0, "k"))
            go(project(0, "v"))
            for h in range(4):
                done = dones[h]
                turn_v(h)
                pg = project(h, "g")
                y = []
                for half in range(2):
                    b, rel = banks.take()
                    for i in range(4):
                        c = 512 * half + 128 * i
                        m = tr(bank(b)[:, 128 * i:128 * i + 128], KH[:, c:c + 128], done["k"] + rel)
                    y = cp(KM[:, 4 * half:4 * half + 4, :], bank(b).rearrange("p (a b) -> p a b", a=4), [m] + prev["km"])
                    banks.free(b, [y])
                z1 = ts(VZ[:, :, 0:128], VM, ZE[:, h, 2:3], None, ALU.mult, after=done["v"] + prev["km"])
                z2 = ts(VZ[:, :, 128:256], VM, ZE[:, 4 + h, 2:3], None, ALU.mult)
                next(pg)
                kb = []
                for n in range(4):
                    b, rel = banks.take()
                    for i in range(2):
                        m = mm(bank(b)[:, 256 * i:256 * i + 256], KM[:, 2 * n + i, :], VZ[:, 2 * n + i, :], True, True, [z2, y] + rel)
                    kb.append((b, m))
                m_kv = m
                u = cp(PV[:, 0, 0:128], SC[:, h, 0:128], prev["o"])
                v = cp(PV[:, 7, 128:256], SC[:, h, 128:256], prev["o"])
                for n in range(7):
                    b, m = kb[n // 2]
                    u = stt(PV[:, n + 1, 0:128], PV[:, n, 0:128], ZE[:, h, 3:4], bank(b)[:, 256 * (n % 2):256 * (n % 2) + 128],
                            ALU.mult, ALU.add, [u, m])
                    n2 = 7 - n
                    b, m = kb[n2 // 2]
                    v = stt(PV[:, n2 - 1, 128:256], PV[:, n2, 128:256], ZE[:, 4 + h, 3:4],
                            bank(b)[:, 256 * (n2 % 2) + 128:256 * (n2 % 2) + 256], ALU.mult, ALU.add, [v, m])
                for b, m in kb:
                    banks.free(b, [u, v])
                sd = []
                for half in range(2):
                    b, rel = banks.take()
                    for i in range(4):
                        c = 512 * half + 128 * i
                        m = mm(bank(b)[:, 128 * i:128 * i + 128], KH[:, c:c + 128], QH[:, c:c + 128], True, True, done["q"] + rel)
                    y = tt(SS[:, 4 * half:4 * half + 4, :], bank(b).rearrange("p (a b) -> p a b", a=4),
                           DM[:, h, :].unsqueeze(1).broadcast_to([128, 4, 128]), ALU.mult, [m] + prev["o"])
                    banks.free(b, [y])
                    sd.append(y)
                for dr in range(2):
                    qx = tt(QX[:, dr, :].rearrange("p (a b) -> p a b", a=8), QH.rearrange("p (a b) -> p a b", a=8),
                            XI[:, h, dr, :].unsqueeze(1).broadcast_to([128, 8, 128]), ALU.mult, done["q"] + prev["o"])
                prev["q"], prev["k"], prev["km"] = [m, qx], [m], [m_kv]
                go(pg)
                if h < 3:
                    go(project(h + 1, "q"))
                else:
                    weights.prepare(weights.used + 1)
                ys = []
                for half in range(2):
                    b, rel = banks.take()
                    for i in range(4):
                        n = 4 * half + i
                        o = bank(b)[:, 128 * i:128 * i + 128]
                        mm(o, VM[:, n, :], SS[:, n, :], True, False, [sd[half], u, v, qx] + rel)
                        mm(o, PV[:, n, 0:128], QX[:, 0, 128 * n:128 * n + 128], False, False)
                        m = mm(o, PV[:, n, 128:256], QX[:, 1, 128 * n:128 * n + 128], False, True)
                    y = cp(OH[:, 512 * half:512 * half + 512], bank(b), [m] + oh_rel)
                    q = ac(T3[:, half, :], bank(b), ACT.Square, [y] + t3r[half])
                    banks.free(b, [q])
                    ys.append(q)
                prev["o"], prev["v"] = [m], [m, z2]
                if h < 3:
                    go(project(h + 1, "k"))
                vs_ = []
                for half in range(2):
                    b, rel = banks.take()
                    m2 = mm(bank(b), ones, T3[:, half, :], True, True, [ys[half]] + rel)
                    vs_.append(ts(T4[:, half, :], bank(b), 1.0 / 128, 1e-6, ALU.mult, ALU.add, after=[m2]))
                    banks.free(b, [vs_[-1]])
                tw = T4.rearrange("p a b -> p (a b)")
                v_ = ac(tw, tw, ACT.Ln, vs_)
                v_ = ac(tw, tw, ACT.Exp, [v_], scale=-0.5)
                v_ = stt(OH, OH, 0.5, tw, ALU.mult, ALU.mult, [v_])
                t3r[0] = t3r[1] = [v_]
                v_ = tt(OH, OH, GH_, ALU.mult, [v_] + done["g"])
                prev["g"] = [v_]
                dd = pool.dma(ch("os2"), os_[h][:, 0:SEQ], OH, [v_])
                oh_rel[:] = [dd]
                stored[h] = dd
                if h < 3:
                    go(project(h + 1, "v"))
        oh_rel, stored = [], {}

        def fourier(ready):
            phase(FM[0])
            FTt = r3(4, 1024)
            CD = carve(256)
            MX = r3(8, 1024)
            GA = carve(1024)
            XL = r3(4, 1024)
            J = carve(1024)
            TB = r3(2, 512)
            dh = [pool.dma(ch(f"h{g}"), MX[:, g, :], os_[g][:, 0:SEQ], [stored[g], stored[3]]) for g in range(4)]
            xl = [pool.dma(ch(f"r{t}"), XL[:, t, :], xs[128 * t:128 * t + 128, :]) for t in range(4)]
            dg = gate_rows(GA, J, 0, 2)
            d0 = pool.dma(ch("b3"), CD, A["k_cd"])
            w = A["w_in_2"][0]
            fin = []
            for g in range(4):
                def evac(o, c, n, m):
                    x = ac(FTt[:, g, c:c + n], o, ACT.Copy, [m])
                    fin.append(x)
                    return [x]
                for _ in gemm_f(CH2, evac, ready):
                    pass
            alldone = pe.items[-1]
            AHf = AH[:, :, :].rearrange("p a b -> p (a b)")[:, 0:8192].rearrange("p (m g c) -> p m g c", m=8, g=4)
            ALf = AL[:, :, :].rearrange("p a b -> p (a b)")[:, 0:8192].rearrange("p (m g c) -> p m g c", m=8, g=4)
            for g in range(4):
                for mt in range(0, 8, 2):
                    b, rel = banks.take()
                    for i in range(2):
                        c = 128 * (mt + i)
                        m = mm(bank(b)[:, 256 * i:256 * i + 256], FTt[:, g, c:c + 128], CD, True, True, [d0, fin[2 * g + 1]] + rel)
                    src = bank(b).rearrange("p (a b) -> p a b", a=2)
                    h = ac(AHf[:, mt:mt + 2, g, :], src, ACT.Copy, [m, alldone])
                    lo = tt(ALf[:, mt:mt + 2, g, :], src, f(AHf[:, mt:mt + 2, g, :]), ALU.subtract, [h])
                    banks.free(b, [lo])
            bs = [banks.take() for _ in range(8)]
            for j in range(16):
                mt, cs = j // 2, j % 2
                t, wl_ = weights.next()
                for g in range(4):
                    yh = AHf[:, mt, g, 128 * cs:128 * cs + 128]
                    yl = ALf[:, mt, g, 128 * cs:128 * cs + 128]
                    for half in range(2):
                        b, rel = bs[2 * g + half]
                        wv = slice(512 * half, 512 * half + 512)
                        m = mm3(bank(b), yh, yl, WH[:, t, wv], WL[:, t, wv], j == 0, j == 15, [lo, wl_] + rel)
                wr.free(t, [m])
            ready_k = {}
            for g in (4, 5, 0, 1, 2, 3, 6, 7):
                for half in range(2 if g > 3 else 1):
                    if g > 3:
                        bk = bs[2 * (g - 4) + half][0]
                        src, cc = bank(bk), slice(512 * half, 512 * half + 512)
                    else:
                        src, cc = MX[:, g, :], slice(0, SEQ)
                    h = ac(AH[:, g, cc], src, ACT.Copy, [m] + ([] if g > 3 else [dh[g]]))
                    ready_k[g] = [tt(AL[:, g, cc], src, f(AH[:, g, cc]), ALU.subtract, [h])]
                    if g > 3:
                        banks.free(bk, ready_k[g])

            def evac(b, t, n, q, last):
                y = (ac if t % 4 else cp)(MX[:, t:t + n, 256 * q:256 * q + 256], b, after=[last])
                fin[t] = fin[t + 1] = fin.get(t, []) + [y]
                return [y]
            fin = {}
            out_proj([128 * t for t in range(8)], evac, ready_k)
            ready, ys, st_ = {}, [], []

            def first(t0):
                v = stats([(MX[:, t, :], fin[t] + [dg]) for t in range(t0, t0 + 4)], RSTD[:, t0:t0 + 4], 1e-6, J)
                for t in range(t0, t0 + 4):
                    x = MX[:, t, :]
                    y = stt(x, x, RSTD[:, t:t + 1], GA, ALU.mult, ALU.mult, [v, dg])
                    y = tt(x, x, XL[:, t % 4, :], ALU.add, [y, xl[t]])
                    if t < 4:
                        xl.append(pool.dma(ch(f"r{t}"), XL[:, t, :], xs[128 * t + 512:128 * t + 640, :], [y]))
                    ys.append(y)
                    st_.append(pool.dma(ch(f"s{t}"), xs[128 * t:128 * t + 128, :], x, [y]))
                return v

            def second(t0):
                return stats([(MX[:, t, :], [ys[t]]) for t in range(t0, t0 + 4)], RSTD[:, 8 + t0:12 + t0], 1e-6, J)

            first(0)
            v = second(0)
            for t in range(4):
                ready[t] = ts(FTt[:, t, :], MX[:, t, :], RSTD[:, 8 + t:9 + t], None, ALU.mult, after=[v])
            first(4)
            v = second(4)
            for t in range(4, 8):
                ready[t] = ts(XL[:, t - 4, :], MX[:, t, :], RSTD[:, 8 + t:9 + t], None, ALU.mult, after=[v])
            x_stored[:] = st_
            return fill_a([((FTt if t < 4 else XL)[:, t % 4, :], 128 * t) for t in range(8)], ready, lambda k: G1[:, 2, k:k + 1], lambda k: B1[:, 2, k:k + 1], TB)[0]

        x_stored = []

        def ffn(ready):
            phase()
            pend.extend(x_stored)
            CW = carve(4 * 44).rearrange("p (a b) -> p a b", a=4)
            NR = 17
            CV = r3(2, 1024)
            CU = r3(2, 1024)
            TH = r3(2, 1024)
            G = r3(NR, 1024)
            gsp = S["gsp"]
            d0 = pool.dma(ch("b5"), CW, A["k_conv"].rearrange("p (a b) -> p a b", a=4))
            w = A["w_up_2"][0]
            cvr, thr = Ring(2), Ring(2)

            def conv(o, dst, c, j, after):
                x = ac(dst[:, c:c + 512], o, ACT.Identity, after + [d0], scale=CW[:, 1, j:j + 1], bias=CW[:, 3, j:j + 1])
                d3 = dst[:, c:c + 512].rearrange("p (r t) -> p r t", t=64)
                o3 = o.rearrange("p (r t) -> p r t", t=64)
                y = stt(d3[:, :, 1:64], o3[:, :, 0:63], CW[:, 0, j:j + 1], d3[:, :, 1:64], ALU.mult, ALU.add, [x])
                return stt(d3[:, :, 0:63], o3[:, :, 1:64], CW[:, 2, j:j + 1], d3[:, :, 0:63], ALU.mult, ALU.add, [y])
            gdone = []
            for j in range(FT):
                ci, crel = cvr.take()
                ti, trel = thr.take()
                va, vb, th = CV[:, ci, :], CU[:, ci, :], TH[:, ti, :]
                ya, yb = [], []

                def evac(o, c, n, m):
                    y = conv(o, va, c, j, [m] + crel)
                    ya.append(y)
                    return [y]
                for _ in gemm_f(CH2, evac, ready):
                    pass
                t_ = ac(th, va, ACT.Tanh, ya + trel, scale=0.5)

                def evac(o, c, n, m):
                    y = conv(o, vb, c, FT + j, [m] + crel)
                    yb.append(y)
                    return [y]
                for _ in gemm_f(CH2, evac, ready):
                    pass
                a1 = stt(va, th, 1.0, va, ALU.add, ALU.mult, [t_])
                thr.free(ti, [a1])
                if j < NR:
                    a2 = stt(G[:, j, :], va, 0.5, vb, ALU.mult, ALU.mult, [a1, yb[-1]] + (x_stored if j == 0 else []))
                    cvr.free(ci, [a2])
                else:
                    a2 = stt(va, va, 0.5, vb, ALU.mult, ALU.mult, [a1, yb[-1]])
                    a2 = pool.dma(ch(f"s{ci}"), gsp[j - NR], va, [a2])
                    cvr.free(ci, [a2])
                    pend.append(a2)
                gdone.append(a2)
            barrier()
            GL_ = CU
            wd = A["w_down_2"][0]
            glr, ar = Ring(2), Ring(8)
            F = {}
            fdone = {}
            parts = []

            def split_g(n):
                while len(parts) <= min(n, 2 * FT - 1):
                    k = len(parts) % FT
                    ai, arel = ar.take()
                    if k < NR:
                        src, dep = G[:, k, :], []
                    else:
                        gi_, grel = glr.take()
                        d = pool.dma(ch(f"g{gi_}"), GL_[:, gi_, :], gsp[k - NR], grel)
                        src, dep = GL_[:, gi_, :], [d]
                    h = ac(AH[:, ai, 0:SEQ], src, ACT.Copy, dep + arel)
                    lo = tt(AL[:, ai, 0:SEQ], src, f(AH[:, ai, 0:SEQ]), ALU.subtract, [h])
                    if k >= NR:
                        glr.free(gi_, [lo])
                    parts.append((ai, lo))

            for half in range(2):
                bs = [banks.take() for _ in range(8)]
                wt = None
                for k in range(FT):
                    if k % 2 == 0:
                        wt, wlo = weights.next()
                    split_g(FT * half + k + 3)
                    ai, lo = parts[FT * half + k]
                    wv = slice(512 * (k % 2), 512 * (k % 2) + 512)
                    for t in range(8):
                        b, rel = bs[t]
                        m = mm3(bank(b), AH[:, ai, 128 * t:128 * t + 128], AL[:, ai, 128 * t:128 * t + 128],
                                WH[:, wt, wv], WL[:, wt, wv], k == 0, k == FT - 1, [lo, wlo] + (rel if k == 0 else []))
                        if k == FT - 1:
                            if half == 0:
                                dst = (CV if t < 4 else TH)[:, (t // 2) % 2, 512 * (t % 2):512 * (t % 2) + 512]
                            else:
                                dst = G[:, t, 0:512]
                            F[(t, half)] = dst
                            y = (ac if t % 2 else cp)(dst, bank(b), after=[m])
                            fdone[(t, half)] = y
                            banks.free(b, [y])
                    ar.free(ai, [m])
                    if k % 2 == 1:
                        wr.free(wt, [m])
            split = parts[FT + NR - 1][1]
            GA, XL, J, J2 = G[:, 8, :], G[:, 9:17, :], CU[:, 0, :], CU[:, 1, :]
            dg = gate_rows(GA, J2, 1, 5, [split, lo])
            xl = [pool.dma(ch(f"r{t}"), XL[:, t, :], xs[128 * t:128 * t + 128, :], [split]) for t in range(8)]
            q = lo
            for t0 in (0, 4):
                for t in range(t0, t0 + 4):
                    ac(J[:, 0:512], F[(t, 0)], ACT.Square, [lo, q, fdone[(t, 0)]], accum=RSTD[:, t:t + 1])
                    q = ac(J[:, 512:1024], F[(t, 1)], ACT.Square, [fdone[(t, 1)]], accum=RSTD[:, 8 + t:9 + t])
                r = RSTD[:, t0:t0 + 4]
                v = tt(r, r, RSTD[:, 8 + t0:12 + t0], ALU.add, [q])
                v = rstd_of(r, 128, 1.0 / D, 1e-6, [v])
                for t in range(t0, t0 + 4):
                    for half in range(2):
                        hv = slice(512 * half, 512 * half + 512)
                        y = stt(F[(t, half)], F[(t, half)], RSTD[:, t:t + 1], GA[:, hv], ALU.mult, ALU.mult, [v, dg])
                        y = tt(XL[:, t, hv], XL[:, t, hv], F[(t, half)], ALU.add, [y, xl[t]])
                    pend.append(pool.dma(ch(f"s{t}"), O["out"][0][128 * t:128 * t + 128, :], XL[:, t, :], [y]))

        ada_phase()
        tabs = ctx_phase()
        lo = prep_x(FM[0])
        mixer(*tabs, [lo])
        lo = fourier([lo])
        ffn([lo])
        barrier()
        finish = [c for c in chans.values()]

        for q in (pe, act, dve, pool, sp):
            n = q.number()
        block = ctx.enter_context(nc.Block())

        @block.tensor
        def _(e):
            pe.emit(e)

        @block.scalar
        def _(e):
            act.emit(e)

        @block.vector
        def _(e):
            dve.emit(e)

        @block.gpsimd
        def _(e):
            pool.emit(e)

        @block.sync
        def _(e):
            sp.emit(e)
            for c in finish:
                e.wait_ge(c.sem, 16 * c.n)


def host_constants():
    f = np.float32
    c = {}
    c["k_ident"] = np.eye(128, dtype=f)
    q = np.arange(128)
    m = np.zeros((128, 2, 128), f)
    m[:, 0] = np.where((q[None, :] // 64) <= (q[:, None] // 64), 0.0, NEG)
    m[:, 1] = np.where(q[None, :] <= q[:, None], 0.0, NEG)
    c["k_mask"] = m.reshape(128, 256)
    s = np.zeros((128, 8, 128), f)
    for h in range(8):
        s[h, h] = -1.0
        s[32 + h, h] = -1.0
    c["k_sel"] = s.reshape(128, 1024)
    pos = np.arange(L, dtype=f)
    inv = (1.0 / (np.float32(500000.0) ** (np.arange(0, 16, 2, dtype=f) / np.float32(16)))).astype(f)
    ang = pos[None, :] * inv[:, None]
    cos, sin = np.ones((128, L), f), np.zeros((128, L), f)
    rot = np.zeros((128, 128), f)
    for b in (0, 64):
        cos[b:b + 8] = np.cos(ang)
        cos[b + 8:b + 16] = np.cos(ang)
        sin[b:b + 8] = -np.sin(ang)
        sin[b + 8:b + 16] = np.sin(ang)
        for i in range(8):
            rot[b + 8 + i, b + i] = 1.0
            rot[b + i, b + 8 + i] = 1.0
    c["k_cos"], c["k_sin"], c["k_rot"] = cos, sin, rot
    p = np.arange(128, dtype=f)
    dec = np.zeros((128, 776), f)
    dec[:, 0], dec[:, 1], dec[:, 2], dec[:, 3] = 255 - p, 127 - p, 127 - p, 128
    dec[:, 4], dec[:, 5], dec[:, 6], dec[:, 7] = p, 128 + p, p, 128
    dec[:, 8:136] = p[None, :] + 1
    dec[:, 136:264] = 128 - p[None, :]
    dec[:, 264:392] = np.maximum(p[None, :] - p[:, None], 0)
    dec[:, 392:520] = np.maximum(p[:, None] - p[None, :], 0)
    dec[:, 520:648] = (p[:, None] <= p[None, :])
    dec[:, 648:776] = (p[:, None] > p[None, :])
    c["k_dec"] = dec
    t = np.arange(SEQ)
    fr = (np.float32(10000.0) ** (-np.arange(32, dtype=f) / np.float32(32))).astype(f)
    ang = np.concatenate([(t // 64).astype(f)[:, None] * fr, (t % 64).astype(f)[:, None] * fr], 1).T
    c["k_cos2"] = np.concatenate([np.cos(ang), np.cos(ang)]).astype(f)
    c["k_sin2"] = np.concatenate([np.sin(ang), -np.sin(ang)]).astype(f)
    i = np.arange(128, dtype=np.int64)
    a = 2 * np.pi * ((i[:, None] * i[None, :]) % 128) / 128.0
    c["k_cd"] = (np.concatenate([np.cos(a), np.sin(a)], 1) / np.sqrt(1024.0 * 128.0)).astype(f)
    n = np.arange(SEQ, dtype=np.int64)
    a = 2 * np.pi * ((n[:, None] * n[None, :]) % SEQ) / float(SEQ)
    both = np.stack([np.cos(a), -np.sin(a)], 0).reshape(2, 8, 128, SEQ)
    c["k_dft"] = np.ascontiguousarray(both.transpose(2, 1, 0, 3).reshape(128, 16 * SEQ)).astype(f)
    return c


def layout(inputs):
    f = {k: np.asarray(v) for k, v in inputs.items()}
    a = dict(host_constants())
    for n in ("x", "meta_tokens", "w_in", "w_out"):
        a[n] = f[n]
    cols = np.zeros((128, 32), np.float32)
    for l in range(2):
        cols[:, 8 * l:8 * l + 8] = f["norm_gain"][l].reshape(8, 128).T
        cols[:, 16 + l] = f["subln_gain"][l]
        cols[0:8, 18 + l] = f["forget_bias"][l]
    a["k_cols"] = cols
    for n in ("ctx_2", "w_ada_2", "w_in_2", "w_out_2", "w_up_2", "w_down_2"):
        a[n] = f[n]

    def col(v):
        return v.reshape(-1, 128).T

    def rows(v, n=128):
        return np.repeat(v.reshape(1, -1), n, axis=0)
    a["k_c"] = np.stack([col(f["c_2"][0]), col(f["c_ctx_2"])], 2).reshape(128, 16)
    a["k_brow"] = np.repeat(f["b_ada_2"], 2, axis=0)
    a["k_gpre"] = np.concatenate([col(f["g_mix_pre_2"][0]), col(f["g_ffn_pre_2"][0])], 1)
    a["k_gpost"] = np.concatenate([rows(f["g_mix_post_2"][0]), rows(f["g_ffn_post_2"][0])], 1)
    k2 = np.zeros((128, 24), np.float32)
    k2[:, 0:4], k2[:, 4:8] = rows(f["ret_decay_fwd_2"][0]), rows(f["ret_decay_bwd_2"][0])
    a["k_cols2"] = k2
    a["k_fg"] = rows(f["final_gain"])
    cw = np.concatenate([f["conv_w_2"][0], f["conv_b_2"]], 0)
    a["k_conv"] = cw.reshape(4, 44, 128).transpose(2, 0, 1).reshape(128, 176)
    lam = np.stack([f["lambda_q1"], f["lambda_k1"], f["lambda_q2"], f["lambda_k2"]], 1).reshape(1, 512)
    a["k_lam"] = np.repeat(lam, 128, axis=0)
    return {k: np.ascontiguousarray(v) for k, v in a.items()}


SCRATCH = {"hs": (L, D), "os": (8, 128, L), "xs": (SEQ, D), "ada": (2, 6 * D), "gsp": (FT - 17, 128, SEQ)}


def kernel(**inputs):
    import concourse.bacc as _bacc
    from concourse.bass_utils import run_bass_kernel_spmd as _run

    arrays = layout(inputs)
    nc = _bacc.Bacc("TRN2", target_bir_lowering=False, num_devices=1)
    A = {n: nc.dram_tensor(f"in_{n}", a.shape, mybir.dt.from_np(a.dtype), kind="ExternalInput").ap()
         for n, a in arrays.items()}
    S = {n: nc.dram_tensor(f"s_{n}", s, F32, kind="Internal").ap() for n, s in SCRATCH.items()}
    O = {"out": nc.dram_tensor("out_0", (1, SEQ, D), F32, kind="ExternalOutput").ap()}
    build(nc, A, S, O)
    r = _run(nc, [{f"in_{n}": a for n, a in arrays.items()}], core_ids=[0])
    return r.results[0]["out_0"]
```
